# Optimizing a Trainium2 kernel written in Bass

```python
import math
import jax, jax.numpy as jnp
from jax import lax
import numpy as np

D_MODEL = 1024
BATCH = 1
SEQ = 256
DEPTH = 2

D_RNN = D_MODEL
N_LRU_BLOCKS = 8
LRU_BLOCK = D_RNN // N_LRU_BLOCKS
CONV_WIDTH = 4
CONV_PAD_LEFT = 1
LRU_C = 8.0
HEAD_DIM = 64
HEADS_PER_GROUP = 4
WINDOWS = (128, 512, 2048)
DILATIONS = (1, 4, 16)
N_GROUPS = len(WINDOWS)
N_ATT_HEADS = N_GROUPS * HEADS_PER_GROUP
ATT_WIDTH = N_ATT_HEADS * HEAD_DIM
ATT_OUT = HEADS_PER_GROUP * HEAD_DIM
ROT_DIM = HEAD_DIM // 4
ROPE_THETA = 500000.0
BAND_BLOCK = 64
N_BRANCHES = 2
IN_WIDTH = 2 * D_RNN + 3 * ATT_WIDTH + N_BRANCHES * D_MODEL
D_FF = 2816
N_EXPERTS = 8
TOP_K = 2
D_EXPERT = 3584
N_DENSE = (DEPTH + 1) // 2
N_MOE = DEPTH // 2
RMS_EPS = 1e-6

kernel_name = "hybrid_rglru_dilated_attn_moe_encoder"

def rms_norm(x, g):
    xf = x.astype(jnp.float32)
    y = xf * lax.rsqrt(jnp.mean(xf * xf, axis=-1, keepdims=True) + RMS_EPS)
    return (y * g.astype(jnp.float32)).astype(x.dtype)

def rotary_tables(seq_len):
    pos = jnp.arange(seq_len, dtype=jnp.float32)
    inv_freq = ROPE_THETA ** (-jnp.arange(0, ROT_DIM, 2, dtype=jnp.float32) / ROT_DIM)
    ang = pos[:, None] * inv_freq[None, :]
    return jnp.cos(ang), jnp.sin(ang)

def partial_rotary(t, cos, sin):
    half = ROT_DIM // 2
    rot = t[..., :ROT_DIM].astype(jnp.float32)
    t1, t2 = rot[..., :half], rot[..., half:]
    c, s = cos[None, :, None, :], sin[None, :, None, :]
    rotated = jnp.concatenate([t1 * c - t2 * s, t2 * c + t1 * s], axis=-1).astype(t.dtype)
    return jnp.concatenate([rotated, t[..., ROT_DIM:]], axis=-1)

def centred_depthwise_conv(x, w, b):
    S = x.shape[1]
    xp = jnp.pad(x, ((0, 0), (CONV_PAD_LEFT, CONV_WIDTH - 1 - CONV_PAD_LEFT), (0, 0)))
    y = b
    for j in range(CONV_WIDTH):
        y = y + xp[:, j:j + S] * w[j]
    return y

def _linear_scan_combine(left, right):
    a_l, b_l = left
    a_r, b_r = right
    return a_l * a_r, a_r * b_l + b_r

def rg_lru_direction(xc, w_r, b_r, w_i, b_i, lam, reverse):
    B, S, _ = xc.shape
    xb = xc.reshape(B, S, N_LRU_BLOCKS, LRU_BLOCK)
    r = jax.nn.sigmoid(jnp.einsum('bsnc,ncd->bsnd', xb, w_r.astype(jnp.float32)).reshape(B, S, D_RNN) + b_r)
    i = jax.nn.sigmoid(jnp.einsum('bsnc,ncd->bsnd', xb, w_i.astype(jnp.float32)).reshape(B, S, D_RNN) + b_i)
    log_a = -LRU_C * r * jax.nn.softplus(-lam.astype(jnp.float32))
    a = jnp.exp(log_a)
    u = jnp.sqrt(-jnp.expm1(2.0 * log_a)) * (i * xc)
    if reverse:
        a, u = jnp.flip(a, axis=1), jnp.flip(u, axis=1)
    _, h = lax.associative_scan(_linear_scan_combine, (a, u), axis=1)
    if reverse:
        h = jnp.flip(h, axis=1)
    return h

def dilated_band_attention(q, k, v, dilation, half_keys):
    B, S, H, Dh = q.shape
    L = S // dilation

    def by_residue(t):
        return t.reshape(B, L, dilation, H, Dh).transpose(0, 2, 1, 3, 4)

    qs, ks, vs = by_residue(q), by_residue(k), by_residue(v)
    C = math.gcd(L, BAND_BLOCK)
    nb = L // C
    W = C + 2 * half_keys
    pad = ((0, 0), (0, 0), (half_keys, half_keys), (0, 0), (0, 0))
    kp, vp = jnp.pad(ks, pad), jnp.pad(vs, pad)
    idx = (jnp.arange(nb) * C)[:, None] + jnp.arange(W)[None, :]
    kb = kp[:, :, idx].astype(jnp.float32)
    vb = vp[:, :, idx].astype(jnp.float32)
    qb = qs.reshape(B, dilation, nb, C, H, Dh).astype(jnp.float32)
    s = jnp.einsum('brnqhd,brnkhd->brnhqk', qb, kb) * (HEAD_DIM ** -0.5)
    rel = jnp.arange(W)[None, :] - half_keys - jnp.arange(C)[:, None]
    band = jnp.abs(rel) <= half_keys
    kpos = idx - half_keys
    in_range = (kpos >= 0) & (kpos < L)
    mask = band[None, :, :] & in_range[:, None, :]
    s = jnp.where(mask[None, None, :, None, :, :], s, -jnp.inf)
    lse = jax.nn.logsumexp(s, axis=-1)
    p = jnp.exp(s - lse[..., None])
    o = jnp.einsum('brnhqk,brnkhd->brnqhd', p, vb)
    o = o.reshape(B, dilation, L, H, Dh).transpose(0, 2, 1, 3, 4).reshape(B, S, H, Dh)
    lse = lse.transpose(0, 1, 2, 4, 3).reshape(B, dilation, L, H).transpose(0, 2, 1, 3).reshape(B, S, H)
    return o, lse

def hybrid_mixer(h, w_in, conv_w, conv_b, w_rgate, b_rgate, w_igate, b_igate, lru_lambda,
                 w_proj_lru, w_proj_att, w_out, cos, sin):
    B, S, _ = h.shape
    z = h @ w_in
    cuts = [int(c) for c in np.cumsum([D_RNN, D_RNN, ATT_WIDTH, ATT_WIDTH, ATT_WIDTH])]
    x_rnn, y_gate, q, k, v, g = jnp.split(z, cuts, axis=-1)

    xc = centred_depthwise_conv(x_rnn, conv_w, conv_b).astype(jnp.float32)
    h_fwd = rg_lru_direction(xc, w_rgate[0], b_rgate[0], w_igate[0], b_igate[0], lru_lambda[0], False)
    h_bwd = rg_lru_direction(xc, w_rgate[1], b_rgate[1], w_igate[1], b_igate[1], lru_lambda[1], True)
    lru = ((h_fwd + h_bwd) * jax.nn.gelu(y_gate.astype(jnp.float32), approximate=True)).astype(h.dtype)
    branch_lru = lru @ w_proj_lru

    q = partial_rotary(q.reshape(B, S, N_ATT_HEADS, HEAD_DIM), cos, sin)
    k = partial_rotary(k.reshape(B, S, N_ATT_HEADS, HEAD_DIM), cos, sin)
    v = v.reshape(B, S, N_ATT_HEADS, HEAD_DIM)
    outs, lses = [], []
    for grp in range(N_GROUPS):
        sl = slice(grp * HEADS_PER_GROUP, (grp + 1) * HEADS_PER_GROUP)
        o, lse = dilated_band_attention(q[:, :, sl], k[:, :, sl], v[:, :, sl],
                                        DILATIONS[grp], WINDOWS[grp] // (2 * DILATIONS[grp]))
        outs.append(o)
        lses.append(lse)
    mix = jax.nn.softmax(jnp.stack(lses, axis=0), axis=0)
    att = jnp.sum(mix[..., None] * jnp.stack(outs, axis=0), axis=0)
    branch_att = att.reshape(B, S, ATT_OUT).astype(h.dtype) @ w_proj_att

    gates = jax.nn.sigmoid(g.astype(jnp.float32)).reshape(B, S, N_BRANCHES, D_MODEL)
    merged = gates[:, :, 0] * branch_lru.astype(jnp.float32) + gates[:, :, 1] * branch_att.astype(jnp.float32)
    return merged.astype(h.dtype) @ w_out

def swiglu(h, w_gate, w_up, w_down):
    return (jax.nn.silu(h @ w_gate) * (h @ w_up)) @ w_down

def moe_swiglu(h, w_router, w_gate, w_up, w_down):
    logits = (h @ w_router).astype(jnp.float32)
    top_val, top_idx = lax.top_k(logits, TOP_K)
    top_w = jax.nn.softmax(top_val, axis=-1)
    combine = jnp.sum(jax.nn.one_hot(top_idx, N_EXPERTS, dtype=jnp.float32) * top_w[..., None], axis=-2)
    out = jnp.zeros(h.shape, jnp.float32)
    for e in range(N_EXPERTS):
        y = swiglu(h, w_gate[e], w_up[e], w_down[e]).astype(jnp.float32)
        out = out + combine[..., e:e + 1] * y
    return out.astype(h.dtype)

def setup_inputs(seed: int = 0) -> dict:
    key = jax.random.key(seed)
    ks = jax.random.split(key, 24)
    f32 = jnp.float32

    def nrm(k, shape, fan_in):
        return jax.random.normal(k, shape, f32) * (fan_in ** -0.5)

    u = jax.random.uniform(ks[10], (DEPTH, 2, D_RNN), f32, 0.9, 0.999)
    a0 = u ** (1.0 / LRU_C)
    lru_lambda = jnp.log(a0) - jnp.log1p(-a0)
    return {
        "x": jax.random.normal(ks[0], (BATCH, SEQ, D_MODEL), f32),
        "norm_mix_g": 1.0 + 0.02 * jax.random.normal(ks[1], (DEPTH, D_MODEL), f32),
        "w_in": nrm(ks[2], (DEPTH, D_MODEL, IN_WIDTH), D_MODEL),
        "conv_w": nrm(ks[3], (DEPTH, CONV_WIDTH, D_RNN), CONV_WIDTH),
        "conv_b": 0.02 * jax.random.normal(ks[4], (DEPTH, D_RNN), f32),
        "w_rgate": nrm(ks[5], (DEPTH, 2, N_LRU_BLOCKS, LRU_BLOCK, LRU_BLOCK), LRU_BLOCK),
        "b_rgate": 0.02 * jax.random.normal(ks[6], (DEPTH, 2, D_RNN), f32),
        "w_igate": nrm(ks[7], (DEPTH, 2, N_LRU_BLOCKS, LRU_BLOCK, LRU_BLOCK), LRU_BLOCK),
        "b_igate": 0.02 * jax.random.normal(ks[8], (DEPTH, 2, D_RNN), f32),
        "lru_lambda": lru_lambda,
        "w_proj_lru": nrm(ks[11], (DEPTH, D_RNN, D_MODEL), D_RNN),
        "w_proj_att": nrm(ks[12], (DEPTH, ATT_OUT, D_MODEL), ATT_OUT),
        "w_out": nrm(ks[13], (DEPTH, D_MODEL, D_MODEL), D_MODEL),
        "norm_ffn_g": 1.0 + 0.02 * jax.random.normal(ks[14], (DEPTH, D_MODEL), f32),
        "w_dense_gate": nrm(ks[15], (N_DENSE, D_MODEL, D_FF), D_MODEL),
        "w_dense_up": nrm(ks[16], (N_DENSE, D_MODEL, D_FF), D_MODEL),
        "w_dense_down": nrm(ks[17], (N_DENSE, D_FF, D_MODEL), D_FF),
        "w_router": nrm(ks[18], (N_MOE, D_MODEL, N_EXPERTS), D_MODEL),
        "w_exp_gate": nrm(ks[19], (N_MOE, N_EXPERTS, D_MODEL, D_EXPERT), D_MODEL),
        "w_exp_up": nrm(ks[20], (N_MOE, N_EXPERTS, D_MODEL, D_EXPERT), D_MODEL),
        "w_exp_down": nrm(ks[21], (N_MOE, N_EXPERTS, D_EXPERT, D_MODEL), D_EXPERT),
        "final_norm_g": 1.0 + 0.02 * jax.random.normal(ks[22], (D_MODEL,), f32),
    }

def reference(x, norm_mix_g, w_in, conv_w, conv_b, w_rgate, b_rgate, w_igate, b_igate, lru_lambda,
              w_proj_lru, w_proj_att, w_out, norm_ffn_g, w_dense_gate, w_dense_up, w_dense_down,
              w_router, w_exp_gate, w_exp_up, w_exp_down, final_norm_g):
    cos, sin = rotary_tables(x.shape[1])
    for layer in range(DEPTH):
        hn = rms_norm(x, norm_mix_g[layer])
        x = x + hybrid_mixer(hn, w_in[layer], conv_w[layer], conv_b[layer], w_rgate[layer], b_rgate[layer],
                             w_igate[layer], b_igate[layer], lru_lambda[layer], w_proj_lru[layer],
                             w_proj_att[layer], w_out[layer], cos, sin)
        hn = rms_norm(x, norm_ffn_g[layer])
        j = layer // 2
        if layer % 2 == 0:
            x = x + swiglu(hn, w_dense_gate[j], w_dense_up[j], w_dense_down[j])
        else:
            x = x + moe_swiglu(hn, w_router[j], w_exp_gate[j], w_exp_up[j], w_exp_down[j])
    return rms_norm(x, final_norm_g)


_drawn_inputs = setup_inputs


def setup_inputs(seed=0):
    import zlib

    import numpy as np

    out = dict(_drawn_inputs(seed))
    spreads = {}
    factors = {'b_rgate': 3.326, 'b_igate': 2.945, 'final_norm_g': 2.824}
    for name, (base, spread) in spreads.items():
        noise = np.random.default_rng([zlib.crc32(name.encode()), seed]).standard_normal(out[name].shape)
        drawn = base * np.exp(spread * noise) if base else spread * noise
        out[name] = __import__('jax').numpy.asarray(drawn.astype(out[name].dtype))
    for name, factor in factors.items():
        out[name] = (out[name] * factor).astype(out[name].dtype)
    return out
```

```python
from contextlib import ExitStack

import numpy as np
import concourse.bass as bass
from concourse import mybir

F32 = mybir.dt.float32
F32R = mybir.dt.float32r
I32 = mybir.dt.int32
ALU = mybir.AluOpType
ACT = mybir.ActivationFunctionType
AX = mybir.AxisListType

P = 128
D = 1024
KT = D // P
T = 256
TB = T // P
DEPTH = 2
CB = 512
HEADS, SLOTS, GROUPS, DH = 12, 4, 3, 64
QK = 2 * HEADS * DH
VW = HEADS * DH
WINDOWS, DILATIONS = (128, 512, 2048), (1, 4, 16)
F_DENSE, F_EXP, EXPERTS = 2816, 3584, 8
EPS = 1e-6
SCALE = DH ** -0.5
NEG = -1e30

PART = 2048
HALF = PART // 2
R = 6
H = 4

MIXER = ([(("x", n), "n", 2) for n in range(2)] + [(("qkv", n), "n", 2) for n in range(4)]
         + [(("qkv", 4), "h", 1)] + [(("y", n), "n", 2) for n in range(2)]
         + [(("g1", n), "n", 2) for n in range(2)] + [(("g0", n), "n", 2) for n in range(2)]
         + [(("lru", n), "n", 2) for n in range(2)] + [(("att", 0), "w", 1)]
         + [(("out", n), "n", 2) for n in range(2)])
DSTEPS = F_DENSE // CB
ESTEPS = F_EXP // CB
E_PARTS = 6 * ESTEPS
NPASS_TOKENS = P


def dense_order():
    out = []
    for c in range(DSTEPS + 1):
        tail = c == DSTEPS
        out += [(("gate", c), "h" if tail else "n", 1 if tail else 2),
                (("up", c), "h" if tail else "n", 1 if tail else 2)]
        if c:
            out += [(("down", c - 1, n), "n", 1) for n in range(2)]
    return out + [(("down", DSTEPS, 0), "w", 1)]


def expert_order():
    out = []
    for c in range(ESTEPS):
        out += [("gate", c), ("up", c)]
        if c:
            out += [("down", c - 1)]
    return out + [("down", ESTEPS - 1)]


def schedule():
    steps = []
    for L in range(DEPTH):
        steps.append(("norm", 2 * L))
        side = {}

        def at(gap, *what):
            side.setdefault(gap, []).extend(what)

        at(3, ("evac", ("x", 0)), ("tx", 0), ("conv", 0))
        at(4, ("conv", 1))
        at(5, ("evac", ("x", 1)), ("tx", 1), ("conv", 2))
        at(6, ("conv", 3), ("lg", 0, 0))
        at(7, ("evac", ("qkv", 0)), ("lg", 0, 1), ("la", 0, 0))
        at(8, ("lg", 0, 2), ("lb", 0, 0))
        at(9, ("evac", ("qkv", 1)), ("lg", 0, 3), ("la", 0, 1))
        at(10, ("lb", 0, 1))
        at(11, ("evac", ("qkv", 2)), ("rope",), ("la", 0, 2))
        at(12, ("lb", 0, 2))
        at(13, ("evac", ("qkv", 3)), ("la", 0, 3))
        at(14, ("evac", ("qkv", 4)), ("lb", 0, 3))
        at(15, ("lg", 1, 0), ("la", 1, 0))
        at(16, ("evac", ("y", 0)), ("ty", 0), ("lb", 1, 0))
        at(17, ("lg", 1, 1), ("la", 1, 1))
        at(18, ("evac", ("y", 1)), ("ty", 1), ("lb", 1, 1))
        at(19, ("lg", 1, 2), ("la", 1, 2))
        at(20, ("lb", 1, 2), ("lg", 1, 3), ("la", 1, 3))
        at(21, ("lb", 1, 3), *(("tq", j) for j in range(HEADS // 2)), ("evac", ("g1", 0)))
        at(22, ("evac", ("g1", 1)), ("as", 0), ("lf", 0))
        at(23, ("ap", 0), ("as", 1), ("lf", 1))
        at(24, ("evac", ("g0", 0)), ("av", 0), ("ap", 1), ("as", 2), ("lf", 2))
        at(25, ("av", 1), ("ap", 2), ("as", 3), ("lf", 3))
        at(26, ("evac", ("g0", 1)), ("av", 2), ("ap", 3), ("as", 4))
        at(27, ("av", 3), ("ap", 4), ("as", 5), ("av", 4), ("ap", 5), ("as", 6))
        at(28, ("evac", ("lru", 0)), ("av", 5), ("ap", 6), ("as", 7))
        at(29, ("av", 6), ("ap", 7), ("av", 7), ("ta",))
        at(30, ("evac", ("lru", 1)), ("evac", ("att", 0)), ("tm",))
        at(33, ("evac", ("out", 0)))
        at(34, ("evac", ("out", 1)))
        g = 0
        for name, kind, n in MIXER:
            for i in range(n):
                steps.append(("G", (L, name), i))
                g += 1
                steps += [(s[0], L) + s[1:] for s in side.get(g, [])]
        steps.append(("norm", 2 * L + 1))
        if L == 0:
            pend = []
            order = dense_order()
            for name, kind, n in order:
                if name[0] == "down" and name[2] == 0:
                    if name[1] == DSTEPS:
                        steps += pend
                        pend = []
                    steps.append(("th", L, name[1]))
                for i in range(n):
                    steps.append(("G", (L, name), i))
                    if i == 0:
                        steps += pend
                        pend = []
                pend = [("evac", L, name)]
            steps += pend
    return steps


STEPS = schedule()


def tables():
    first_half, last_half, pair, freed, order, kinds = {}, {}, {}, {}, [], {}
    uses = [0, 0, 0]
    h = 0
    todo = []
    for L in range(DEPTH):
        todo += [((L, n), k, c, 2) for n, k, c in MIXER]
        if L == 0:
            todo += [((L, n), k, c, 3) for n, k, c in dense_order()]
    ring = {2: 0, 3: 0}
    for key, kind, parts, width in todo:
        first_half[key], h = h, h + 2 * parts
        last_half[key] = h
        kinds[key] = kind
        n = 2 if kind == "w" else 1
        pair[key], freed[key] = [], []
        for _ in range(n):
            p = ring[width] % width
            ring[width] += 1
            pair[key].append(p)
            freed[key].append(uses[p])
            uses[p] += TB
    t = {}
    count = {"norm": 4, "tx": 2, "ty": 2, "tq": 1, "ap": 2, "av": 1, "ta": 1, "tm": 4}
    n = 0
    for s in STEPS:
        c = (1 if s[2] == DSTEPS else 2) * 1 if s[0] == "th" else count.get(s[0], 0)
        if s[0] == "th":
            c = TB
        if c:
            t[s] = n
            n += c
    return first_half, last_half, pair, freed, kinds, t, n, h, uses


FIRST_HALF, LAST_HALF, PAIR, FREED, KIND, TURN, N_TURN, N_HALF, PAIR_USES = tables()
STATIC_PARTS = N_HALF // 2
TOTAL_PARTS = STATIC_PARTS + EXPERTS * E_PARTS
assert E_PARTS % R == 0 and (2 * E_PARTS) % H == 0

C_ID, C_IOTA, C_BEFORE, C_ONES = 0, P, 2 * P, 3 * P
C_MASK = 4 * P
C_COS = C_MASK + TB * GROUPS * T
C_SIN = C_COS + TB * 8
C_LOW = C_SIN + TB * 8
C_END = C_LOW + EXPERTS * EXPERTS
V_CONVW = 0
V_CONVB = V_CONVW + DEPTH * 4 * KT
V_BR = V_CONVB + DEPTH * KT
V_BI = V_BR + DEPTH * 2 * KT
V_LAM = V_BI + DEPTH * 2 * KT
V_ROUTER = V_LAM + DEPTH * 2 * KT
V_END = V_ROUTER + KT * EXPERTS

U_COMB, U_SLOT, U_HID, U_GATH = 0, 4, 5, 5 + ESTEPS
E_TURNS = 7 + ESTEPS
E_END = {key: 4 * (i + 1) for i, key in enumerate(expert_order())}
assert E_TURNS % 2 == 0


def build(nc, stream, gates_w, x_in, norms, consts_in, vecs_in, out):
    with ExitStack() as ctx:
        def keep(name, shape, dt=F32, into=ctx):
            return into.enter_context(nc.sbuf_tensor(name, shape, dt))

        def sem(name):
            return ctx.enter_context(nc.semaphore(name))

        raw = keep("raw", [P, R, PART])
        w_hi = keep("w_hi", [P, H, HALF], F32R)
        w_lo = keep("w_lo", [P, H, HALF], F32R)
        x = keep("x", [P, TB, D])
        a_hi = keep("a_hi", [P, KT, T], F32R)
        a_lo = keep("a_lo", [P, KT, T], F32R)
        xn = keep("xn", [P, TB, D])
        gain = keep("gain", [P, D])
        const = keep("const", [P, C_END])
        vec = keep("vec", [P, V_END])
        NC = DEPTH * 2 * KT
        rate = keep("rate", [P, 3, NC])
        small = keep("small", [P, 64])
        with ExitStack() as m:
            wg = keep("wg", [P, 2, 2, KT, P], into=m)
        with ExitStack() as m:
            sm = keep("sm", [P, 2, GROUPS * T], into=m)
            pt = keep("pt", [P, 2 * GROUPS, P], into=m)
            att = keep("att", [P, TB, T], into=m)
            att_hi = keep("att_hi", [P, 2, T], F32R, m)
            att_lo = keep("att_lo", [P, 2, T], F32R, m)
        keep("wg_place", [P, 4 * KT * P])
        arena = ExitStack()
        with arena:
            qk = keep("qk", [P, TB, QK], into=arena)
            v = keep("v", [P, TB, VW], into=arena)
            gy = keep("gy", [P, KT, T], into=arena)
            with ExitStack() as m:
                rg = keep("rg", [P, KT, T], into=m)
                ig = keep("ig", [P, KT, T], into=m)
                tq_ = keep("tanh", [P, 2, T], into=m)
                dq_ = keep("den", [P, 2, T], into=m)
            with ExitStack() as m:
                qkT = keep("qkT", [P, HEADS // 2, 2, T], into=m)
                sg0 = keep("sg0", [P, TB, D], into=m)
            keep("u_place", [P, 2 * KT * T + 4 * T], into=arena)
            with ExitStack() as m:
                xT = keep("xT", [P, KT, T + 3], into=m)
                xc = keep("xc", [P, KT, T], into=m)
            with ExitStack() as m:
                lru_lo = keep("lru_lo", [P, KT, T], F32R, m)
                keep("gap", [P, KT * 3], into=m)
                lru_hi = keep("lru_hi", [P, KT, T], F32R, m)
        with ExitStack() as m:
            hid = [keep(f"hid{i}", [P, TB, CB], into=m) for i in range(2)]
            hT_hi = [keep(f"hT_hi{i}", [P, 4, T], F32R, m) for i in range(2)]
            hT_lo = [keep(f"hT_lo{i}", [P, 4, T], F32R, m) for i in range(2)]
        with ExitStack() as m:
            xn_hi = keep("xn_hi", [P, TB, D], F32R, m)
            xn_lo = keep("xn_lo", [P, TB, D], F32R, m)
            g_hi = keep("g_hi", [P, KT, P], F32R, m)
            g_lo = keep("g_lo", [P, KT, P], F32R, m)
            eh = [keep(f"eh{i}", [P, CB], into=m) for i in range(2)]
            eT_hi = [keep(f"eT_hi{i}", [P, 4, P], F32R, m) for i in range(2)]
            eT_lo = [keep(f"eT_lo{i}", [P, 4, P], F32R, m) for i in range(2)]
            y_hi = keep("y_hi", [P, D], F32R, m)
            y_lo = keep("y_lo", [P, D], F32R, m)
            sel = keep("sel", [P, TB, P], F32R, m)
            selT = keep("selT", [P, T], F32R, m)
            rw = keep("rw", [P, 2, KT * EXPERTS], F32R, m)
            lg = keep("lg", [P, TB, EXPERTS], into=m)
            cmp_ = keep("cmp", [P, TB, EXPERTS, EXPERTS], into=m)
            cmp2 = keep("cmp2", [P, TB, EXPERTS, EXPERTS], into=m)
            mask = keep("mask", [P, TB, EXPERTS], into=m)
            top = keep("top", [P, TB, 8], into=m)
            wsum = keep("wsum", [P, TB, 4], into=m)
            slot = keep("slot", [P, TB, EXPERTS + 2], into=m)
            share = keep("share", [P, TB, EXPERTS + 2], into=m)
            most = keep("most", [P, 2], into=m)
            most_i = keep("most_i", [P, 2], I32, m)

        bank = [ctx.enter_context(nc.psum_tensor(f"bank{i}", [P, CB], F32)) for i in range(4)]
        mid = ctx.enter_context(nc.psum_tensor("mid", [P, 2, CB], F32))
        turn = [ctx.enter_context(nc.psum_tensor(f"turn{i}", [P, CB], F32)) for i in range(2)]

        def acc(p, b):
            return mid[:, b, :] if p == 2 else bank[2 * p + b][:, :]

        ident = const[:, C_ID:C_ID + P]
        iota = const[:, C_IOTA:C_IOTA + P]
        before = const[:, C_BEFORE:C_BEFORE + P]
        ones = const[:, C_ONES:C_ONES + P]
        band = const[:, C_MASK:C_COS].rearrange("p (b k) -> p b k", b=TB)
        cos = const[:, C_COS:C_SIN].rearrange("p (b k) -> p b k", b=TB)
        sin = const[:, C_SIN:C_LOW].rearrange("p (b k) -> p b k", b=TB)
        lower = const[:, C_LOW:C_END].rearrange("p (a b) -> p a b", a=EXPERTS)
        convw = vec[:, V_CONVW:V_CONVB].rearrange("p (l j n) -> p l j n", l=DEPTH, j=4)
        convb = vec[:, V_CONVB:V_BR].rearrange("p (l n) -> p l n", l=DEPTH)
        b_r = vec[:, V_BR:V_BI].rearrange("p (l d n) -> p l d n", l=DEPTH, d=2)
        b_i = vec[:, V_BI:V_LAM].rearrange("p (l d n) -> p l d n", l=DEPTH, d=2)
        lam = vec[:, V_LAM:V_ROUTER]
        router = vec[:, V_ROUTER:V_END]
        ss, ms, sd, rstd = (small[:, 2 * i:2 * i + 2] for i in range(4))
        mx, nm, rs, rr = (small[:, 8 + 2 * i:10 + 2 * i] for i in range(4))

        s_const = sem("consts_landed")
        s_x = sem("x_landed")
        s_gain = sem("gain_landed")
        s_wg = sem("gate_weights_landed")
        landed = [sem(f"part_landed{i}") for i in range(R)]
        hi_ready = sem("hi_ready")
        lo_ready = sem("lo_ready")
        used = sem("halves_used")
        pair_free = [sem(f"pair_free{i}") for i in range(3)]
        turned = sem("turned")
        turn_hi = sem("turn_hi")
        turn_free = [sem(f"turn_free{i}") for i in range(2)]
        chain = sem("vector_chain")
        rate_s = sem("rate_exp")
        rate_ready = sem("rate_ready")
        ms_ready = sem("mean_square_ready")
        sd_ready = sem("deviation_ready")
        xn_ready = sem("xn_ready")
        xc_ready = sem("xc_ready")
        mid_full = sem("mid_full")
        mid_free = sem("mid_free")
        tanh_ready = sem("tanh_ready")
        decay_ready = sem("decay_ready")
        q_ready = sem("q_ready")
        ix_ready = sem("gated_input_ready")
        sq_ready = sem("root_ready")
        scanned = sem("scanned")
        rope_s = sem("rope_parts")
        rope_done = sem("rope_done")
        gelu_ready = sem("gelu_ready")
        lru_full = sem("lru_full")
        lru_hi_ready = sem("lru_hi_ready")
        lru_ready = sem("lru_ready")
        nm_ready = sem("neg_max_ready")
        p_ready = sem("probs_ready")
        merged = sem("merged")
        silu_ready = sem("silu_ready")
        xn_hi_ready = sem("xn_hi_ready")
        xn_lo_ready = sem("xn_lo_ready")
        rw_ready = sem("router_weights_ready")
        logit_full = sem("logits_full")
        top_ready = sem("top_ready")
        share_exp = sem("share_exp")
        mask_ready = sem("mask_ready")
        rank_full = sem("rank_full")
        route_ready = sem("route_ready")
        sel_ready = sem("sel_ready")
        g_hi_ready = sem("gathered_hi")
        e_silu = sem("expert_silu")
        e_hid = sem("expert_hidden")
        eT_hi_ready = sem("expert_hidden_hi")
        y_hi_ready = sem("y_hi_ready")
        y_ready = sem("y_ready")
        zeroed = sem("zeroed")
        out_sem = sem("out_landed")
        done = sem("final_ready")

        def product_done(eng, key):
            eng.wait_ge(used, LAST_HALF[key])

        def bank_full(eng, idx):
            eng.wait_ge(turned, idx + 1)

        def bank_read(eng, idx):
            eng.wait_ge(turn_free[idx % 2], idx // 2 + 1)

        def split_hi(act, h, e=0):
            part = h // 2
            if h % 2 == 0:
                act.wait_ge(landed[part % R], 16 * (part // R + 1) + e * (16 * E_PARTS // R))
            if h >= H:
                act.wait_ge(used, h - H + 1 + e * 2 * E_PARTS)
            lo = (h % 2) * HALF
            nc.scalar.activation(w_hi[:, h % H, :], raw[:, part % R, lo:lo + HALF],
                                 ACT.Copy).then_inc(hi_ready, 1)

        def split_lo(dve, h, e=0):
            part = h // 2
            lo = (h % 2) * HALF
            dve.wait_ge(hi_ready, h + 1 + e * 2 * E_PARTS)
            nc.vector.tensor_tensor(w_lo[:, h % H, :], raw[:, part % R, lo:lo + HALF],
                                    w_hi[:, h % H, :].bitcast(F32), ALU.subtract).then_inc(lo_ready, 1)

        def mm3(out_, s_hi, s_lo, wh, wl, start, stop):
            nc.tensor.matmul(out_, s_hi, wh, start=start, stop=False)
            nc.tensor.matmul(out_, s_hi, wl, start=False, stop=False)
            return nc.tensor.matmul(out_, s_lo, wh, start=False, stop=stop)

        def half_of(key, part):
            return FIRST_HALF[key] + 2 * part

        def scans_before(L, d, pr):
            return (L * 2 + d) * KT + 2 * (pr + 1)

        def evac_value(key, n=0):
            return FREED[key][n] + TB

        def evacuated(eng, key, n=0):
            eng.wait_ge(pair_free[PAIR[key][n]], evac_value(key, n))

        def mid_before(L, use):
            lru = min(use, 8)
            at_ = use - lru
            return L * 16 + use, L * (8 * 4 + 8) + 4 * lru + at_

        def xslice(n):
            return slice(n * CB, (n + 1) * CB)

        H0 = N_HALF
        T0 = N_TURN

        block = ctx.enter_context(nc.Block())

        @block.sync
        def _(sp):
            def load(slot_, part, group):
                sp.dma_start(raw[:, slot_, :], stream[part, :, :]).then_inc(landed[slot_], 16)

            for i in range(R):
                load(i, i, 0)
            with sp.Fori(1, TOTAL_PARTS // R) as g:
                for i in range(R):
                    sp.wait_ge(lo_ready, 2 * R * g + (2 * (i + 1) - 2 * R))
                    load(i, g * R + i, g)
            for part in range(TOTAL_PARTS // R * R, TOTAL_PARTS):
                sp.wait_ge(lo_ready, 2 * (part - R + 1))
                load(part % R, part, 0)
            sp.wait_ge(route_ready, 1)
            n = sp.value_load(most_i[0:1, 0:1], min_val=0, max_val=T)
            with sp.If(n > NPASS_TOKENS):
                with sp.Fori(0, EXPERTS) as e:
                    for i in range(E_PARTS):
                        part = TOTAL_PARTS + i
                        sp.wait_ge(lo_ready, 2 * (part - R + 1) + e * 2 * E_PARTS)
                        load(part % R, STATIC_PARTS + e * E_PARTS + i, 0)
            for b in range(TB):
                sp.wait_ge(done, b + 1)
                sp.dma_start(out[b * P:(b + 1) * P, :], xn[:, b, :]).then_inc(out_sem, 16)
            sp.wait_ge(out_sem, 16 * TB)

        @block.gpsimd
        def _(pool):
            def load_gain(k):
                pool.dma_start(gain[:, :], norms[k:k + 1, :].to_broadcast([P, D])).then_inc(s_gain, 16)

            load_gain(0)
            pool.dma_start(wg[:, :, :, :, :].rearrange("p a b n d -> p (a b n d)"),
                           gates_w[0, :, :]).then_inc(s_wg, 16)
            for s in STEPS:
                if s[0] == "norm":
                    pool.wait_ge(xn_ready, TB * (s[1] + 1))
                    load_gain(s[1] + 1)
                elif s[0] == "G" and s[1] == (0, ("out", 0)) and s[2] == 0:
                    pool.wait_ge(used, LAST_HALF[(0, ("att", 0))])
                    pool.dma_start(wg[:, :, :, :, :].rearrange("p a b n d -> p (a b n d)"),
                                   gates_w[1, :, :]).then_inc(s_wg, 16)
                elif s[0] == "la":
                    _, L, d, pr = s
                    pool.wait_ge(mid_free, mid_before(L, d * 4 + pr)[1] + 4)
                    ii = ig[:, 2 * pr:2 * pr + 2, :]
                    nc.gpsimd.tensor_tensor(ii, ii, xc[:, 2 * pr:2 * pr + 2, :],
                                            ALU.mult).then_inc(ix_ready, 1)
                elif s[0] == "rope":
                    L = s[1]
                    for n in range(3):
                        evacuated(pool, (L, ("qkv", n)))
                    bank_read(pool, TURN[("tx", L, 1)] + 1)
                    bank_read(pool, TURN[("tx", L, 1)])
                    z = qk[:, :, :].rearrange("p b (h w) -> p b h w", w=DH)
                    NH = QK // DH
                    t1, t2 = z[:, :, :, 0:8], z[:, :, :, 8:16]
                    cb = cos.rearrange("p b (o k) -> p b o k", o=1).to_broadcast([P, TB, NH, 8])
                    sb_ = sin.rearrange("p b (o k) -> p b o k", o=1).to_broadcast([P, TB, NH, 8])
                    flat = xn[:, :, :].rearrange("p b w -> p (b w)")
                    W = TB * NH * 8
                    tmp = [flat[:, i * W:(i + 1) * W].rearrange("p (b h k) -> p b h k", b=TB, k=8)
                           for i in range(4)]
                    for o, (a, c) in zip(tmp, ((t1, cb), (t2, sb_), (t2, cb), (t1, sb_))):
                        nc.gpsimd.tensor_tensor(o, a, c, ALU.mult).then_inc(rope_s, 1)
                    pool.wait_ge(rope_s, 4 * (L + 1))
                    nc.gpsimd.tensor_tensor(t1, tmp[0], tmp[1], ALU.subtract).then_inc(rope_done, 1)
                    nc.gpsimd.tensor_tensor(t2, tmp[2], tmp[3], ALU.add).then_inc(rope_done, 1)
            pool.wait_ge(s_gain, 16 * (2 * DEPTH + 1))

        @block.scalar
        def _(act):
            act.dma_start(x[:, :, :], x_in.rearrange("(b p) d -> p b d", p=P)).then_inc(s_x, 16)
            act.dma_start(const[:, :], consts_in).then_inc(s_const, 16)
            act.dma_start(vec[:, :], vecs_in).then_inc(s_const, 16)

            hi = [0]

            def turn_high(dst, src, idx):
                bank_full(act, idx)
                nc.scalar.activation(dst, src, ACT.Copy).then_inc(turn_hi, 1)
                hi[0] += 1

            act.wait_ge(chain, 1)
            nc.scalar.activation(rate[:, 1, :], rate[:, 0, :], ACT.Exp).then_inc(rate_s, 1)

            for s in STEPS:
                kind = s[0]
                if kind == "norm":
                    act.wait_ge(ms_ready, s[1] + 1)
                    nc.scalar.activation(sd, ms, ACT.Sqrt).then_inc(sd_ready, 1)
                    for b in range(TB):
                        for j in range(2):
                            idx = TURN[s] + 2 * b + j
                            turn_high(a_hi[:, 4 * j:4 * j + 4, b * P:(b + 1) * P],
                                      turn[idx % 2][:, :].rearrange("p (k t) -> p k t", k=4), idx)
                elif kind == "G":
                    h = half_of(s[1], s[2])
                    split_hi(act, h)
                    split_hi(act, h + 1)
                elif kind == "evac":
                    L, name = s[1:]
                    key = (L, name)
                    what, n = name[0], name[1]
                    p = PAIR[key][0]
                    if what in ("x", "y", "qkv"):
                        product_done(act, key)
                        if what == "y" and n == 0:
                            act.wait_ge(rope_done, 2 * (L + 1))
                        w = CB
                        if what != "qkv":
                            dst = xn[:, 0, xslice(n)]
                        else:
                            w = CB if n < 4 else VW - CB
                            dst = qk[:, 0, xslice(n)] if n < 3 else v[:, 0, (n - 3) * CB:(n - 3) * CB + w]
                        nc.scalar.activation(dst, acc(p, 0)[:, 0:w], ACT.Copy).then_inc(pair_free[p], 1)
                    elif what in ("g0", "g1"):
                        product_done(act, key)
                        if what == "g1":
                            bank_read(act, TURN[("tq", L, 4)])
                            bank_read(act, TURN[("tq", L, 5)])
                        else:
                            act.wait_ge(scanned, scans_before(L, 1, 3))
                        for b in range(TB):
                            dst = qk[:, b, xslice(n)] if what == "g1" else sg0[:, b, xslice(n)]
                            nc.scalar.activation(dst, acc(p, b), ACT.Sigmoid).then_inc(pair_free[p], 1)
                    elif what == "gate":
                        product_done(act, key)
                        w = CB if n < DSTEPS else 2 * P
                        if n >= 2:
                            bank_full(act, TURN[("th", 0, n - 2)] + 1)
                        for b in range(TB):
                            nc.scalar.activation(hid[n % 2][:, b, 0:w], acc(p, b)[:, 0:w],
                                                 ACT.Silu).then_inc(pair_free[p], 1)
                elif kind == "ty":
                    _, L, c = s
                    for k in range(2):
                        idx = TURN[s] + k
                        n = 4 * c + 2 * k
                        bank_full(act, idx)
                        nc.scalar.activation(gy[:, n:n + 2, :],
                                             turn[idx % 2][:, :].rearrange("p (n t) -> p n t", n=2),
                                             ACT.Gelu_apprx_tanh).then_inc(turn_free[idx % 2], 1)
                elif kind == "lg":
                    _, L, d, pr = s
                    k = (L * 2 + d) * 4 + pr
                    act.wait_ge(mid_full, mid_before(L, d * 4 + pr)[0] + 1)
                    if k >= 4:
                        act.wait_ge(scanned, 2 * (k - 3))
                    for q in range(2):
                        n = 2 * pr + q
                        for g, (dst, bias) in enumerate(((rg, b_r), (ig, b_i))):
                            nc.scalar.activation(dst[:, n, :], mid[:, q, g * T:(g + 1) * T], ACT.Sigmoid,
                                                 bias=bias[:, L, d, n:n + 1]).then_inc(mid_free, 1)
                elif kind == "la":
                    _, L, d, pr = s
                    k = (L * 2 + d) * 4 + pr
                    if k == 0:
                        act.wait_ge(rate_ready, 2)
                    if k >= 1:
                        act.wait_ge(sq_ready, k)
                    act.wait_ge(mid_free, mid_before(L, d * 4 + pr)[1] + 4)
                    for q in range(2):
                        n = 2 * pr + q
                        col = (L * 2 + d) * KT + n
                        nc.scalar.activation(tq_[:, q, :], rg[:, n, :], ACT.Tanh,
                                             scale=rate[:, 0, col:col + 1]).then_inc(tanh_ready, 1)
                    act.wait_ge(tanh_ready, 2 * (k + 1))
                    for q in range(2):
                        n = 2 * pr + q
                        col = (L * 2 + d) * KT + n
                        nc.scalar.activation(rg[:, n, :], rg[:, n, :], ACT.Exp,
                                             scale=rate[:, 1, col:col + 1]).then_inc(decay_ready, 1)
                elif kind == "lb":
                    _, L, d, pr = s
                    k = (L * 2 + d) * 4 + pr
                    act.wait_ge(q_ready, k + 1)
                    nc.scalar.activation(dq_[:, :, :], tq_[:, :, :], ACT.Sqrt).then_inc(sq_ready, 1)
                elif kind == "lf":
                    _, L, pr = s
                    act.wait_ge(lru_full, 4 * L + pr + 1)
                    nc.scalar.activation(lru_hi[:, 2 * pr:2 * pr + 2, :], gy[:, 2 * pr:2 * pr + 2, :],
                                         ACT.Copy).then_inc(lru_hi_ready, 1)
                elif kind == "tq" and s[2] % 2 == 0:
                    idx = TURN[s]
                    bank_full(act, idx)
                    act.wait_ge(scanned, scans_before(s[1], 1, 3))
                    nc.scalar.activation(qkT[:, s[2], :, :],
                                         turn[idx % 2][:, :].rearrange("p (a t) -> p a t", a=2),
                                         ACT.Copy).then_inc(turn_free[idx % 2], 1)
                elif kind == "as":
                    _, L, u = s
                    k = 8 * L + u
                    act.wait_ge(nm_ready, k + 1)
                    nc.scalar.activation(sm[:, u % 2, :], sm[:, u % 2, :], ACT.Exp,
                                         bias=nm[:, u % 2:u % 2 + 1], scale=SCALE,
                                         accum_out=rs[:, u % 2:u % 2 + 1]).then_inc(p_ready, 1)
                elif kind == "ap":
                    idx = TURN[s]
                    bank_full(act, idx)
                    nc.scalar.activation(pt[:, 0:4, :],
                                         turn[idx % 2][:, :].rearrange("p (a t) -> p a t", a=4),
                                         ACT.Copy).then_inc(turn_free[idx % 2], 1)
                elif kind == "ta":
                    turn_high(att_hi[:, :, :],
                              turn[TURN[s] % 2][:, :].rearrange("p (a t) -> p a t", a=2), TURN[s])
                elif kind == "tm":
                    for b in range(TB):
                        for j in range(2):
                            idx = TURN[s] + 2 * b + j
                            turn_high(a_hi[:, 4 * j:4 * j + 4, b * P:(b + 1) * P],
                                      turn[idx % 2][:, :].rearrange("p (k t) -> p k t", k=4), idx)
                elif kind == "th":
                    c = s[2]
                    w = 4 if c < DSTEPS else 2
                    for b in range(TB):
                        idx = TURN[s] + b
                        if b == 0 and c >= 2:
                            product_done(act, (0, ("down", c - 2, 1)))
                        turn_high(hT_hi[c % 2][:, 0:w, b * P:(b + 1) * P],
                                  turn[idx % 2][:, 0:w * P].rearrange("p (k t) -> p k t", k=w), idx)

            for b in range(TB):
                act.wait_ge(xn_ready, TB * 2 * DEPTH - TB + b + 1)
                nc.scalar.activation(xn_hi[:, b, :], xn[:, b, :], ACT.Copy).then_inc(xn_hi_ready, 1)
            nc.scalar.activation(rw[:, 0, :], router, ACT.Copy).then_inc(rw_ready, 1)
            act.wait_ge(top_ready, 1)
            nc.scalar.activation(lg[:, :, :], lg[:, :, :], ACT.Exp).then_inc(share_exp, 1)

            def gather(n, e, first):
                for j in range(2):
                    bank_full_e(act, first + j, e)
                    t_ = (first + j) % 2
                    nc.scalar.activation(g_hi[:, 4 * j:4 * j + 4, :],
                                         turn[t_][:, :].rearrange("p (k t) -> p k t", k=4),
                                         ACT.Copy).then_inc(g_hi_ready, 1)

            def bank_full_e(eng, idx, e):
                eng.wait_ge(turned, idx + 1 + e * E_TURNS)

            def experts(pas):
                g0 = pas * (EXPERTS + 1)
                t0 = T0 + pas * (2 + EXPERTS * E_TURNS + 4)
                h0 = H0 + pas * EXPERTS * 2 * E_PARTS
                s0 = pas * EXPERTS * ESTEPS
                gather(g0, 0, t0)
                tl = t0 + 2
                with act.Fori(0, EXPERTS) as e:
                    h = h0
                    for what, c in expert_order():
                        if what == "down":
                            idx = tl + U_HID + c
                            bank_full_e(act, idx, e)
                            nc.scalar.activation(eT_hi[c % 2][:, :, :],
                                                 turn[idx % 2][:, :].rearrange("p (k t) -> p k t", k=4),
                                                 ACT.Copy).then_inc(eT_hi_ready, 1)
                            if c == ESTEPS - 1:
                                gather(g0 + 1, e, tl + U_GATH)
                        for _ in range(4):
                            split_hi(act, h, e)
                            h += 1
                        if what == "up":
                            act.wait_ge(used, h0 + E_END[("gate", c)] + e * 2 * E_PARTS)
                            nc.scalar.activation(eh[c % 2][:, :], bank[2 * (c % 2)][:, :],
                                                 ACT.Silu).then_inc(e_silu, 1)
                    act.wait_ge(used, h + e * 2 * E_PARTS)
                    for n in range(2):
                        nc.scalar.activation(y_hi[:, xslice(n)], mid[:, n, :],
                                             ACT.Copy).then_inc(y_hi_ready, 1)

            experts(0)
            act.wait_ge(route_ready, 1)
            n = act.value_load(most_i[0:1, 0:1], min_val=0, max_val=T)
            with act.If(n > NPASS_TOKENS):
                experts(1)
            act.wait_ge(ms_ready, 2 * DEPTH + 1)
            nc.scalar.activation(sd, ms, ACT.Sqrt).then_inc(sd_ready, 1)

        @block.tensor
        def _(pe):
            def turn_bank(idx):
                if idx >= 2:
                    pe.wait_ge(turn_free[idx % 2], idx // 2)
                return turn[idx % 2]

            def gemm(key, part, s_hi, s_lo):
                kind = KIND[key]
                parts = (LAST_HALF[key] - FIRST_HALF[key]) // 2
                kts, cols, width = {"n": (2, CB, 1), "h": (4, 2 * P, 1), "w": (1, CB, 2)}[kind]
                if part == 0:
                    for n in range(width):
                        if FREED[key][n]:
                            pe.wait_ge(pair_free[PAIR[key][n]], FREED[key][n])
                for hh in range(2):
                    h = half_of(key, part) + hh
                    pe.wait_ge(lo_ready, h + 1)
                    for k in range(kts):
                        kt = (part * 2 + hh) * kts + k
                        for n in range(width):
                            o = (k * width + n) * cols
                            wh = w_hi[:, h % H, o:o + cols]
                            wl = w_lo[:, h % H, o:o + cols]
                            for b in range(TB):
                                last = kt == parts * 2 * kts - 1
                                ins = mm3(acc(PAIR[key][n], b)[:, 0:cols],
                                          s_hi[:, kt, b * P:(b + 1) * P], s_lo[:, kt, b * P:(b + 1) * P],
                                          wh, wl, start=kt == 0, stop=last)
                    ins.then_inc(used, 1)

            pe.wait_ge(s_const, 32)
            for s in STEPS:
                kind = s[0]
                if kind == "norm":
                    for b in range(TB):
                        pe.wait_ge(xn_ready, TB * s[1] + b + 1)
                        for j in range(2):
                            idx = TURN[s] + 2 * b + j
                            t_ = turn_bank(idx)
                            for k in range(4):
                                kt = 4 * j + k
                                ins = nc.tensor.transpose(t_[:, k * P:(k + 1) * P],
                                                          xn[:, b, kt * P:(kt + 1) * P], ident)
                            ins.then_inc(turned, 1)
                    for i in range(2):
                        bank_read(pe, TURN[s] + 2 + i)
                elif kind == "G":
                    key = s[1]
                    what = key[1][0]
                    if what == "lru":
                        if s[2] == 0 and key[1][1] == 0:
                            pe.wait_ge(lru_ready, 4 * (key[0] + 1))
                        gemm(key, s[2], lru_hi, lru_lo)
                    elif what == "att":
                        gemm(key, s[2], att_hi, att_lo)
                    elif what == "down":
                        gemm(key, s[2], hT_hi[key[1][1] % 2], hT_lo[key[1][1] % 2])
                    else:
                        gemm(key, s[2], a_hi, a_lo)
                elif kind in ("tx", "ty"):
                    _, L, c = s
                    evacuated(pe, (L, ("x" if kind == "tx" else "y", c)))
                    for k in range(2):
                        idx = TURN[s] + k
                        t_ = turn_bank(idx)
                        for q in range(2):
                            n = 4 * c + 2 * k + q
                            for b in range(TB):
                                ins = nc.tensor.transpose(t_[:, q * T + b * P:q * T + (b + 1) * P],
                                                          xn[:, b, n * P:(n + 1) * P], ident)
                        ins.then_inc(turned, 1)
                elif kind == "lg":
                    _, L, d, pr = s
                    uses, frees = mid_before(L, d * 4 + pr)
                    if frees:
                        pe.wait_ge(mid_free, frees)
                    pe.wait_ge(xc_ready, KT * L + 2 * pr + 2)
                    pe.wait_ge(s_wg, 16 * (L + 1))
                    for q in range(2):
                        n = 2 * pr + q
                        for g in range(2):
                            ins = nc.tensor.matmul(mid[:, q, g * T:(g + 1) * T], wg[:, d, g, n, :],
                                                   xc[:, n, :], start=True, stop=True)
                    ins.then_inc(mid_full, 1)
                elif kind == "tq":
                    _, L, j = s
                    pe.wait_ge(rope_done, 2 * (L + 1))
                    idx = TURN[s]
                    t_ = turn_bank(idx)
                    for a in range(2):
                        for b in range(TB):
                            o = a * (QK // 2) + j * P
                            ins = nc.tensor.transpose(t_[:, a * T + b * P:a * T + (b + 1) * P],
                                                      qk[:, b, o:o + P], ident)
                    ins.then_inc(turned, 1)
                elif kind == "as":
                    _, L, u = s
                    b, sl = u // SLOTS, u % SLOTS
                    uses, frees = mid_before(L, 8 + u)
                    pe.wait_ge(mid_free, frees)
                    if u == 0:
                        for j in range(4, 6):
                            bank_read(pe, TURN[("tq", L, j)])
                    flat = mid[:, :, :].rearrange("p a c -> p (a c)")
                    for g in range(GROUPS):
                        head = g * SLOTS + sl
                        o = DH * (head % 2)
                        ins = nc.tensor.matmul(flat[:, g * T:(g + 1) * T],
                                               qkT[o:o + DH, head // 2, 0, b * P:(b + 1) * P],
                                               qkT[o:o + DH, head // 2, 1, :], start=True, stop=True)
                    ins.then_inc(mid_full, 1)
                elif kind == "ap":
                    _, L, u = s
                    pe.wait_ge(p_ready, 8 * L + u + 1)
                    for i, n in enumerate((4, 2)):
                        idx = TURN[s] + i
                        t_ = turn_bank(idx)
                        for k in range(n):
                            o = (4 * i + k) * P
                            ins = nc.tensor.transpose(t_[:, k * P:(k + 1) * P], sm[:, u % 2, o:o + P], ident)
                        ins.then_inc(turned, 1)
                elif kind == "av":
                    _, L, u = s
                    b, sl = u // SLOTS, u % SLOTS
                    for i in range(2):
                        bank_read(pe, TURN[("ap", L, u)] + i)
                    idx = TURN[s]
                    t_ = turn_bank(idx)
                    for i in range(2 * GROUPS):
                        g, kb = i // 2, i % 2
                        o = (g * SLOTS + sl) * DH
                        ins = nc.tensor.matmul(t_[:, 0:DH], pt[:, i, :], v[:, kb, o:o + DH],
                                               start=i == 0, stop=i == 2 * GROUPS - 1)
                    ins.then_inc(turned, 1)
                elif kind == "ta":
                    _, L = s
                    for u in range(6, 8):
                        bank_read(pe, TURN[("av", L, u)])
                    idx = TURN[s]
                    t_ = turn_bank(idx)
                    for a in range(2):
                        for b in range(TB):
                            ins = nc.tensor.transpose(t_[:, a * T + b * P:a * T + (b + 1) * P],
                                                      att[:, b, a * P:(a + 1) * P], ident)
                    ins.then_inc(turned, 1)
                    bank_read(pe, idx)
                elif kind == "tm":
                    L = s[1]
                    for b in range(TB):
                        for j in range(2):
                            pe.wait_ge(merged, L * 4 + 2 * b + j + 1)
                            idx = TURN[s] + 2 * b + j
                            t_ = turn_bank(idx)
                            for k in range(4):
                                kt = 4 * j + k
                                ins = nc.tensor.transpose(t_[:, k * P:(k + 1) * P],
                                                          qk[:, b, kt * P:(kt + 1) * P], ident)
                            ins.then_inc(turned, 1)
                    for i in range(2):
                        bank_read(pe, TURN[s] + 2 + i)
                elif kind == "th":
                    _, L, c = s
                    evacuated(pe, (L, ("up", c)))
                    w = 4 if c < DSTEPS else 2
                    for b in range(TB):
                        idx = TURN[s] + b
                        t_ = turn_bank(idx)
                        for k in range(w):
                            ins = nc.tensor.transpose(t_[:, k * P:(k + 1) * P],
                                                      hid[c % 2][:, b, k * P:(k + 1) * P], ident)
                        ins.then_inc(turned, 1)
                    for b in range(TB):
                        bank_read(pe, TURN[s] + b)

            pe.wait_ge(rw_ready, 2)
            for b in range(TB):
                for kt in range(KT):
                    c = slice(kt * EXPERTS, (kt + 1) * EXPERTS)
                    ins = mm3(mid[:, b, 0:EXPERTS], a_hi[:, kt, b * P:(b + 1) * P],
                              a_lo[:, kt, b * P:(b + 1) * P], rw[:, 0, c], rw[:, 1, c],
                              start=kt == 0, stop=kt == KT - 1)
            ins.then_inc(logit_full, 1)
            pe.wait_ge(mask_ready, 1)
            nc.tensor.matmul(mid[:, 0, 0:EXPERTS], before, mask[:, 0, :], start=True, stop=True)
            nc.tensor.matmul(mid[:, 1, 0:EXPERTS], before, mask[:, 1, :], start=True, stop=False)
            nc.tensor.matmul(mid[:, 1, 0:EXPERTS], ones, mask[:, 0, :], start=False, stop=True)
            nc.tensor.matmul(bank[0][:, 0:EXPERTS], ones, mask[:, 0, :], start=True, stop=False)
            nc.tensor.matmul(bank[0][:, 0:EXPERTS], ones, mask[:, 1, :], start=False,
                             stop=True).then_inc(rank_full, 1)

            def wait_turn(idx, e):
                pe.wait_ge(turn_free[idx % 2], idx // 2 + e * (E_TURNS // 2))
                return turn[idx % 2]

            def read_out(idx, e):
                pe.wait_ge(turn_free[idx % 2], idx // 2 + 1 + e * (E_TURNS // 2))

            def gather(idx, e, sel_n):
                pe.wait_ge(sel_ready, sel_n)
                for j in range(2):
                    t_ = wait_turn(idx + j, e)
                    for k in range(4):
                        kt = 4 * j + k
                        for i, (src, b) in enumerate([(s_, b) for b in range(TB) for s_ in (xn_hi, xn_lo)]):
                            ins = nc.tensor.matmul(t_[:, k * P:(k + 1) * P], src[:, b, kt * P:(kt + 1) * P],
                                                   sel[:, b, :], start=i == 0, stop=i == 2 * TB - 1)
                    ins.then_inc(turned, 1)

            def combine(idx, e, y_n):
                pe.wait_ge(y_ready, y_n)
                for b in range(TB):
                    for n in range(2):
                        i = 2 * b + n
                        t_ = wait_turn(idx + i, e)
                        nc.tensor.matmul(t_[:, :], selT[:, b * P:(b + 1) * P], y_hi[:, xslice(n)],
                                         start=True, stop=False)
                        nc.tensor.matmul(t_[:, :], selT[:, b * P:(b + 1) * P], y_lo[:, xslice(n)],
                                         start=False, stop=True).then_inc(turned, 1)

            def experts(pas):
                g0 = pas * (EXPERTS + 1)
                t0 = T0 + pas * (2 + EXPERTS * E_TURNS + 4)
                h0 = H0 + pas * EXPERTS * 2 * E_PARTS
                s0 = pas * EXPERTS * ESTEPS
                gather(t0, 0, TB * (g0 + 1))
                tl = t0 + 2
                with pe.Fori(0, EXPERTS) as e:
                    h = h0
                    for j in range(2):
                        read_out(t0 + j, e)
                    for what, c in expert_order():
                        if what == "down":
                            idx = tl + U_HID + c
                            t_ = wait_turn(idx, e)
                            pe.wait_ge(e_hid, s0 + c + 1 + e * ESTEPS)
                            for k in range(4):
                                ins = nc.tensor.transpose(t_[:, k * P:(k + 1) * P],
                                                          eh[c % 2][:, k * P:(k + 1) * P], ident)
                            ins.then_inc(turned, 1)
                            if c == ESTEPS - 1:
                                gather(tl + U_GATH, e, TB * (g0 + 2) + e * TB)
                            read_out(idx, e)
                            for hh in range(4):
                                pe.wait_ge(lo_ready, h + 1 + e * 2 * E_PARTS)
                                for n in range(2):
                                    ins = mm3(mid[:, n, :], eT_hi[c % 2][:, hh, :], eT_lo[c % 2][:, hh, :],
                                              w_hi[:, h % H, xslice(n)], w_lo[:, h % H, xslice(n)],
                                              start=c == 0 and hh == 0, stop=c == ESTEPS - 1 and hh == 3)
                                ins.then_inc(used, 1)
                                h += 1
                            continue
                        o_ = bank[2 * (c % 2) + (what == "up")]
                        for hh in range(4):
                            pe.wait_ge(lo_ready, h + 1 + e * 2 * E_PARTS)
                            for k in range(2):
                                kt = 2 * hh + k
                                ins = mm3(o_[:, :], g_hi[:, kt, :], g_lo[:, kt, :],
                                          w_hi[:, h % H, xslice(k)], w_lo[:, h % H, xslice(k)],
                                          start=kt == 0, stop=kt == KT - 1)
                            ins.then_inc(used, 1)
                            h += 1
                        if what == "up" and c == 0:
                            combine(tl + U_COMB, e, 2 + 2 * pas * (EXPERTS + 0) + e * 2)
                            idx = tl + U_SLOT
                            t_ = wait_turn(idx, e)
                            for b in range(TB):
                                ins = nc.tensor.transpose(t_[:, b * P:(b + 1) * P],
                                                          sel[:, b, :].bitcast(F32), ident)
                            ins.then_inc(turned, 1)
                combine(tl + EXPERTS * E_TURNS, 0, 2 + 2 * EXPERTS * (pas + 1))

            experts(0)
            pe.wait_ge(route_ready, 1)
            n = pe.value_load(most_i[0:1, 0:1], min_val=0, max_val=T)
            with pe.If(n > NPASS_TOKENS):
                experts(1)

        @block.vector
        def _(dve):
            links = [0]
            hi = [0]

            def link(ins):
                ins.then_inc(chain, 1)
                links[0] += 1
                dve.wait_ge(chain, links[0])

            def turn_low(dst, dst_hi, src, idx):
                hi[0] += 1
                dve.wait_ge(turn_hi, hi[0])
                nc.vector.tensor_tensor(dst, src, dst_hi.bitcast(F32),
                                        ALU.subtract).then_inc(turn_free[idx % 2], 1)

            def norm(k, final=False):
                for b in range(TB):
                    ins = nc.vector.tensor_tensor_reduce(out=xn[:, b, :], in0=x[:, b, :], in1=x[:, b, :],
                                                         scale=1.0, scalar=0.0, op0=ALU.mult, op1=ALU.add,
                                                         accum_out=ss[:, b:b + 1])
                    link(ins)
                nc.vector.tensor_scalar(ms, ss, 1.0 / D, EPS, ALU.mult, ALU.add).then_inc(ms_ready, 1)
                dve.wait_ge(sd_ready, k + 1)
                link(nc.vector.reciprocal(rstd, sd))
                dve.wait_ge(s_gain, 16 * (k + 1))
                for b in range(TB):
                    nc.vector.scalar_tensor_tensor(out=xn[:, b, :], in0=x[:, b, :], scalar=rstd[:, b:b + 1],
                                                   in1=gain[:, :], op0=ALU.mult,
                                                   op1=ALU.mult).then_inc(done if final else xn_ready, 1)

            dve.wait_ge(s_const, 32)
            r0, r1, r2 = rate[:, 0, :], rate[:, 1, :], rate[:, 2, :]
            nc.vector.scalar_tensor_tensor(out=r0, in0=lam, scalar=-1.0, in1=lam, op0=ALU.mult,
                                           op1=ALU.min).then_inc(chain, 1)
            links[0] += 1
            dve.wait_ge(rate_s, 1)
            link(nc.vector.tensor_scalar(r2, r1, 2.0, None, ALU.add))
            link(nc.vector.reciprocal(r2, r2))
            link(nc.vector.tensor_tensor(r0, r1, r2, ALU.mult))
            link(nc.vector.tensor_tensor(r1, r0, r0, ALU.mult))
            TERMS = 9
            link(nc.vector.tensor_scalar(r2, r1, 1.0 / (2 * TERMS + 1), 1.0 / (2 * TERMS - 1),
                                         ALU.mult, ALU.add))
            for i in range(TERMS - 2, -1, -1):
                link(nc.vector.tensor_tensor(r2, r2, r1, ALU.mult))
                link(nc.vector.tensor_scalar(r2, r2, 1.0 / (2 * i + 1), None, ALU.add))
            link(nc.vector.scalar_tensor_tensor(out=r2, in0=r2, scalar=2.0, in1=r0, op0=ALU.mult, op1=ALU.mult))
            link(nc.vector.tensor_scalar(r1, lam, -1.0, 0.0, ALU.mult, ALU.max))
            link(nc.vector.tensor_tensor(r2, r2, r1, ALU.add))
            nc.vector.tensor_scalar(r0, r2, 8.0, None, ALU.mult).then_inc(rate_ready, 1)
            nc.vector.tensor_scalar(r1, r2, -8.0, None, ALU.mult).then_inc(rate_ready, 1)
            dve.wait_ge(s_x, 16)

            for s in STEPS:
                kind = s[0]
                if kind == "norm":
                    k = s[1]
                    if k:
                        L = (k - 1) // 2
                        for key in ([(L, ("out", 0)), (L, ("out", 1))] if k % 2 else
                                    [(L, ("down", DSTEPS, 0))]):
                            for n in range(len(PAIR[key])):
                                evacuated(dve, key, n)
                    norm(k)
                    if k % 2 == 0:
                        nc.vector.memset(xT[:, :, 0:1], 0.0).then_inc(chain, 1)
                        nc.vector.memset(xT[:, :, T + 1:T + 3], 0.0).then_inc(chain, 1)
                        links[0] += 2
                    for b in range(TB):
                        for j in range(2):
                            idx = TURN[s] + 2 * b + j
                            c = (slice(None), slice(4 * j, 4 * j + 4), slice(b * P, (b + 1) * P))
                            turn_low(a_lo[c], a_hi[c],
                                     turn[idx % 2][:, :].rearrange("p (k t) -> p k t", k=4), idx)
                elif kind == "G":
                    h = half_of(s[1], s[2])
                    split_lo(dve, h)
                    split_lo(dve, h + 1)
                elif kind == "evac":
                    L, name = s[1:]
                    key = (L, name)
                    what, n = name[0], name[1]
                    p = PAIR[key][0]
                    if what in ("x", "y", "qkv"):
                        product_done(dve, key)
                        if what == "y" and n == 0:
                            dve.wait_ge(rope_done, 2 * (L + 1))
                        w = CB
                        if what != "qkv":
                            dst = xn[:, 1, xslice(n)]
                        else:
                            w = CB if n < 4 else VW - CB
                            dst = qk[:, 1, xslice(n)] if n < 3 else v[:, 1, (n - 3) * CB:(n - 3) * CB + w]
                        nc.vector.tensor_copy(dst, acc(p, 1)[:, 0:w]).then_inc(pair_free[p], 1)
                    elif what == "lru":
                        product_done(dve, key)
                        evacuated(dve, (L, ("g0", n)))
                        for b in range(TB):
                            g = sg0[:, b, xslice(n)]
                            nc.vector.tensor_tensor(g, acc(p, b), g, ALU.mult).then_inc(pair_free[p], 1)
                    elif what == "att":
                        product_done(dve, key)
                        for n in range(2):
                            evacuated(dve, (L, ("g1", n)))
                            evacuated(dve, (L, ("lru", n)))
                        for b in range(TB):
                            for n in range(2):
                                g = qk[:, b, xslice(n)]
                                nc.vector.tensor_tensor(g, acc(PAIR[key][n], b), g,
                                                        ALU.mult).then_inc(pair_free[PAIR[key][n]], 1)
                            for n in range(2):
                                g = qk[:, b, xslice(n)]
                                dve.wait_ge(pair_free[PAIR[key][n]], FREED[key][n] + b + 1)
                                nc.vector.tensor_tensor(g, g, sg0[:, b, xslice(n)],
                                                        ALU.add).then_inc(merged, 1)
                    elif what in ("out", "down"):
                        product_done(dve, key)
                        wide = KIND[key] == "w"
                        for i in range(len(PAIR[key])):
                            n_ = i if wide else (name[1] if what == "out" else name[2])
                            if what == "down" and (name[1] > 0):
                                evacuated(dve, (L, ("down", name[1] - 1, n_)))
                            for b in range(TB):
                                xs = x[:, b, xslice(n_)]
                                nc.vector.tensor_tensor(xs, acc(PAIR[key][i], b), xs,
                                                        ALU.add).then_inc(pair_free[PAIR[key][i]], 1)
                    elif what == "up":
                        product_done(dve, key)
                        evacuated(dve, (L, ("gate", n)))
                        w = CB if n < DSTEPS else 2 * P
                        for b in range(TB):
                            hs = hid[n % 2][:, b, 0:w]
                            nc.vector.tensor_tensor(hs, acc(p, b)[:, 0:w], hs,
                                                    ALU.mult).then_inc(pair_free[p], 1)
                elif kind == "tx":
                    _, L, c = s
                    for k in range(2):
                        idx = TURN[s] + k
                        n = 4 * c + 2 * k
                        bank_full(dve, idx)
                        nc.vector.tensor_copy(xT[:, n:n + 2, 1:T + 1],
                                              turn[idx % 2][:, :].rearrange("p (n t) -> p n t", n=2)
                                              ).then_inc(turn_free[idx % 2], 1)
                elif kind == "conv":
                    _, L, pr = s
                    bank_read(dve, TURN[("tx", L, pr // 2)] + pr % 2)
                    for q in range(2):
                        n = 2 * pr + q
                        nc.vector.tensor_scalar(xc[:, n, :], xT[:, n, 0:T], convw[:, L, 0, n:n + 1],
                                                convb[:, L, n:n + 1], ALU.mult, ALU.add).then_inc(chain, 1)
                        links[0] += 1
                    for j in range(1, 4):
                        for q in range(2):
                            n = 2 * pr + q
                            dve.wait_ge(chain, links[0] - 1 + (0 if j == 1 or q == 0 else 0))
                            ins = nc.vector.scalar_tensor_tensor(
                                out=xc[:, n, :], in0=xT[:, n, j:j + T], scalar=convw[:, L, j, n:n + 1],
                                in1=xc[:, n, :], op0=ALU.mult, op1=ALU.add)
                            if j < 3:
                                ins.then_inc(chain, 1)
                                links[0] += 1
                            else:
                                ins.then_inc(xc_ready, 1)
                            if j == 3 and q == 0:
                                dve.wait_ge(chain, links[0])
                elif kind == "la":
                    _, L, d, pr = s
                    k = (L * 2 + d) * 4 + pr
                    if k:
                        dve.wait_ge(scanned, 2 * k)
                    dve.wait_ge(tanh_ready, 2 * (k + 1))
                    link(nc.vector.tensor_scalar(dq_[:, :, :], tq_[:, :, :], 1.0, None, ALU.add))
                    link(nc.vector.reciprocal(dq_[:, :, :], dq_[:, :, :]))
                    nc.vector.scalar_tensor_tensor(out=tq_[:, :, :], in0=tq_[:, :, :], scalar=2.0,
                                                   in1=dq_[:, :, :], op0=ALU.mult,
                                                   op1=ALU.mult).then_inc(q_ready, 1)
                elif kind == "lb":
                    _, L, d, pr = s
                    k = (L * 2 + d) * 4 + pr
                    dve.wait_ge(sq_ready, k + 1)
                    dve.wait_ge(ix_ready, k + 1)
                    ii = ig[:, 2 * pr:2 * pr + 2, :]
                    link(nc.vector.tensor_tensor(ii, dq_[:, :, :], ii, ALU.mult))
                    dve.wait_ge(decay_ready, 2 * (k + 1))
                    for q in range(2):
                        n = 2 * pr + q
                        if d == 0:
                            nc.vector.tensor_tensor_scan(xT[:, n, 0:T], rg[:, n, :], ig[:, n, :], 0.0,
                                                         ALU.mult, ALU.add).then_inc(scanned, 1)
                        else:
                            back = slice(T - 1, None, -1)
                            nc.vector.tensor_tensor_scan(dq_[:, q, back], rg[:, n, back], ig[:, n, back],
                                                         0.0, ALU.mult, ALU.add).then_inc(chain, 1)
                            links[0] += 1
                    if d == 1:
                        dve.wait_ge(chain, links[0])
                        for q in range(2):
                            n = 2 * pr + q
                            nc.vector.tensor_tensor(xT[:, n, 0:T], xT[:, n, 0:T], dq_[:, q, :],
                                                    ALU.add).then_inc(scanned, 1)
                elif kind == "lf":
                    _, L, pr = s
                    dve.wait_ge(scanned, scans_before(L, 1, 3))
                    for i in range(2):
                        bank_read(dve, TURN[("ty", L, 1)] + i)
                    y2 = gy[:, 2 * pr:2 * pr + 2, :]
                    nc.vector.tensor_tensor(y2, xT[:, 2 * pr:2 * pr + 2, 0:T], y2,
                                            ALU.mult).then_inc(lru_full, 1)
                    dve.wait_ge(lru_hi_ready, 4 * L + pr + 1)
                    nc.vector.tensor_tensor(lru_lo[:, 2 * pr:2 * pr + 2, :], y2,
                                            lru_hi[:, 2 * pr:2 * pr + 2, :].bitcast(F32),
                                            ALU.subtract).then_inc(lru_ready, 1)
                elif kind == "tq" and s[2] % 2 == 1:
                    idx = TURN[s]
                    bank_full(dve, idx)
                    dve.wait_ge(scanned, scans_before(s[1], 1, 3))
                    nc.vector.tensor_copy(qkT[:, s[2], :, :],
                                          turn[idx % 2][:, :].rearrange("p (a t) -> p a t", a=2)
                                          ).then_inc(turn_free[idx % 2], 1)
                elif kind == "as":
                    _, L, u = s
                    b = u // SLOTS
                    uses, frees = mid_before(L, 8 + u)
                    dve.wait_ge(mid_full, uses + 1)
                    if u >= 2:
                        bank_full(dve, TURN[("ap", L, u - 2)] + 1)
                        bank_read(dve, TURN[("av", L, u - 2)])
                    flat = mid[:, :, :].rearrange("p a c -> p (a c)")
                    nc.vector.tensor_tensor_reduce(out=sm[:, u % 2, :], in0=flat[:, 0:GROUPS * T],
                                                   in1=band[:, b, :], scale=1.0, scalar=NEG, op0=ALU.add,
                                                   op1=ALU.max,
                                                   accum_out=mx[:, u % 2:u % 2 + 1]).then_inc(mid_free, 1)
                    dve.wait_ge(mid_free, frees + 1)
                    nc.vector.tensor_scalar(nm[:, u % 2:u % 2 + 1], mx[:, u % 2:u % 2 + 1], -SCALE, None,
                                            ALU.mult).then_inc(nm_ready, 1)
                elif kind == "ap":
                    _, L, u = s
                    idx = TURN[s] + 1
                    bank_full(dve, idx)
                    nc.vector.tensor_copy(pt[:, 4:6, :],
                                          turn[idx % 2][:, 0:2 * P].rearrange("p (a t) -> p a t", a=2)
                                          ).then_inc(turn_free[idx % 2], 1)
                    dve.wait_ge(p_ready, 8 * L + u + 1)
                    link(nc.vector.reciprocal(rr[:, u % 2:u % 2 + 1], rs[:, u % 2:u % 2 + 1]))
                elif kind == "av":
                    _, L, u = s
                    b, sl = u // SLOTS, u % SLOTS
                    idx = TURN[s]
                    bank_full(dve, idx)
                    nc.vector.tensor_scalar(att[:, b, sl * DH:(sl + 1) * DH], turn[idx % 2][:, 0:DH],
                                            rr[:, u % 2:u % 2 + 1], None,
                                            ALU.mult).then_inc(turn_free[idx % 2], 1)
                elif kind == "ta":
                    turn_low(att_lo[:, :, :], att_hi[:, :, :],
                             turn[TURN[s] % 2][:, :].rearrange("p (a t) -> p a t", a=2), TURN[s])
                elif kind == "tm":
                    for b in range(TB):
                        for j in range(2):
                            idx = TURN[s] + 2 * b + j
                            c = (slice(None), slice(4 * j, 4 * j + 4), slice(b * P, (b + 1) * P))
                            turn_low(a_lo[c], a_hi[c],
                                     turn[idx % 2][:, :].rearrange("p (k t) -> p k t", k=4), idx)
                elif kind == "th":
                    c = s[2]
                    w = 4 if c < DSTEPS else 2
                    for b in range(TB):
                        idx = TURN[s] + b
                        r_ = (slice(None), slice(0, w), slice(b * P, (b + 1) * P))
                        turn_low(hT_lo[c % 2][r_], hT_hi[c % 2][r_],
                                 turn[idx % 2][:, 0:w * P].rearrange("p (k t) -> p k t", k=w), idx)

            for b in range(TB):
                dve.wait_ge(xn_hi_ready, b + 1)
                nc.vector.tensor_tensor(xn_lo[:, b, :], xn[:, b, :], xn_hi[:, b, :].bitcast(F32),
                                        ALU.subtract).then_inc(xn_lo_ready, 1)
            dve.wait_ge(rw_ready, 1)
            nc.vector.tensor_tensor(rw[:, 1, :], router, rw[:, 0, :].bitcast(F32),
                                    ALU.subtract).then_inc(rw_ready, 1)
            nc.vector.memset(y_hi[:, :].bitcast(F32), 0.0).then_inc(chain, 1)
            nc.vector.memset(y_lo[:, :].bitcast(F32), 0.0).then_inc(chain, 1)
            nc.vector.memset(selT[:, :].bitcast(F32), 0.0).then_inc(chain, 1)
            nc.vector.memset(slot[:, :, :], -1.0).then_inc(chain, 1)
            links[0] += 4
            dve.wait_ge(chain, links[0])
            nc.vector.memset(share[:, :, :], 0.0).then_inc(y_ready, 2)
            dve.wait_ge(y_ready, 2)
            dve.wait_ge(logit_full, 1)
            link(nc.vector.tensor_copy(lg[:, :, :], mid[:, :, 0:EXPERTS]))
            shape = [P, TB, EXPERTS, EXPERTS]
            for b in range(TB):
                nc.vector.max(top[:, b, :], lg[:, b, :]).then_inc(chain, 1)
            rival = lg[:, :, :].rearrange("p b (o e) -> p b o e", o=1).to_broadcast(shape)
            own = lg[:, :, :].rearrange("p b (e o) -> p b e o", o=1).to_broadcast(shape)
            low = lower.rearrange("p (o a) e -> p o a e", o=1).to_broadcast(shape)
            nc.vector.tensor_tensor(cmp_[:, :, :, :], rival, own, ALU.is_gt).then_inc(chain, 1)
            nc.vector.tensor_tensor(cmp2[:, :, :, :], rival, own, ALU.is_equal).then_inc(chain, 1)
            links[0] += TB + 2
            dve.wait_ge(chain, links[0])
            link(nc.vector.tensor_tensor(cmp2[:, :, :, :], cmp2[:, :, :, :], low, ALU.mult))
            link(nc.vector.tensor_tensor(cmp_[:, :, :, :], cmp_[:, :, :, :], cmp2[:, :, :, :], ALU.add))
            link(nc.vector.tensor_reduce(mask[:, :, :], cmp_[:, :, :, :], AX.X, ALU.add))
            nc.vector.tensor_scalar(mask[:, :, :], mask[:, :, :], 1.5, None, ALU.is_lt).then_inc(mask_ready, 1)
            for b in range(TB):
                ins = nc.vector.tensor_scalar(lg[:, b, :], lg[:, b, :], top[:, b, 0:1], None, ALU.subtract)
                ins.then_inc(chain, 1) if b == 0 else ins.then_inc(top_ready, 1)
            links[0] += 1
            dve.wait_ge(mask_ready, 1)
            dve.wait_ge(share_exp, 1)
            link(nc.vector.tensor_tensor(lg[:, :, :], lg[:, :, :], mask[:, :, :], ALU.mult))
            link(nc.vector.tensor_reduce(wsum[:, :, 0:1], lg[:, :, :], AX.X, ALU.add))
            link(nc.vector.reciprocal(wsum[:, :, 1:2], wsum[:, :, 0:1]))
            for b in range(TB):
                link(nc.vector.tensor_scalar(share[:, b, 1:EXPERTS + 1], lg[:, b, :], wsum[:, b, 1:2], None,
                                             ALU.mult))
            dve.wait_ge(rank_full, 1)
            ranks = slot[:, :, 1:EXPERTS + 1]
            link(nc.vector.tensor_scalar(ranks, mid[:, :, 0:EXPERTS], 1.0, None, ALU.add))
            link(nc.vector.tensor_tensor(ranks, ranks, mask[:, :, :], ALU.mult))
            link(nc.vector.tensor_scalar(ranks, ranks, -1.0, None, ALU.add))
            link(nc.vector.tensor_reduce(most[:, 0:1], bank[0][:, 0:EXPERTS], AX.X, ALU.max))
            nc.vector.tensor_copy(most_i[:, 0:1], most[:, 0:1]).then_inc(route_ready, 1)
            for b in range(TB):
                dve.wait_ge(xn_lo_ready, b + 1)

            def select(col):
                for b in range(TB):
                    nc.vector.tensor_scalar(sel[:, b, :], iota, slot[:, b, col], None,
                                            ALU.is_equal).then_inc(sel_ready, 1)

            def gather(n, e, first):
                for j in range(2):
                    dve.wait_ge(g_hi_ready, n + j + 1 + e * 2)
                    t_ = (first + j) % 2
                    nc.vector.tensor_tensor(g_lo[:, 4 * j:4 * j + 4, :],
                                            turn[t_][:, :].rearrange("p (k t) -> p k t", k=4),
                                            g_hi[:, 4 * j:4 * j + 4, :].bitcast(F32),
                                            ALU.subtract).then_inc(turn_free[t_], 1)

            def combine(first, e, col):
                for b in range(TB):
                    for n in range(2):
                        idx = first + 2 * b + n
                        dve.wait_ge(turned, idx + 1 + e * E_TURNS)
                        xs = x[:, b, xslice(n)]
                        nc.vector.scalar_tensor_tensor(out=xs, in0=turn[idx % 2][:, :],
                                                       scalar=share[:, b, col], in1=xs, op0=ALU.mult,
                                                       op1=ALU.add).then_inc(turn_free[idx % 2], 1)

            def experts(pas):
                g0 = pas * (EXPERTS + 1)
                t0 = T0 + pas * (2 + EXPERTS * E_TURNS + 4)
                h0 = H0 + pas * EXPERTS * 2 * E_PARTS
                s0 = pas * EXPERTS * ESTEPS
                select(slice(1, 2))
                gather(2 * g0, 0, t0)
                tl = t0 + 2
                with dve.Fori(0, EXPERTS) as e:
                    h = h0
                    for what, c in expert_order():
                        if what == "down":
                            if c == ESTEPS - 1:
                                select(bass.ds(e + 2, 1))
                            idx = tl + U_HID + c
                            dve.wait_ge(eT_hi_ready, s0 + c + 1 + e * ESTEPS)
                            nc.vector.tensor_tensor(eT_lo[c % 2][:, :, :],
                                                    turn[idx % 2][:, :].rearrange("p (k t) -> p k t", k=4),
                                                    eT_hi[c % 2][:, :, :].bitcast(F32),
                                                    ALU.subtract).then_inc(turn_free[idx % 2], 1)
                            if c == ESTEPS - 1:
                                gather(2 * (g0 + 1), e, tl + U_GATH)
                        for _ in range(4):
                            split_lo(dve, h, e)
                            h += 1
                        if what == "gate" and c == 1:
                            combine(tl + U_COMB, e, bass.ds(e, 1))
                            idx = tl + U_SLOT
                            dve.wait_ge(turned, idx + 1 + e * E_TURNS)
                            nc.vector.tensor_copy(selT[:, :], turn[idx % 2][:, 0:T]
                                                  ).then_inc(turn_free[idx % 2], 1)
                        if (what == "gate" and c >= 1) or (what == "down" and c == ESTEPS - 2):
                            cc = c - 1 if what == "gate" else ESTEPS - 1
                            dve.wait_ge(e_silu, s0 + cc + 1 + e * ESTEPS)
                            dve.wait_ge(used, h0 + E_END[("up", cc)] + e * 2 * E_PARTS)
                            nc.vector.tensor_tensor(eh[cc % 2][:, :], bank[2 * (cc % 2) + 1][:, :],
                                                    eh[cc % 2][:, :], ALU.mult).then_inc(e_hid, 1)
                    for n in range(2):
                        dve.wait_ge(y_hi_ready, 2 * pas * EXPERTS + n + 1 + e * 2)
                        nc.vector.tensor_tensor(y_lo[:, xslice(n)], mid[:, n, :],
                                                y_hi[:, xslice(n)].bitcast(F32),
                                                ALU.subtract).then_inc(y_ready, 1)
                combine(tl + EXPERTS * E_TURNS, 0, slice(EXPERTS, EXPERTS + 1))
                for i in range(2, 4):
                    bank_read(dve, tl + EXPERTS * E_TURNS + i)

            experts(0)
            n = dve.value_load(most_i[0:1, 0:1], min_val=0, max_val=T)
            with dve.If(n > NPASS_TOKENS):
                nc.vector.tensor_scalar(slot[:, :, :], slot[:, :, :], -float(NPASS_TOKENS), None,
                                        ALU.add).then_inc(zeroed, 1)
                dve.wait_ge(zeroed, 1)
                experts(1)
            norm(2 * DEPTH, final=True)


def pack_cols(w, kt, cols):
    return w.reshape(kt, P, cols).transpose(1, 0, 2)


def parts_of(w, kind):
    kt = {"n": 4, "h": 8, "w": 2}[kind]
    return [pack_cols(w[i * kt * P:(i + 1) * kt * P], kt, w.shape[1]).reshape(P, PART)
            for i in range(w.shape[0] // (kt * P))]


def weight_stream(inp):
    out = np.empty((TOTAL_PARTS, P, PART), np.float32)
    n = 0

    def put(parts):
        nonlocal n
        for p in parts:
            out[n] = p
            n += 1

    q0, y0, g0 = D, D, 2 * D + 3 * VW
    for L in range(DEPTH):
        w_in = inp["w_in"][L]
        for name, kind, _ in MIXER:
            what, i = name
            c = i * CB
            if what == "x":
                w = w_in[:, c:c + CB]
            elif what == "y":
                w = w_in[:, D + c:D + c + CB]
            elif what == "qkv":
                w = w_in[:, 2 * D + c:2 * D + min(c + CB, 3 * VW)]
            elif what == "g0":
                w = w_in[:, g0 + c:g0 + c + CB]
            elif what == "g1":
                w = w_in[:, g0 + D + c:g0 + D + c + CB]
            elif what == "lru":
                w = inp["w_proj_lru"][L][:, c:c + CB]
            elif what == "att":
                w = inp["w_proj_att"][L]
            else:
                w = inp["w_out"][L][:, c:c + CB]
            put(parts_of(w, kind))
        if L == 0:
            for name, kind, _ in dense_order():
                f = name[1] * CB
                if name[0] == "down":
                    w = inp["w_dense_down"][0][f:f + CB]
                    if kind == "n":
                        w = w[:, name[2] * CB:(name[2] + 1) * CB]
                else:
                    w = inp["w_dense_" + name[0]][0][:, f:f + CB]
                put(parts_of(w, kind))
    for e in range(EXPERTS):
        for what, c in expert_order():
            f = c * CB
            if what == "down":
                put(parts_of(inp["w_exp_down"][0, e][f:f + CB], "w"))
            else:
                put(parts_of(inp["w_exp_" + what][0, e][:, f:f + CB], "n"))
    assert n == TOTAL_PARTS
    return out


def constants():
    c = np.zeros((P, C_END), np.float32)
    i = np.arange(P)
    c[:, C_ID:C_ID + P] = np.eye(P)
    c[:, C_IOTA:C_IOTA + P] = i[None, :]
    c[:, C_BEFORE:C_BEFORE + P] = i[:, None] < i[None, :]
    c[:, C_ONES:C_ONES + P] = 1
    k = np.arange(T)
    for b in range(TB):
        rel = (b * P + i)[:, None] - k[None, :]
        for g in range(GROUPS):
            ok = (rel % DILATIONS[g] == 0) & (np.abs(rel) <= WINDOWS[g] // 2)
            o = C_MASK + (b * GROUPS + g) * T
            c[:, o:o + T] = np.where(ok, 0, NEG)
        freq = (np.float32(500000.0) ** (-np.arange(0, 16, 2, dtype=np.float32) / np.float32(16))).astype(np.float32)
        ang = (b * P + i)[:, None].astype(np.float32) * freq[None, :]
        c[:, C_COS + 8 * b:C_COS + 8 * b + 8] = np.cos(ang)
        c[:, C_SIN + 8 * b:C_SIN + 8 * b + 8] = np.sin(ang)
    e = np.arange(EXPERTS)
    c[:, C_LOW:C_END] = (e[None, :] < e[:, None]).astype(np.float32).reshape(1, -1)
    return c


def by_channel(a):
    a = a.reshape(a.shape[:-1] + (a.shape[-1] // P, P))
    return np.moveaxis(a, -1, 0).reshape(P, -1)


def kernel(**inputs):
    import concourse.bacc as bacc
    from concourse.bass_utils import run_bass_kernel_spmd

    inp = {k: np.asarray(a) for k, a in inputs.items()}
    router = inp["w_router"][0].reshape(KT, P, EXPERTS).transpose(1, 0, 2).reshape(P, -1)
    vecs = np.concatenate([by_channel(inp["conv_w"]), by_channel(inp["conv_b"]), by_channel(inp["b_rgate"]),
                           by_channel(inp["b_igate"]), by_channel(inp["lru_lambda"]), router], axis=1)
    gates = np.stack([inp["w_rgate"], inp["w_igate"]], axis=2)
    gates = gates.transpose(0, 4, 1, 2, 3, 5).reshape(DEPTH, P, -1)
    norms = np.stack([inp["norm_mix_g"][0], inp["norm_ffn_g"][0], inp["norm_mix_g"][1],
                      inp["norm_ffn_g"][1], inp["final_norm_g"]])
    arrays = {
        "stream": weight_stream(inp), "gates": np.ascontiguousarray(gates),
        "x": inp["x"].reshape(T, D), "norms": norms, "consts": constants(),
        "vecs": np.ascontiguousarray(vecs),
    }
    nc = bacc.Bacc("TRN2", target_bir_lowering=False, num_devices=1)
    aps = [nc.dram_tensor(f"in_{k}", a.shape, mybir.dt.from_np(a.dtype), kind="ExternalInput").ap()
           for k, a in arrays.items()]
    out = nc.dram_tensor("out_x", (T, D), F32, kind="ExternalOutput").ap()
    build(nc, *aps, out)
    r = run_bass_kernel_spmd(nc, [{f"in_{k}": a for k, a in arrays.items()}], core_ids=[0])
    return r.results[0]["out_x"].reshape(1, T, D)
```

```python
from contextlib import ExitStack

import numpy as np
import concourse.bass as bass
from concourse import mybir

F32 = mybir.dt.float32
F32R = mybir.dt.float32r
I32 = mybir.dt.int32
ALU = mybir.AluOpType
ACT = mybir.ActivationFunctionType
AX = mybir.AxisListType

P = 128
D = 1024
KT = D // P
T = 256
TB = T // P
DEPTH = 2
CB = 512
HEADS, SLOTS, GROUPS, DH = 12, 4, 3, 64
QK = 2 * HEADS * DH
VW = HEADS * DH
WINDOWS, DILATIONS = (128, 512, 2048), (1, 4, 16)
F_DENSE, F_EXP, EXPERTS = 2816, 3584, 8
EPS = 1e-6
SCALE = DH ** -0.5
NEG = -1e30

PART = 2048
HALF = PART // 2
R = 6
H = 4

MIXER = ([(("x", n), "n", i) for n in range(2) for i in range(2)]
         + [(("qkv", n), "n", i) for n in range(4) for i in range(2)] + [(("qkv", 4), "h", 0)]
         + [((w, n), "n", i) for w in ("y", "g1", "g0") for n in range(2) for i in range(2)]
         + [(("lru", 0), "n", i) for i in range(2)] + [(("att", 0), "w", 0)]
         + [(("lru", 1), "n", i) for i in range(2)]
         + [(("out", n), "n", i) for i in range(2) for n in range(2)])
DSTEPS = F_DENSE // CB
ESTEPS = F_EXP // CB
E_PARTS = 6 * ESTEPS
NPASS_TOKENS = P


def dense_order():
    out = []
    for c in range(DSTEPS + 1):
        kind, parts = ("n", 2) if c < DSTEPS else ("h", 1)
        out += [((w, c), kind, i) for w in ("gate", "up") for i in range(parts)]
        if c:
            out += [(("down", c - 1, n), "n", 0) for n in range(2)]
    return out + [(("down", DSTEPS, 0), "w", 0)]


def expert_order():
    out = []
    for c in range(ESTEPS):
        out += [("gate", c), ("up", c)]
        if 0 < c < ESTEPS - 2:
            out += [("down", c - 1)]
    return out + [("down", c) for c in range(ESTEPS - 3, ESTEPS)]


def schedule():
    steps = []
    for L in range(DEPTH):
        steps.append(("norm", 2 * L))
        side = {}

        def at(gap, *what):
            side.setdefault(gap, []).extend(what)

        at(2, ("evac", ("x", 0)))
        at(3, ("tx", 0), ("conv", 0))
        at(4, ("evac", ("x", 1)), ("conv", 1))
        at(5, ("tx", 1), ("lg", 0, 0), ("conv", 2))
        at(6, ("evac", ("qkv", 0)), ("conv", 3), ("lg", 0, 1))
        at(7, ("lg", 0, 2))
        at(8, ("evac", ("qkv", 1)), ("lg", 0, 3), ("la", 0, 0))
        at(9, ("lb", 0, 0))
        at(10, ("evac", ("qkv", 2)), ("rope",), ("la", 0, 1))
        at(11, ("lb", 0, 1))
        at(12, ("evac", ("qkv", 3)), ("lg", 1, 0))
        at(13, ("evac", ("qkv", 4)), ("lg", 1, 1))
        at(14, ("la", 1, 0), ("lg", 1, 2))
        at(15, ("evac", ("y", 0)), ("lb", 1, 0), ("lg", 1, 3))
        at(16, ("ty", 0), ("la", 1, 1))
        at(17, ("evac", ("y", 1)), ("lb", 1, 1))
        at(18, ("ty", 1), *(("tq", j) for j in range(HEADS // 2)))
        at(19, ("evac", ("g1", 0)), ("as", 0), ("lf", 0))
        at(20, ("ap", 0), ("as", 1), ("lf", 1))
        at(21, ("evac", ("g1", 1)), ("av", 0), ("ap", 1), ("as", 2), ("av", 1), ("ap", 2), ("as", 3))
        at(22, ("av", 2), ("ap", 3), ("as", 4), ("lf", 2))
        at(23, ("evac", ("g0", 0)), ("av", 3), ("ap", 4), ("as", 5), ("av", 4), ("ap", 5), ("as", 6))
        at(24, ("av", 5), ("ap", 6), ("as", 7), ("lf", 3))
        at(25, ("evac", ("g0", 1)), ("av", 6), ("ap", 7))
        at(26, ("av", 7))
        at(27, ("evac", ("lru", 0)), ("ta",))
        at(28, ("evac", ("att", 0)))
        at(29, ("merge", 0))
        at(30, ("tm", 0), ("evac", ("lru", 1)), ("merge", 1))
        at(31, ("tm", 1))
        at(33, ("evac", ("out", 0)))
        at(34, ("evac", ("out", 1)))
        for g, (name, _, i) in enumerate(MIXER):
            steps.append(("G", (L, name), i))
            steps += [(s[0], L) + s[1:] for s in side.get(g + 1, [])]
        steps.append(("norm", 2 * L + 1))
        if L == 0:
            order = dense_order()
            for j, (name, _, i) in enumerate(order):
                steps.append(("G", (L, name), i))
                ended = j + 1 == len(order) or order[j + 1][0] != name
                if ended:
                    steps.append(("evac", L, name))
                if ended and name[0] == "gate" and name[1]:
                    steps.append(("th", L, name[1] - 1))
                if name == ("down", DSTEPS - 1, 0):
                    steps.append(("th", L, DSTEPS))
    return steps


STEPS = schedule()


def tables():
    half_at, last_half, pair, freed, kinds = {}, {}, {}, {}, {}
    uses, ring = [0, 0, 0], {2: 0, 3: 0}
    todo = []
    for L in range(DEPTH):
        todo += [((L, n), k, i, 2) for n, k, i in MIXER]
        if L == 0:
            todo += [((L, n), k, i, 3) for n, k, i in dense_order()]
    for j, (key, kind, i, width) in enumerate(todo):
        half_at[key, i], last_half[key] = 2 * j, 2 * j + 2
        if key not in kinds:
            kinds[key] = kind
            pair[key], freed[key] = [], []
            for _ in range(2 if kind == "w" else 1):
                p = ring[width] % width
                ring[width] += 1
                pair[key].append(p)
                freed[key].append(uses[p])
                uses[p] += TB
    turn, n = {}, 0
    count = {"norm": 4, "tx": 2, "ty": 2, "tq": 1, "ap": 2, "av": 1, "ta": 1, "tm": 2, "th": 2}
    for s in STEPS:
        if s[0] in count:
            turn[s] = n
            n += count[s[0]]
    return half_at, last_half, pair, freed, kinds, turn, n, 2 * len(todo)


HALF_AT, LAST_HALF, PAIR, FREED, KIND, TURN, N_TURN, N_HALF = tables()
STATIC_PARTS = N_HALF // 2
TOTAL_PARTS = STATIC_PARTS + EXPERTS * E_PARTS
assert E_PARTS % R == 0 and (2 * E_PARTS) % H == 0

C_ID, C_IOTA, C_BEFORE, C_ONES = 0, P, 2 * P, 3 * P
C_MASK = 4 * P
C_COS = C_MASK + TB * GROUPS * T
C_SIN = C_COS + TB * 8
C_LOW = C_SIN + TB * 8
C_END = C_LOW + EXPERTS * EXPERTS
V_CONVW = 0
V_CONVB = V_CONVW + DEPTH * 4 * KT
V_BR = V_CONVB + DEPTH * KT
V_BI = V_BR + DEPTH * 2 * KT
V_LAM = V_BI + DEPTH * 2 * KT
V_ROUTER = V_LAM + DEPTH * 2 * KT
V_END = V_ROUTER + KT * EXPERTS

U_COMB, U_SLOT, U_HID, U_GATH = 0, 4, 5, 5 + ESTEPS
E_TURNS = 7 + ESTEPS
E_AT = {key: 4 * i for i, key in enumerate(expert_order())}
E_HALVES = 2 * E_PARTS
AT_COMBINE = [E_AT["up", 0] + 2 + i for i in range(4)]
AT_SLOT = E_AT["up", 0] + 6
AT_HID = [E_AT["up", c + 1] for c in range(ESTEPS - 2)] + [E_AT["down", c] for c in
                                                          range(ESTEPS - 3, ESTEPS - 1)]
AT_GATHER = [E_AT["down", ESTEPS - 2] + 2 + j for j in range(2)]
assert E_TURNS % 2 == 0


def build(nc, stream, gates_w, x_in, norms, consts_in, vecs_in, out):
    with ExitStack() as ctx:
        def keep(name, shape, dt=F32, into=ctx):
            return into.enter_context(nc.sbuf_tensor(name, shape, dt))

        def sem(name):
            return ctx.enter_context(nc.semaphore(name))

        raw = keep("raw", [P, R, PART])
        w_hi = keep("w_hi", [P, H, HALF], F32R)
        w_lo = keep("w_lo", [P, H, HALF], F32R)
        x = keep("x", [P, TB, D])
        a_hi = keep("a_hi", [P, KT, T], F32R)
        a_lo = keep("a_lo", [P, KT, T], F32R)
        xn = keep("xn", [P, TB, D])
        gain = keep("gain", [P, D])
        const = keep("const", [P, C_END])
        vec = keep("vec", [P, V_END])
        NC = DEPTH * 2 * KT
        rate = keep("rate", [P, 3, NC])
        small = keep("small", [P, 64])
        with ExitStack() as m:
            wg = keep("wg", [P, 2, 2, KT, P], into=m)
        with ExitStack() as m:
            sm = keep("sm", [P, 2, GROUPS * T], into=m)
            pt = keep("pt", [P, 2 * GROUPS, P], into=m)
            att = keep("att", [P, TB, T], into=m)
            att_hi = keep("att_hi", [P, 2, T], F32R, m)
            att_lo = keep("att_lo", [P, 2, T], F32R, m)
        keep("wg_place", [P, 4 * KT * P])
        arena = ExitStack()
        with arena:
            qk = keep("qk", [P, TB, QK], into=arena)
            v = keep("v", [P, TB, VW], into=arena)
            gy = keep("gy", [P, KT, T], into=arena)
            with ExitStack() as m:
                rg = keep("rg", [P, KT, T], into=m)
                ig = keep("ig", [P, KT, T], into=m)
                root = keep("root", [P, 4, T], into=m)
            with ExitStack() as m:
                qkT = keep("qkT", [P, HEADS // 2, 2, T], into=m)
                sg0 = keep("sg0", [P, TB, D], into=m)
            keep("u_place", [P, 2 * KT * T + 4 * T], into=arena)
            with ExitStack() as m:
                xT = keep("xT", [P, KT, T + 3], into=m)
                xc = keep("xc", [P, KT, T], into=m)
            with ExitStack() as m:
                lru_lo = keep("lru_lo", [P, KT, T], F32R, m)
                keep("gap", [P, KT * 3], into=m)
                lru_hi = keep("lru_hi", [P, KT, T], F32R, m)
        with ExitStack() as m:
            hid = [keep(f"hid{i}", [P, TB, CB], into=m) for i in range(2)]
            hT_hi = [keep(f"hT_hi{i}", [P, 4, T], F32R, m) for i in range(2)]
            hT_lo = [keep(f"hT_lo{i}", [P, 4, T], F32R, m) for i in range(2)]
        with ExitStack() as m:
            xn_hi = keep("xn_hi", [P, TB, D], F32R, m)
            xn_lo = keep("xn_lo", [P, TB, D], F32R, m)
            g_hi = keep("g_hi", [P, KT, P], F32R, m)
            g_lo = keep("g_lo", [P, KT, P], F32R, m)
            eh = [keep(f"eh{i}", [P, CB], into=m) for i in range(2)]
            eT_hi = [keep(f"eT_hi{i}", [P, 4, P], F32R, m) for i in range(2)]
            eT_lo = [keep(f"eT_lo{i}", [P, 4, P], F32R, m) for i in range(2)]
            y_hi = keep("y_hi", [P, D], F32R, m)
            y_lo = keep("y_lo", [P, D], F32R, m)
            sel = keep("sel", [P, TB, P], F32R, m)
            selT = keep("selT", [P, T], F32R, m)
            rw = keep("rw", [P, 2, KT * EXPERTS], F32R, m)
            lg = keep("lg", [P, TB, EXPERTS], into=m)
            cmp_ = keep("cmp", [P, TB, EXPERTS, EXPERTS], into=m)
            cmp2 = keep("cmp2", [P, TB, EXPERTS, EXPERTS], into=m)
            mask = keep("mask", [P, TB, EXPERTS], into=m)
            top = keep("top", [P, TB, 8], into=m)
            wsum = keep("wsum", [P, TB, 4], into=m)
            slot = keep("slot", [P, TB, EXPERTS + 2], into=m)
            share = keep("share", [P, TB, EXPERTS + 2], into=m)
            most = keep("most", [P, 2], into=m)
            most_i = keep("most_i", [P, 2], I32, m)

        bank = [ctx.enter_context(nc.psum_tensor(f"bank{i}", [P, CB], F32)) for i in range(4)]
        mid = ctx.enter_context(nc.psum_tensor("mid", [P, 2, CB], F32))
        turn = [ctx.enter_context(nc.psum_tensor(f"turn{i}", [P, CB], F32)) for i in range(2)]

        def acc(p, b):
            return mid[:, b, :] if p == 2 else bank[2 * p + b][:, :]

        ident = const[:, C_ID:C_ID + P]
        iota = const[:, C_IOTA:C_IOTA + P]
        before = const[:, C_BEFORE:C_BEFORE + P]
        ones = const[:, C_ONES:C_ONES + P]
        band = const[:, C_MASK:C_COS].rearrange("p (b k) -> p b k", b=TB)
        cos = const[:, C_COS:C_SIN].rearrange("p (b k) -> p b k", b=TB)
        sin = const[:, C_SIN:C_LOW].rearrange("p (b k) -> p b k", b=TB)
        lower = const[:, C_LOW:C_END].rearrange("p (a b) -> p a b", a=EXPERTS)
        convw = vec[:, V_CONVW:V_CONVB].rearrange("p (l j n) -> p l j n", l=DEPTH, j=4)
        convb = vec[:, V_CONVB:V_BR].rearrange("p (l n) -> p l n", l=DEPTH)
        b_r = vec[:, V_BR:V_BI].rearrange("p (l d n) -> p l d n", l=DEPTH, d=2)
        b_i = vec[:, V_BI:V_LAM].rearrange("p (l d n) -> p l d n", l=DEPTH, d=2)
        lam = vec[:, V_LAM:V_ROUTER]
        router = vec[:, V_ROUTER:V_END]
        ms, sd, rstd = (small[:, 2 * i:2 * i + 2] for i in range(3))
        mx, nm, rs, rr = (small[:, 8 + 2 * i:10 + 2 * i] for i in range(4))
        ss = small[:, 16:20].rearrange("p (n b) -> p n b", n=2)
        idle = small[:, 20:21]

        s_const = sem("consts_landed")
        s_x = sem("x_landed")
        s_gain0 = sem("first_gain_landed")
        s_gain = sem("gain_landed")
        s_wg = sem("gate_weights_landed")
        landed = [sem(f"part_landed{i}") for i in range(R)]
        hi_ready = sem("hi_ready")
        lo_ready = sem("lo_ready")
        used = sem("halves_used")
        pair_free = [sem(f"pair_free{i}") for i in range(3)]
        turned = sem("turned")
        turn_hi = sem("turn_hi")
        turn_free = [sem(f"turn_free{i}") for i in range(2)]
        chain = sem("vector_chain")
        rate_s = sem("rate_exp")
        rate_ready = sem("rate_ready")
        sq_sum = sem("squares_summed")
        ms_ready = sem("mean_square_ready")
        sd_ready = sem("deviation_ready")
        xn_ready = sem("xn_ready")
        xc_ready = sem("xc_ready")
        mid_full = sem("mid_full")
        mid_free = sem("mid_free")
        tanh_ready = sem("tanh_ready")
        decay_ready = sem("decay_ready")
        ix_ready = sem("gated_input_ready")
        sq_ready = sem("root_ready")
        scanned = sem("scanned")
        rope_s = sem("rope_parts")
        rope_done = sem("rope_done")
        gelu_ready = sem("gelu_ready")
        lru_full = sem("lru_full")
        lru_hi_ready = sem("lru_hi_ready")
        lru_ready = sem("lru_ready")
        nm_ready = sem("neg_max_ready")
        p_ready = sem("probs_ready")
        merged = sem("merged")
        silu_ready = sem("silu_ready")
        xn_hi_ready = sem("xn_hi_ready")
        xn_lo_ready = sem("xn_lo_ready")
        rw_ready = sem("router_weights_ready")
        logit_full = sem("logits_full")
        top_ready = sem("top_ready")
        share_exp = sem("share_exp")
        mask_ready = sem("mask_ready")
        rank_full = sem("rank_full")
        route_ready = sem("route_ready")
        sel_ready = sem("sel_ready")
        g_hi_ready = sem("gathered_hi")
        e_silu = sem("expert_silu")
        e_hid = sem("expert_hidden")
        eT_hi_ready = sem("expert_hidden_hi")
        y_hi_ready = sem("y_hi_ready")
        y_ready = sem("y_ready")
        zeroed = sem("zeroed")
        idle_s = sem("root_table_fetched")
        out_sem = sem("out_landed")
        x_final = sem("x_final")
        done = sem("final_ready")

        def product_done(eng, key):
            eng.wait_ge(used, LAST_HALF[key])

        def bank_full(eng, idx):
            eng.wait_ge(turned, idx + 1)

        def bank_read(eng, idx):
            eng.wait_ge(turn_free[idx % 2], idx // 2 + 1)

        def split_hi(act, h, e=0):
            part = h // 2
            if h % 2 == 0:
                act.wait_ge(landed[part % R], 16 * (part // R + 1) + e * (16 * E_PARTS // R))
            if h >= H:
                act.wait_ge(used, h - H + 1 + e * 2 * E_PARTS)
            lo = (h % 2) * HALF
            nc.scalar.activation(w_hi[:, h % H, :], raw[:, part % R, lo:lo + HALF],
                                 ACT.Copy).then_inc(hi_ready, 1)

        def split_lo(dve, h, e=0):
            part = h // 2
            lo = (h % 2) * HALF
            dve.wait_ge(hi_ready, h + 1 + e * 2 * E_PARTS)
            nc.vector.tensor_tensor(w_lo[:, h % H, :], raw[:, part % R, lo:lo + HALF],
                                    w_hi[:, h % H, :].bitcast(F32), ALU.subtract).then_inc(lo_ready, 1)

        def mm3(out_, s_hi, s_lo, wh, wl, start, stop):
            nc.tensor.matmul(out_, s_hi, wh, start=start, stop=False)
            nc.tensor.matmul(out_, s_hi, wl, start=False, stop=False)
            return nc.tensor.matmul(out_, s_lo, wh, start=False, stop=stop)

        def half_of(key, part):
            return HALF_AT[key, part]

        def scans_done(L, d, hf):
            return (L * 2 + d) * KT + 4 * (hf + 1)

        def evac_value(key, n=0):
            return FREED[key][n] + TB

        def evacuated(eng, key, n=0):
            eng.wait_ge(pair_free[PAIR[key][n]], evac_value(key, n))

        def mid_before(L, use):
            lru = min(use, 8)
            at_ = use - lru
            return L * 16 + use, L * (8 * 4 + 8) + 4 * lru + at_

        def xslice(n):
            return slice(n * CB, (n + 1) * CB)

        def x_done(eng, k, n, b):
            L = (k - 1) // 2
            if k % 2:
                key, i = (L, ("out", n)), 0
            else:
                key, i = (L, ("down", DSTEPS, 0)), n
            eng.wait_ge(pair_free[PAIR[key][i]], FREED[key][i] + b + 1)

        H0 = N_HALF
        T0 = N_TURN

        block = ctx.enter_context(nc.Block())

        @block.sync
        def _(sp):
            def load(slot_, part, group):
                sp.dma_start(raw[:, slot_, :], stream[part, :, :]).then_inc(landed[slot_], 16)

            sp.dma_start(x[:, :, :], x_in.rearrange("(b p) d -> p b d", p=P)).then_inc(s_x, 16)
            for i in range(R):
                load(i, i, 0)
            with sp.Fori(1, TOTAL_PARTS // R) as g:
                for i in range(R):
                    sp.wait_ge(lo_ready, 2 * R * g + 2 * (i + 1) - 2 * R)
                    load(i, g * R + i, g)
            for part in range(TOTAL_PARTS // R * R, TOTAL_PARTS):
                sp.wait_ge(lo_ready, 2 * (part - R + 1))
                load(part % R, part, 0)
            sp.wait_ge(route_ready, 1)
            n = sp.value_load(most_i[0:1, 0:1], min_val=0, max_val=T)
            with sp.If(n > NPASS_TOKENS):
                with sp.Fori(0, EXPERTS) as e:
                    for i in range(E_PARTS):
                        part = TOTAL_PARTS + i
                        sp.wait_ge(lo_ready, 2 * (part - R + 1) + e * 2 * E_PARTS)
                        load(part % R, STATIC_PARTS + e * E_PARTS + i, 0)
            for n in range(2):
                for b in range(TB):
                    sp.wait_ge(done, 2 * n + b + 1)
                    sp.dma_start(out[b * P:(b + 1) * P, xslice(n)], xn[:, b, xslice(n)]).then_inc(out_sem, 16)
            sp.wait_ge(out_sem, 16 * 2 * TB)

        @block.gpsimd
        def _(pool):
            def load_gain(k):
                pool.dma_start(gain[:, :], norms[k:k + 1, :].to_broadcast([P, D])).then_inc(s_gain, 16)

            pool.wait_ge(s_x, 16)
            pool.dma_start(wg[:, :, :, :, :].rearrange("p a b n d -> p (a b n d)"),
                           gates_w[0, :, :]).then_inc(s_wg, 16)
            for s in STEPS:
                if s[0] == "norm":
                    pool.wait_ge(xn_ready, 2 * TB * (s[1] + 1))
                    load_gain(s[1] + 1)
                elif s == ("evac", 0, ("out", 0)):
                    product_done(pool, (0, ("att", 0)))
                    pool.dma_start(wg[:, :, :, :, :].rearrange("p a b n d -> p (a b n d)"),
                                   gates_w[1, :, :]).then_inc(s_wg, 16)
                elif s[0] == "la":
                    _, L, d, hf = s
                    n = slice(4 * hf, 4 * hf + 4)
                    pool.wait_ge(mid_free, mid_before(L, d * 4 + 2 * hf + 1)[1] + 4)
                    nc.gpsimd.tensor_tensor(ig[:, n, :], ig[:, n, :], xc[:, n, :],
                                            ALU.mult).then_inc(ix_ready, 1)
                elif s[0] == "rope":
                    L = s[1]
                    for n in range(3):
                        evacuated(pool, (L, ("qkv", n)))
                    bank_read(pool, TURN[("tx", L, 1)] + 1)
                    bank_read(pool, TURN[("tx", L, 1)])
                    z = qk[:, :, :].rearrange("p b (h w) -> p b h w", w=DH)
                    NH = QK // DH
                    t1, t2 = z[:, :, :, 0:8], z[:, :, :, 8:16]
                    cb = cos.rearrange("p b (o k) -> p b o k", o=1).to_broadcast([P, TB, NH, 8])
                    sb_ = sin.rearrange("p b (o k) -> p b o k", o=1).to_broadcast([P, TB, NH, 8])
                    flat = xn[:, :, :].rearrange("p b w -> p (b w)")
                    W = TB * NH * 8
                    tmp = [flat[:, i * W:(i + 1) * W].rearrange("p (b h k) -> p b h k", b=TB, k=8)
                           for i in range(4)]
                    for o, (a, c) in zip(tmp, ((t1, cb), (t2, sb_), (t2, cb), (t1, sb_))):
                        nc.gpsimd.tensor_tensor(o, a, c, ALU.mult).then_inc(rope_s, 1)
                    pool.wait_ge(rope_s, 4 * (L + 1))
                    nc.gpsimd.tensor_tensor(t1, tmp[0], tmp[1], ALU.subtract).then_inc(rope_done, 1)
                    nc.gpsimd.tensor_tensor(t2, tmp[2], tmp[3], ALU.add).then_inc(rope_done, 1)
            pool.wait_ge(s_gain, 16 * 2 * DEPTH)

        @block.scalar
        def _(act):
            act.dma_start(vec[:, :], vecs_in).then_inc(s_const, 16)
            act.dma_start(gain[:, :], norms[0:1, :].to_broadcast([P, D])).then_inc(s_gain0, 16)
            act.dma_start(const[:, :], consts_in).then_inc(s_const, 16)

            hi = [0]

            def turn_high(dst, src, idx):
                bank_full(act, idx)
                nc.scalar.activation(dst, src, ACT.Copy).then_inc(turn_hi, 1)
                hi[0] += 1

            act.wait_ge(chain, 1)
            nc.scalar.activation(rate[:, 1, :], rate[:, 0, :], ACT.Exp).then_inc(rate_s, 1)
            part = [0]

            def split_part():
                if part[0] < STATIC_PARTS:
                    split_hi(act, 2 * part[0])
                    split_hi(act, 2 * part[0] + 1)
                part[0] += 1

            def norm(k, x_ready):
                for n in range(2):
                    for b in range(TB):
                        x_ready(n, b)
                        if n == 0 and b == 0 and k:
                            act.wait_ge(ms_ready, k)
                        nc.scalar.activation(xn[:, b, xslice(n)], x[:, b, xslice(n)], ACT.Square,
                                             accum_out=ss[:, n, b:b + 1]).then_inc(sq_sum, 1)
                act.wait_ge(ms_ready, k + 1)
                nc.scalar.activation(sd, ms, ACT.Sqrt).then_inc(sd_ready, 1)

            split_part()

            for s in STEPS:
                kind = s[0]
                if kind == "norm":
                    k = s[1]

                    def x_ready(n, b):
                        if k == 0:
                            act.wait_ge(s_x, 16)
                        else:
                            x_done(act, k, n, b)

                    norm(k, x_ready)
                    for j in range(2):
                        for b in range(TB):
                            idx = TURN[s] + 2 * j + b
                            turn_high(a_hi[:, 4 * j:4 * j + 4, b * P:(b + 1) * P],
                                      turn[idx % 2][:, :].rearrange("p (k t) -> p k t", k=4), idx)
                elif kind == "G":
                    split_part()
                elif kind == "evac":
                    L, name = s[1:]
                    key = (L, name)
                    what, n = name[0], name[1]
                    p = PAIR[key][0]
                    if what in ("x", "y", "qkv"):
                        product_done(act, key)
                        if what == "y" and n == 0:
                            act.wait_ge(rope_done, 2 * (L + 1))
                        w = CB
                        if what != "qkv":
                            dst = xn[:, 0, xslice(n)]
                        else:
                            w = CB if n < 4 else VW - CB
                            dst = qk[:, 0, xslice(n)] if n < 3 else v[:, 0, (n - 3) * CB:(n - 3) * CB + w]
                        nc.scalar.activation(dst, acc(p, 0)[:, 0:w], ACT.Copy).then_inc(pair_free[p], 1)
                    elif what in ("g0", "g1"):
                        product_done(act, key)
                        if what == "g1":
                            bank_read(act, TURN[("tq", L, 4)])
                            bank_read(act, TURN[("tq", L, 5)])
                        else:
                            act.wait_ge(scanned, scans_done(L, 1, 1))
                        for b in range(TB):
                            dst = qk[:, b, xslice(n)] if what == "g1" else sg0[:, b, xslice(n)]
                            nc.scalar.activation(dst, acc(p, b), ACT.Sigmoid).then_inc(pair_free[p], 1)
                    elif what in ("out", "down"):
                        if name in (("out", 0), ("down", DSTEPS - 1, 1)):
                            nc.scalar.activation(idle, ident[:, 0:1], ACT.Sqrt).then_inc(idle_s, 1)
                    elif what == "gate":
                        product_done(act, key)
                        w = CB if n < DSTEPS else 2 * P
                        if n >= 2:
                            bank_full(act, TURN[("th", 0, n - 2)] + 1)
                        for b in range(TB):
                            nc.scalar.activation(hid[n % 2][:, b, 0:w], acc(p, b)[:, 0:w],
                                                 ACT.Silu).then_inc(pair_free[p], 1)
                elif kind == "ty":
                    _, L, c = s
                    for k in range(2):
                        idx = TURN[s] + k
                        n = 4 * c + 2 * k
                        bank_full(act, idx)
                        nc.scalar.activation(gy[:, n:n + 2, :],
                                             turn[idx % 2][:, :].rearrange("p (n t) -> p n t", n=2),
                                             ACT.Gelu_apprx_tanh).then_inc(turn_free[idx % 2], 1)
                elif kind == "lg":
                    _, L, d, pr = s
                    act.wait_ge(mid_full, mid_before(L, d * 4 + pr)[0] + 1)
                    if L or d:
                        act.wait_ge(scanned, scans_done(L, d - 1, pr // 2))
                    for q in range(2):
                        n = 2 * pr + q
                        for g, (dst, bias) in enumerate(((rg, b_r), (ig, b_i))):
                            nc.scalar.activation(dst[:, n, :], mid[:, q, g * T:(g + 1) * T], ACT.Sigmoid,
                                                 bias=bias[:, L, d, n:n + 1]).then_inc(mid_free, 1)
                elif kind == "la":
                    _, L, d, hf = s
                    k = (L * 2 + d) * 2 + hf
                    if k == 0:
                        act.wait_ge(rate_ready, 2)
                    else:
                        act.wait_ge(scanned, 4 * k)
                    act.wait_ge(mid_free, mid_before(L, d * 4 + 2 * hf + 1)[1] + 4)
                    for q in range(4):
                        n = 4 * hf + q
                        col = (L * 2 + d) * KT + n
                        nc.scalar.activation(root[:, q, :], rg[:, n, :], ACT.Tanh,
                                             scale=rate[:, 0, col:col + 1]).then_inc(tanh_ready, 1)
                    act.wait_ge(tanh_ready, 4 * (k + 1))
                    for q in range(4):
                        n = 4 * hf + q
                        col = (L * 2 + d) * KT + n
                        nc.scalar.activation(rg[:, n, :], rg[:, n, :], ACT.Exp,
                                             scale=rate[:, 1, col:col + 1]).then_inc(decay_ready, 1)
                elif kind == "lb":
                    nc.scalar.activation(root[:, :, :], root[:, :, :], ACT.Sqrt).then_inc(sq_ready, 1)
                elif kind == "lf":
                    _, L, pr = s
                    act.wait_ge(lru_full, 4 * L + pr + 1)
                    nc.scalar.activation(lru_hi[:, 2 * pr:2 * pr + 2, :], gy[:, 2 * pr:2 * pr + 2, :],
                                         ACT.Copy).then_inc(lru_hi_ready, 1)
                elif kind == "tq" and s[2] % 2 == 0:
                    idx = TURN[s]
                    bank_full(act, idx)
                    act.wait_ge(scanned, scans_done(s[1], 1, 1))
                    nc.scalar.activation(qkT[:, s[2], :, :],
                                         turn[idx % 2][:, :].rearrange("p (a t) -> p a t", a=2),
                                         ACT.Copy).then_inc(turn_free[idx % 2], 1)
                elif kind == "as":
                    _, L, u = s
                    k = 8 * L + u
                    act.wait_ge(nm_ready, k + 1)
                    nc.scalar.activation(sm[:, u % 2, :], sm[:, u % 2, :], ACT.Exp,
                                         bias=nm[:, u % 2:u % 2 + 1], scale=SCALE,
                                         accum_out=rs[:, u % 2:u % 2 + 1]).then_inc(p_ready, 1)
                elif kind == "ap":
                    idx = TURN[s]
                    bank_full(act, idx)
                    nc.scalar.activation(pt[:, 0:4, :],
                                         turn[idx % 2][:, :].rearrange("p (a t) -> p a t", a=4),
                                         ACT.Copy).then_inc(turn_free[idx % 2], 1)
                elif kind == "ta":
                    turn_high(att_hi[:, :, :],
                              turn[TURN[s] % 2][:, :].rearrange("p (a t) -> p a t", a=2), TURN[s])
                elif kind == "tm":
                    j = s[2]
                    for b in range(TB):
                        idx = TURN[s] + b
                        turn_high(a_hi[:, 4 * j:4 * j + 4, b * P:(b + 1) * P],
                                  turn[idx % 2][:, :].rearrange("p (k t) -> p k t", k=4), idx)
                elif kind == "th":
                    c = s[2]
                    w = 4 if c < DSTEPS else 2
                    for b in range(TB):
                        idx = TURN[s] + b
                        if b == 0 and c >= 2:
                            product_done(act, (0, ("down", c - 2, 1)))
                        turn_high(hT_hi[c % 2][:, 0:w, b * P:(b + 1) * P],
                                  turn[idx % 2][:, 0:w * P].rearrange("p (k t) -> p k t", k=w), idx)

            for b in range(TB):
                act.wait_ge(xn_ready, 2 * TB * 2 * DEPTH - TB + b + 1)
                nc.scalar.activation(xn_hi[:, b, :], xn[:, b, :], ACT.Copy).then_inc(xn_hi_ready, 1)
            nc.scalar.activation(rw[:, 0, :], router, ACT.Copy).then_inc(rw_ready, 1)
            act.wait_ge(top_ready, 1)
            nc.scalar.activation(lg[:, :, :], lg[:, :, :], ACT.Exp).then_inc(share_exp, 1)

            def experts(pas):
                t0 = T0 + pas * (2 + EXPERTS * E_TURNS + 4)
                h0 = H0 + pas * EXPERTS * E_HALVES

                def full(idx, e):
                    act.wait_ge(turned, idx + 1 + e * E_TURNS)

                def gather_hi(first, j, e):
                    full(first + j, e)
                    nc.scalar.activation(g_hi[:, 4 * j:4 * j + 4, :],
                                         turn[(first + j) % 2][:, :].rearrange("p (k t) -> p k t", k=4),
                                         ACT.Copy).then_inc(g_hi_ready, 1)

                def output_hi(n, e):
                    act.wait_ge(used, h0 + e * E_HALVES)
                    nc.scalar.activation(y_hi[:, xslice(n)], mid[:, n, :], ACT.Copy).then_inc(y_hi_ready, 1)

                for j in range(2):
                    gather_hi(t0, j, 0)
                tl = t0 + 2
                with act.Fori(0, EXPERTS) as e:
                    for i in range(E_HALVES):
                        split_hi(act, h0 + i, e)
                        for n in range(2):
                            if i == 1 + n:
                                output_hi(n, e)
                        for c in range(ESTEPS):
                            if i == AT_HID[c] + 1:
                                idx = tl + U_HID + c
                                full(idx, e)
                                nc.scalar.activation(eT_hi[c % 2][:, :, :],
                                                     turn[idx % 2][:, :].rearrange("p (k t) -> p k t", k=4),
                                                     ACT.Copy).then_inc(eT_hi_ready, 1)
                            if i == E_AT["gate", c] + 5:
                                act.wait_ge(used, h0 + E_AT["gate", c] + 4 + e * E_HALVES)
                                nc.scalar.activation(eh[c % 2][:, :], bank[2 * (c % 2)][:, :],
                                                     ACT.Silu).then_inc(e_silu, 1)
                        for j in range(2):
                            if i == AT_GATHER[j] + 1:
                                gather_hi(tl + U_GATH, j, e)
                for n in range(2):
                    output_hi(n, EXPERTS)

            experts(0)
            act.wait_ge(route_ready, 1)
            n = act.value_load(most_i[0:1, 0:1], min_val=0, max_val=T)
            with act.If(n > NPASS_TOKENS):
                experts(1)
            norm(2 * DEPTH, lambda n, b: act.wait_ge(x_final, 1))

        @block.tensor
        def _(pe):
            def turn_bank(idx):
                if idx >= 2:
                    pe.wait_ge(turn_free[idx % 2], idx // 2)
                return turn[idx % 2]

            def gemm(key, part, s_hi, s_lo):
                kind = KIND[key]
                kts, cols, width = {"n": (2, CB, 1), "h": (4, 2 * P, 1), "w": (1, CB, 2)}[kind]
                last_kt = (1 if (key, 1) not in HALF_AT else 2) * 2 * kts - 1
                if part == 0:
                    for n in range(width):
                        if FREED[key][n]:
                            pe.wait_ge(pair_free[PAIR[key][n]], FREED[key][n])
                for hh in range(2):
                    h = half_of(key, part) + hh
                    pe.wait_ge(lo_ready, h + 1)
                    for k in range(kts):
                        kt = (part * 2 + hh) * kts + k
                        for n in range(width):
                            o = (k * width + n) * cols
                            wh = w_hi[:, h % H, o:o + cols]
                            wl = w_lo[:, h % H, o:o + cols]
                            for b in range(TB):
                                ins = mm3(acc(PAIR[key][n], b)[:, 0:cols],
                                          s_hi[:, kt, b * P:(b + 1) * P], s_lo[:, kt, b * P:(b + 1) * P],
                                          wh, wl, start=kt == 0, stop=kt == last_kt)
                    ins.then_inc(used, 1)

            pe.wait_ge(s_const, 32)
            for s in STEPS:
                kind = s[0]
                if kind == "norm":
                    for j in range(2):
                        for b in range(TB):
                            pe.wait_ge(xn_ready, 2 * TB * s[1] + 2 * j + b + 1)
                            idx = TURN[s] + 2 * j + b
                            t_ = turn_bank(idx)
                            for k in range(4):
                                kt = 4 * j + k
                                ins = nc.tensor.transpose(t_[:, k * P:(k + 1) * P],
                                                          xn[:, b, kt * P:(kt + 1) * P], ident)
                            ins.then_inc(turned, 1)
                    a_from = TURN[s]
                elif kind == "G":
                    key = s[1]
                    what = key[1][0]
                    if what == "out" and key[1][1] == 0:
                        a_from = TURN[("tm", key[0], 0)]
                    if what == "lru":
                        if s[2] == 0 and key[1][1] == 0:
                            pe.wait_ge(lru_ready, 4 * (key[0] + 1))
                        gemm(key, s[2], lru_hi, lru_lo)
                    elif what == "att":
                        bank_read(pe, TURN[("ta", key[0])])
                        gemm(key, s[2], att_hi, att_lo)
                    elif what == "down":
                        for b in range(TB):
                            bank_read(pe, TURN[("th", 0, key[1][1])] + b)
                        gemm(key, s[2], hT_hi[key[1][1] % 2], hT_lo[key[1][1] % 2])
                    else:
                        first = 0 if KIND[key] == "n" and s[2] == 0 else 2
                        for b in range(TB):
                            bank_read(pe, a_from + first + b)
                        gemm(key, s[2], a_hi, a_lo)
                elif kind in ("tx", "ty"):
                    _, L, c = s
                    evacuated(pe, (L, ("x" if kind == "tx" else "y", c)))
                    for k in range(2):
                        idx = TURN[s] + k
                        t_ = turn_bank(idx)
                        for q in range(2):
                            n = 4 * c + 2 * k + q
                            for b in range(TB):
                                ins = nc.tensor.transpose(t_[:, q * T + b * P:q * T + (b + 1) * P],
                                                          xn[:, b, n * P:(n + 1) * P], ident)
                        ins.then_inc(turned, 1)
                elif kind == "lg":
                    _, L, d, pr = s
                    uses, frees = mid_before(L, d * 4 + pr)
                    if frees:
                        pe.wait_ge(mid_free, frees)
                    pe.wait_ge(xc_ready, KT * L + 2 * pr + 2)
                    pe.wait_ge(s_wg, 16 * (L + 1))
                    for q in range(2):
                        n = 2 * pr + q
                        for g in range(2):
                            ins = nc.tensor.matmul(mid[:, q, g * T:(g + 1) * T], wg[:, d, g, n, :],
                                                   xc[:, n, :], start=True, stop=True)
                    ins.then_inc(mid_full, 1)
                elif kind == "tq":
                    _, L, j = s
                    pe.wait_ge(rope_done, 2 * (L + 1))
                    idx = TURN[s]
                    t_ = turn_bank(idx)
                    for a in range(2):
                        for b in range(TB):
                            o = a * (QK // 2) + j * P
                            ins = nc.tensor.transpose(t_[:, a * T + b * P:a * T + (b + 1) * P],
                                                      qk[:, b, o:o + P], ident)
                    ins.then_inc(turned, 1)
                elif kind == "as":
                    _, L, u = s
                    b, sl = u // SLOTS, u % SLOTS
                    uses, frees = mid_before(L, 8 + u)
                    pe.wait_ge(mid_free, frees)
                    if u == 0:
                        for j in range(4, 6):
                            bank_read(pe, TURN[("tq", L, j)])
                    flat = mid[:, :, :].rearrange("p a c -> p (a c)")
                    for g in range(GROUPS):
                        head = g * SLOTS + sl
                        o = DH * (head % 2)
                        ins = nc.tensor.matmul(flat[:, g * T:(g + 1) * T],
                                               qkT[o:o + DH, head // 2, 0, b * P:(b + 1) * P],
                                               qkT[o:o + DH, head // 2, 1, :], start=True, stop=True)
                    ins.then_inc(mid_full, 1)
                elif kind == "ap":
                    _, L, u = s
                    pe.wait_ge(p_ready, 8 * L + u + 1)
                    for i, n in enumerate((4, 2)):
                        idx = TURN[s] + i
                        t_ = turn_bank(idx)
                        for k in range(n):
                            o = (4 * i + k) * P
                            ins = nc.tensor.transpose(t_[:, k * P:(k + 1) * P], sm[:, u % 2, o:o + P], ident)
                        ins.then_inc(turned, 1)
                elif kind == "av":
                    _, L, u = s
                    b, sl = u // SLOTS, u % SLOTS
                    for i in range(2):
                        bank_read(pe, TURN[("ap", L, u)] + i)
                    idx = TURN[s]
                    t_ = turn_bank(idx)
                    for i in range(2 * GROUPS):
                        g, kb = i // 2, i % 2
                        o = (g * SLOTS + sl) * DH
                        ins = nc.tensor.matmul(t_[:, 0:DH], pt[:, i, :], v[:, kb, o:o + DH],
                                               start=i == 0, stop=i == 2 * GROUPS - 1)
                    ins.then_inc(turned, 1)
                elif kind == "ta":
                    _, L = s
                    for u in range(6, 8):
                        bank_read(pe, TURN[("av", L, u)])
                    idx = TURN[s]
                    t_ = turn_bank(idx)
                    for a in range(2):
                        for b in range(TB):
                            ins = nc.tensor.transpose(t_[:, a * T + b * P:a * T + (b + 1) * P],
                                                      att[:, b, a * P:(a + 1) * P], ident)
                    ins.then_inc(turned, 1)
                elif kind == "tm":
                    _, L, j = s
                    pe.wait_ge(merged, 2 * L + j + 1)
                    for b in range(TB):
                        idx = TURN[s] + b
                        t_ = turn_bank(idx)
                        for k in range(4):
                            kt = 4 * j + k
                            ins = nc.tensor.transpose(t_[:, k * P:(k + 1) * P],
                                                      qk[:, b, kt * P:(kt + 1) * P], ident)
                        ins.then_inc(turned, 1)
                elif kind == "th":
                    _, L, c = s
                    evacuated(pe, (L, ("up", c)))
                    w = 4 if c < DSTEPS else 2
                    for b in range(TB):
                        idx = TURN[s] + b
                        t_ = turn_bank(idx)
                        for k in range(w):
                            ins = nc.tensor.transpose(t_[:, k * P:(k + 1) * P],
                                                      hid[c % 2][:, b, k * P:(k + 1) * P], ident)
                        ins.then_inc(turned, 1)

            pe.wait_ge(rw_ready, 2)
            for b in range(TB):
                for kt in range(KT):
                    c = slice(kt * EXPERTS, (kt + 1) * EXPERTS)
                    ins = mm3(mid[:, b, 0:EXPERTS], a_hi[:, kt, b * P:(b + 1) * P],
                              a_lo[:, kt, b * P:(b + 1) * P], rw[:, 0, c], rw[:, 1, c],
                              start=kt == 0, stop=kt == KT - 1)
            ins.then_inc(logit_full, 1)
            pe.wait_ge(mask_ready, 1)
            nc.tensor.matmul(mid[:, 0, 0:EXPERTS], before, mask[:, 0, :], start=True, stop=True)
            nc.tensor.matmul(mid[:, 1, 0:EXPERTS], before, mask[:, 1, :], start=True, stop=False)
            nc.tensor.matmul(mid[:, 1, 0:EXPERTS], ones, mask[:, 0, :], start=False, stop=True)
            nc.tensor.matmul(bank[0][:, 0:EXPERTS], ones, mask[:, 0, :], start=True, stop=False)
            nc.tensor.matmul(bank[0][:, 0:EXPERTS], ones, mask[:, 1, :], start=False,
                             stop=True).then_inc(rank_full, 1)

            def wait_turn(idx, e):
                pe.wait_ge(turn_free[idx % 2], idx // 2 + e * (E_TURNS // 2))
                return turn[idx % 2]

            def read_out(idx, e):
                pe.wait_ge(turn_free[idx % 2], idx // 2 + 1 + e * (E_TURNS // 2))

            def gather(idx, j, e):
                t_ = wait_turn(idx + j, e)
                for k in range(4):
                    kt = 4 * j + k
                    for i, (src, b) in enumerate([(s_, b) for b in range(TB) for s_ in (xn_hi, xn_lo)]):
                        ins = nc.tensor.matmul(t_[:, k * P:(k + 1) * P], src[:, b, kt * P:(kt + 1) * P],
                                               sel[:, b, :], start=i == 0, stop=i == 2 * TB - 1)
                ins.then_inc(turned, 1)

            def combine(idx, i, e):
                b, n = i // 2, i % 2
                t_ = wait_turn(idx + i, e)
                nc.tensor.matmul(t_[:, :], selT[:, b * P:(b + 1) * P], y_hi[:, xslice(n)],
                                 start=True, stop=False)
                nc.tensor.matmul(t_[:, :], selT[:, b * P:(b + 1) * P], y_lo[:, xslice(n)],
                                 start=False, stop=True).then_inc(turned, 1)

            def experts(pas):
                g0 = pas * (EXPERTS + 1)
                t0 = T0 + pas * (2 + EXPERTS * E_TURNS + 4)
                h0 = H0 + pas * EXPERTS * E_HALVES
                s0 = pas * EXPERTS * ESTEPS
                pe.wait_ge(sel_ready, TB * (g0 + 1))
                for j in range(2):
                    gather(t0, j, 0)
                tl = t0 + 2
                with pe.Fori(0, EXPERTS) as e:
                    for j in range(2):
                        read_out(t0 + j, e)
                    for i in range(E_HALVES):
                        for m, at_ in enumerate(AT_COMBINE):
                            if i == at_:
                                if m == 0:
                                    pe.wait_ge(y_ready, 2 + 2 * (g0 + 1) + e * 2)
                                combine(tl + U_COMB, m, e)
                        if i == AT_SLOT:
                            t_ = wait_turn(tl + U_SLOT, e)
                            for b in range(TB):
                                ins = nc.tensor.transpose(t_[:, b * P:(b + 1) * P],
                                                          sel[:, b, :].bitcast(F32), ident)
                            ins.then_inc(turned, 1)
                        for c in range(ESTEPS):
                            if i == AT_HID[c]:
                                t_ = wait_turn(tl + U_HID + c, e)
                                pe.wait_ge(e_hid, s0 + c + 1 + e * ESTEPS)
                                for k in range(4):
                                    ins = nc.tensor.transpose(t_[:, k * P:(k + 1) * P],
                                                              eh[c % 2][:, k * P:(k + 1) * P], ident)
                                ins.then_inc(turned, 1)
                        for j in range(2):
                            if i == AT_GATHER[j]:
                                if j == 0:
                                    pe.wait_ge(sel_ready, TB * (g0 + 2) + e * TB)
                                gather(tl + U_GATH, j, e)
                        (what, c), hh = expert_order()[i // 4], i % 4
                        h = h0 + i
                        if what == "down":
                            if hh == 0:
                                read_out(tl + U_HID + c, e)
                            pe.wait_ge(lo_ready, h + 1 + e * E_HALVES)
                            for n in range(2):
                                ins = mm3(mid[:, n, :], eT_hi[c % 2][:, hh, :], eT_lo[c % 2][:, hh, :],
                                          w_hi[:, h % H, xslice(n)], w_lo[:, h % H, xslice(n)],
                                          start=c == 0 and hh == 0, stop=c == ESTEPS - 1 and hh == 3)
                        else:
                            o_ = bank[2 * (c % 2) + (what == "up")]
                            pe.wait_ge(lo_ready, h + 1 + e * E_HALVES)
                            for k in range(2):
                                kt = 2 * hh + k
                                ins = mm3(o_[:, :], g_hi[:, kt, :], g_lo[:, kt, :],
                                          w_hi[:, h % H, xslice(k)], w_lo[:, h % H, xslice(k)],
                                          start=kt == 0, stop=kt == KT - 1)
                        ins.then_inc(used, 1)
                pe.wait_ge(y_ready, 2 + 2 * (EXPERTS + 1) * (pas + 1))
                for m in range(4):
                    combine(tl + EXPERTS * E_TURNS, m, 0)

            experts(0)
            pe.wait_ge(route_ready, 1)
            n = pe.value_load(most_i[0:1, 0:1], min_val=0, max_val=T)
            with pe.If(n > NPASS_TOKENS):
                experts(1)

        @block.vector
        def _(dve):
            links = [0]
            hi = [0]

            def link(ins):
                ins.then_inc(chain, 1)
                links[0] += 1
                dve.wait_ge(chain, links[0])

            def turn_low(dst, dst_hi, src, idx):
                hi[0] += 1
                dve.wait_ge(turn_hi, hi[0])
                nc.vector.tensor_tensor(dst, src, dst_hi.bitcast(F32),
                                        ALU.subtract).then_inc(turn_free[idx % 2], 1)

            def norm(k, final=False):
                dve.wait_ge(sq_sum, 4 * (k + 1))
                link(nc.vector.tensor_tensor(ms, ss[:, 0, :], ss[:, 1, :], ALU.add))
                nc.vector.tensor_scalar(ms, ms, 1.0 / D, EPS, ALU.mult, ALU.add).then_inc(ms_ready, 1)
                dve.wait_ge(sd_ready, k + 1)
                link(nc.vector.reciprocal(rstd, sd))
                if k == 0:
                    dve.wait_ge(s_gain0, 16)
                else:
                    dve.wait_ge(s_gain, 16 * k)
                for n in range(2):
                    for b in range(TB):
                        nc.vector.scalar_tensor_tensor(
                            out=xn[:, b, xslice(n)], in0=x[:, b, xslice(n)], scalar=rstd[:, b:b + 1],
                            in1=gain[:, xslice(n)], op0=ALU.mult,
                            op1=ALU.mult).then_inc(done if final else xn_ready, 1)

            dve.wait_ge(s_const, 32)
            part = [0]

            def split_part():
                if part[0] < STATIC_PARTS:
                    split_lo(dve, 2 * part[0])
                    split_lo(dve, 2 * part[0] + 1)
                part[0] += 1

            r0, r1, r2 = rate[:, 0, :], rate[:, 1, :], rate[:, 2, :]
            nc.vector.scalar_tensor_tensor(out=r0, in0=lam, scalar=-1.0, in1=lam, op0=ALU.mult,
                                           op1=ALU.min).then_inc(chain, 1)
            links[0] += 1
            dve.wait_ge(rate_s, 1)
            link(nc.vector.tensor_scalar(r2, r1, 2.0, None, ALU.add))
            link(nc.vector.reciprocal(r2, r2))
            link(nc.vector.tensor_tensor(r0, r1, r2, ALU.mult))
            link(nc.vector.tensor_tensor(r1, r0, r0, ALU.mult))
            TERMS = 9
            link(nc.vector.tensor_scalar(r2, r1, 1.0 / (2 * TERMS + 1), 1.0 / (2 * TERMS - 1),
                                         ALU.mult, ALU.add))
            for i in range(TERMS - 2, -1, -1):
                link(nc.vector.tensor_tensor(r2, r2, r1, ALU.mult))
                link(nc.vector.tensor_scalar(r2, r2, 1.0 / (2 * i + 1), None, ALU.add))
            link(nc.vector.scalar_tensor_tensor(out=r2, in0=r2, scalar=2.0, in1=r0, op0=ALU.mult, op1=ALU.mult))
            link(nc.vector.tensor_scalar(r1, lam, -1.0, 0.0, ALU.mult, ALU.max))
            link(nc.vector.tensor_tensor(r2, r2, r1, ALU.add))
            nc.vector.tensor_scalar(r0, r2, 4.0, None, ALU.mult).then_inc(rate_ready, 1)
            nc.vector.tensor_scalar(r1, r2, -8.0, None, ALU.mult).then_inc(rate_ready, 1)
            split_part()

            for s in STEPS:
                kind = s[0]
                if kind == "norm":
                    k = s[1]
                    norm(k)
                    if k % 2 == 0:
                        nc.vector.memset(xT[:, :, 0:1], 0.0).then_inc(chain, 1)
                        nc.vector.memset(xT[:, :, T + 1:T + 3], 0.0).then_inc(chain, 1)
                        links[0] += 2
                    for j in range(2):
                        for b in range(TB):
                            idx = TURN[s] + 2 * j + b
                            c = (slice(None), slice(4 * j, 4 * j + 4), slice(b * P, (b + 1) * P))
                            turn_low(a_lo[c], a_hi[c],
                                     turn[idx % 2][:, :].rearrange("p (k t) -> p k t", k=4), idx)
                elif kind == "G":
                    split_part()
                elif kind == "evac":
                    L, name = s[1:]
                    key = (L, name)
                    what, n = name[0], name[1]
                    p = PAIR[key][0]
                    if what in ("x", "y", "qkv"):
                        product_done(dve, key)
                        if what == "y" and n == 0:
                            dve.wait_ge(rope_done, 2 * (L + 1))
                        w = CB
                        if what != "qkv":
                            dst = xn[:, 1, xslice(n)]
                        else:
                            w = CB if n < 4 else VW - CB
                            dst = qk[:, 1, xslice(n)] if n < 3 else v[:, 1, (n - 3) * CB:(n - 3) * CB + w]
                        nc.vector.tensor_copy(dst, acc(p, 1)[:, 0:w]).then_inc(pair_free[p], 1)
                    elif what == "lru":
                        product_done(dve, key)
                        evacuated(dve, (L, ("g0", n)))
                        for b in range(TB):
                            g = sg0[:, b, xslice(n)]
                            nc.vector.tensor_tensor(g, acc(p, b), g, ALU.mult).then_inc(pair_free[p], 1)
                    elif what == "att":
                        product_done(dve, key)
                        for n in range(2):
                            evacuated(dve, (L, ("g1", n)))
                            for b in range(TB):
                                g = qk[:, b, xslice(n)]
                                nc.vector.tensor_tensor(g, acc(PAIR[key][n], b), g,
                                                        ALU.mult).then_inc(pair_free[PAIR[key][n]], 1)
                    elif what in ("out", "down"):
                        product_done(dve, key)
                        wide = KIND[key] == "w"
                        for i in range(len(PAIR[key])):
                            n_ = i if wide else (name[1] if what == "out" else name[2])
                            if what == "down" and (name[1] > 0):
                                evacuated(dve, (L, ("down", name[1] - 1, n_)))
                            for b in range(TB):
                                xs = x[:, b, xslice(n_)]
                                nc.vector.tensor_tensor(xs, acc(PAIR[key][i], b), xs,
                                                        ALU.add).then_inc(pair_free[PAIR[key][i]], 1)
                    elif what == "up":
                        product_done(dve, key)
                        evacuated(dve, (L, ("gate", n)))
                        w = CB if n < DSTEPS else 2 * P
                        for b in range(TB):
                            hs = hid[n % 2][:, b, 0:w]
                            nc.vector.tensor_tensor(hs, acc(p, b)[:, 0:w], hs,
                                                    ALU.mult).then_inc(pair_free[p], 1)
                elif kind == "merge":
                    _, L, j = s
                    evacuated(dve, (L, ("att", 0)), j)
                    evacuated(dve, (L, ("lru", j)))
                    g = qk[:, :, xslice(j)]
                    nc.vector.tensor_tensor(g, g, sg0[:, :, xslice(j)], ALU.add).then_inc(merged, 1)
                elif kind == "tx":
                    _, L, c = s
                    for k in range(2):
                        idx = TURN[s] + k
                        n = 4 * c + 2 * k
                        bank_full(dve, idx)
                        nc.vector.tensor_copy(xT[:, n:n + 2, 1:T + 1],
                                              turn[idx % 2][:, :].rearrange("p (n t) -> p n t", n=2)
                                              ).then_inc(turn_free[idx % 2], 1)
                elif kind == "conv":
                    _, L, pr = s
                    bank_read(dve, TURN[("tx", L, pr // 2)] + pr % 2)
                    for q in range(2):
                        n = 2 * pr + q
                        nc.vector.tensor_scalar(xc[:, n, :], xT[:, n, 0:T], convw[:, L, 0, n:n + 1],
                                                convb[:, L, n:n + 1], ALU.mult, ALU.add).then_inc(chain, 1)
                        links[0] += 1
                    for j in range(1, 4):
                        for q in range(2):
                            n = 2 * pr + q
                            dve.wait_ge(chain, links[0] - 1)
                            ins = nc.vector.scalar_tensor_tensor(
                                out=xc[:, n, :], in0=xT[:, n, j:j + T], scalar=convw[:, L, j, n:n + 1],
                                in1=xc[:, n, :], op0=ALU.mult, op1=ALU.add)
                            if j < 3:
                                ins.then_inc(chain, 1)
                                links[0] += 1
                            else:
                                ins.then_inc(xc_ready, 1)
                            if j == 3 and q == 0:
                                dve.wait_ge(chain, links[0])
                elif kind == "lb":
                    _, L, d, hf = s
                    k = (L * 2 + d) * 2 + hf
                    n4 = slice(4 * hf, 4 * hf + 4)
                    dve.wait_ge(decay_ready, 4 * (k + 1))
                    dve.wait_ge(sq_ready, k + 1)
                    link(nc.vector.scalar_tensor_tensor(out=root[:, :, :], in0=rg[:, n4, :], scalar=1.0,
                                                        in1=root[:, :, :], op0=ALU.add, op1=ALU.mult))
                    dve.wait_ge(ix_ready, k + 1)
                    link(nc.vector.tensor_tensor(ig[:, n4, :], root[:, :, :], ig[:, n4, :], ALU.mult))
                    for q in range(4):
                        n = 4 * hf + q
                        if d == 0:
                            nc.vector.tensor_tensor_scan(xT[:, n, 0:T], rg[:, n, :], ig[:, n, :], 0.0,
                                                         ALU.mult, ALU.add).then_inc(scanned, 1)
                        else:
                            back = slice(T - 1, None, -1)
                            nc.vector.tensor_tensor_scan(root[:, q, back], rg[:, n, back], ig[:, n, back],
                                                         0.0, ALU.mult, ALU.add).then_inc(chain, 1)
                            links[0] += 1
                    if d == 1:
                        dve.wait_ge(chain, links[0])
                        nc.vector.tensor_tensor(xT[:, n4, 0:T], xT[:, n4, 0:T], root[:, :, :],
                                                ALU.add).then_inc(scanned, 4)
                elif kind == "lf":
                    _, L, pr = s
                    dve.wait_ge(scanned, scans_done(L, 1, 1))
                    for i in range(2):
                        bank_read(dve, TURN[("ty", L, 1)] + i)
                    y2 = gy[:, 2 * pr:2 * pr + 2, :]
                    nc.vector.tensor_tensor(y2, xT[:, 2 * pr:2 * pr + 2, 0:T], y2,
                                            ALU.mult).then_inc(lru_full, 1)
                    dve.wait_ge(lru_hi_ready, 4 * L + pr + 1)
                    nc.vector.tensor_tensor(lru_lo[:, 2 * pr:2 * pr + 2, :], y2,
                                            lru_hi[:, 2 * pr:2 * pr + 2, :].bitcast(F32),
                                            ALU.subtract).then_inc(lru_ready, 1)
                elif kind == "tq" and s[2] % 2 == 1:
                    idx = TURN[s]
                    bank_full(dve, idx)
                    dve.wait_ge(scanned, scans_done(s[1], 1, 1))
                    nc.vector.tensor_copy(qkT[:, s[2], :, :],
                                          turn[idx % 2][:, :].rearrange("p (a t) -> p a t", a=2)
                                          ).then_inc(turn_free[idx % 2], 1)
                elif kind == "as":
                    _, L, u = s
                    b = u // SLOTS
                    uses, frees = mid_before(L, 8 + u)
                    dve.wait_ge(mid_full, uses + 1)
                    if u >= 2:
                        bank_full(dve, TURN[("ap", L, u - 2)] + 1)
                        bank_read(dve, TURN[("av", L, u - 2)])
                    flat = mid[:, :, :].rearrange("p a c -> p (a c)")
                    nc.vector.tensor_tensor_reduce(out=sm[:, u % 2, :], in0=flat[:, 0:GROUPS * T],
                                                   in1=band[:, b, :], scale=1.0, scalar=NEG, op0=ALU.add,
                                                   op1=ALU.max,
                                                   accum_out=mx[:, u % 2:u % 2 + 1]).then_inc(mid_free, 1)
                    dve.wait_ge(mid_free, frees + 1)
                    nc.vector.tensor_scalar(nm[:, u % 2:u % 2 + 1], mx[:, u % 2:u % 2 + 1], -SCALE, None,
                                            ALU.mult).then_inc(nm_ready, 1)
                elif kind == "ap":
                    _, L, u = s
                    idx = TURN[s] + 1
                    bank_full(dve, idx)
                    nc.vector.tensor_copy(pt[:, 4:6, :],
                                          turn[idx % 2][:, 0:2 * P].rearrange("p (a t) -> p a t", a=2)
                                          ).then_inc(turn_free[idx % 2], 1)
                    dve.wait_ge(p_ready, 8 * L + u + 1)
                    link(nc.vector.reciprocal(rr[:, u % 2:u % 2 + 1], rs[:, u % 2:u % 2 + 1]))
                elif kind == "av":
                    _, L, u = s
                    b, sl = u // SLOTS, u % SLOTS
                    idx = TURN[s]
                    bank_full(dve, idx)
                    nc.vector.tensor_scalar(att[:, b, sl * DH:(sl + 1) * DH], turn[idx % 2][:, 0:DH],
                                            rr[:, u % 2:u % 2 + 1], None,
                                            ALU.mult).then_inc(turn_free[idx % 2], 1)
                elif kind == "ta":
                    turn_low(att_lo[:, :, :], att_hi[:, :, :],
                             turn[TURN[s] % 2][:, :].rearrange("p (a t) -> p a t", a=2), TURN[s])
                elif kind == "tm":
                    j = s[2]
                    for b in range(TB):
                        idx = TURN[s] + b
                        c = (slice(None), slice(4 * j, 4 * j + 4), slice(b * P, (b + 1) * P))
                        turn_low(a_lo[c], a_hi[c],
                                 turn[idx % 2][:, :].rearrange("p (k t) -> p k t", k=4), idx)
                elif kind == "th":
                    c = s[2]
                    w = 4 if c < DSTEPS else 2
                    for b in range(TB):
                        idx = TURN[s] + b
                        r_ = (slice(None), slice(0, w), slice(b * P, (b + 1) * P))
                        turn_low(hT_lo[c % 2][r_], hT_hi[c % 2][r_],
                                 turn[idx % 2][:, 0:w * P].rearrange("p (k t) -> p k t", k=w), idx)

            for b in range(TB):
                dve.wait_ge(xn_hi_ready, b + 1)
                nc.vector.tensor_tensor(xn_lo[:, b, :], xn[:, b, :], xn_hi[:, b, :].bitcast(F32),
                                        ALU.subtract).then_inc(xn_lo_ready, 1)
            dve.wait_ge(rw_ready, 1)
            nc.vector.tensor_tensor(rw[:, 1, :], router, rw[:, 0, :].bitcast(F32),
                                    ALU.subtract).then_inc(rw_ready, 1)
            nc.vector.memset(y_hi[:, :].bitcast(F32), 0.0).then_inc(chain, 1)
            nc.vector.memset(y_lo[:, :].bitcast(F32), 0.0).then_inc(chain, 1)
            nc.vector.memset(selT[:, :].bitcast(F32), 0.0).then_inc(chain, 1)
            nc.vector.memset(slot[:, :, :], -1.0).then_inc(chain, 1)
            links[0] += 4
            dve.wait_ge(chain, links[0])
            nc.vector.memset(share[:, :, :], 0.0).then_inc(y_ready, 2)
            dve.wait_ge(y_ready, 2)
            dve.wait_ge(logit_full, 1)
            link(nc.vector.tensor_copy(lg[:, :, :], mid[:, :, 0:EXPERTS]))
            shape = [P, TB, EXPERTS, EXPERTS]
            for b in range(TB):
                nc.vector.max(top[:, b, :], lg[:, b, :]).then_inc(chain, 1)
            rival = lg[:, :, :].rearrange("p b (o e) -> p b o e", o=1).to_broadcast(shape)
            own = lg[:, :, :].rearrange("p b (e o) -> p b e o", o=1).to_broadcast(shape)
            low = lower.rearrange("p (o a) e -> p o a e", o=1).to_broadcast(shape)
            nc.vector.tensor_tensor(cmp_[:, :, :, :], rival, own, ALU.is_gt).then_inc(chain, 1)
            nc.vector.tensor_tensor(cmp2[:, :, :, :], rival, own, ALU.is_equal).then_inc(chain, 1)
            links[0] += TB + 2
            dve.wait_ge(chain, links[0])
            link(nc.vector.tensor_tensor(cmp2[:, :, :, :], cmp2[:, :, :, :], low, ALU.mult))
            link(nc.vector.tensor_tensor(cmp_[:, :, :, :], cmp_[:, :, :, :], cmp2[:, :, :, :], ALU.add))
            link(nc.vector.tensor_reduce(mask[:, :, :], cmp_[:, :, :, :], AX.X, ALU.add))
            nc.vector.tensor_scalar(mask[:, :, :], mask[:, :, :], 1.5, None, ALU.is_lt).then_inc(mask_ready, 1)
            for b in range(TB):
                ins = nc.vector.tensor_scalar(lg[:, b, :], lg[:, b, :], top[:, b, 0:1], None, ALU.subtract)
                ins.then_inc(chain, 1) if b == 0 else ins.then_inc(top_ready, 1)
            links[0] += 1
            dve.wait_ge(mask_ready, 1)
            dve.wait_ge(share_exp, 1)
            link(nc.vector.tensor_tensor(lg[:, :, :], lg[:, :, :], mask[:, :, :], ALU.mult))
            link(nc.vector.tensor_reduce(wsum[:, :, 0:1], lg[:, :, :], AX.X, ALU.add))
            link(nc.vector.reciprocal(wsum[:, :, 1:2], wsum[:, :, 0:1]))
            for b in range(TB):
                link(nc.vector.tensor_scalar(share[:, b, 1:EXPERTS + 1], lg[:, b, :], wsum[:, b, 1:2], None,
                                             ALU.mult))
            dve.wait_ge(rank_full, 1)
            ranks = slot[:, :, 1:EXPERTS + 1]
            link(nc.vector.tensor_scalar(ranks, mid[:, :, 0:EXPERTS], 1.0, None, ALU.add))
            link(nc.vector.tensor_tensor(ranks, ranks, mask[:, :, :], ALU.mult))
            link(nc.vector.tensor_scalar(ranks, ranks, -1.0, None, ALU.add))
            link(nc.vector.tensor_reduce(most[:, 0:1], bank[0][:, 0:EXPERTS], AX.X, ALU.max))
            nc.vector.tensor_copy(most_i[:, 0:1], most[:, 0:1]).then_inc(route_ready, 1)
            for b in range(TB):
                dve.wait_ge(xn_lo_ready, b + 1)

            def select(col):
                for b in range(TB):
                    nc.vector.tensor_scalar(sel[:, b, :], iota, slot[:, b, col], None,
                                            ALU.is_equal).then_inc(sel_ready, 1)

            def experts(pas):
                g0 = pas * (EXPERTS + 1)
                t0 = T0 + pas * (2 + EXPERTS * E_TURNS + 4)
                h0 = H0 + pas * EXPERTS * E_HALVES
                s0 = pas * EXPERTS * ESTEPS

                def gather_lo(first, j, n):
                    dve.wait_ge(g_hi_ready, n)
                    nc.vector.tensor_tensor(g_lo[:, 4 * j:4 * j + 4, :],
                                            turn[(first + j) % 2][:, :].rearrange("p (k t) -> p k t", k=4),
                                            g_hi[:, 4 * j:4 * j + 4, :].bitcast(F32),
                                            ALU.subtract).then_inc(turn_free[(first + j) % 2], 1)

                def output_lo(n, e):
                    dve.wait_ge(y_hi_ready, 2 * g0 + n + 1 + e * 2)
                    nc.vector.tensor_tensor(y_lo[:, xslice(n)], mid[:, n, :], y_hi[:, xslice(n)].bitcast(F32),
                                            ALU.subtract).then_inc(y_ready, 1)

                def add_output(first, i, e, col):
                    b, n = i // 2, i % 2
                    idx = first + i
                    dve.wait_ge(turned, idx + 1 + e * E_TURNS)
                    xs = x[:, b, xslice(n)]
                    nc.vector.scalar_tensor_tensor(out=xs, in0=turn[idx % 2][:, :], scalar=share[:, b, col],
                                                   in1=xs, op0=ALU.mult,
                                                   op1=ALU.add).then_inc(turn_free[idx % 2], 1)

                select(slice(1, 2))
                for j in range(2):
                    gather_lo(t0, j, 2 * g0 + j + 1)
                tl = t0 + 2
                with dve.Fori(0, EXPERTS) as e:
                    for i in range(E_HALVES):
                        split_lo(dve, h0 + i, e)
                        for n in range(2):
                            if i == 1 + n:
                                output_lo(n, e)
                        for m, at_ in enumerate(AT_COMBINE):
                            if i == at_ + 1:
                                add_output(tl + U_COMB, m, e, bass.ds(e, 1))
                        if i == AT_SLOT + 1:
                            idx = tl + U_SLOT
                            dve.wait_ge(turned, idx + 1 + e * E_TURNS)
                            nc.vector.tensor_copy(selT[:, :], turn[idx % 2][:, 0:T]
                                                  ).then_inc(turn_free[idx % 2], 1)
                        if i == E_AT["down", 0]:
                            select(bass.ds(e + 2, 1))
                        for c in range(ESTEPS):
                            if i == E_AT["up", c] + 5:
                                dve.wait_ge(e_silu, s0 + c + 1 + e * ESTEPS)
                                dve.wait_ge(used, h0 + E_AT["up", c] + 4 + e * E_HALVES)
                                nc.vector.tensor_tensor(eh[c % 2][:, :], bank[2 * (c % 2) + 1][:, :],
                                                        eh[c % 2][:, :], ALU.mult).then_inc(e_hid, 1)
                            if i == AT_HID[c] + 1:
                                idx = tl + U_HID + c
                                dve.wait_ge(eT_hi_ready, s0 + c + 1 + e * ESTEPS)
                                nc.vector.tensor_tensor(eT_lo[c % 2][:, :, :],
                                                        turn[idx % 2][:, :].rearrange("p (k t) -> p k t", k=4),
                                                        eT_hi[c % 2][:, :, :].bitcast(F32),
                                                        ALU.subtract).then_inc(turn_free[idx % 2], 1)
                        for j in range(2):
                            if i == AT_GATHER[j] + 1:
                                gather_lo(tl + U_GATH, j, 2 * (g0 + 1) + j + 1 + e * 2)
                for n in range(2):
                    output_lo(n, EXPERTS)
                for m in range(4):
                    add_output(tl + EXPERTS * E_TURNS, m, 0, slice(EXPERTS, EXPERTS + 1))
                for m in range(2, 4):
                    bank_read(dve, tl + EXPERTS * E_TURNS + m)

            experts(0)
            n = dve.value_load(most_i[0:1, 0:1], min_val=0, max_val=T)
            with dve.If(n > NPASS_TOKENS):
                nc.vector.tensor_scalar(slot[:, :, :], slot[:, :, :], -float(NPASS_TOKENS), None,
                                        ALU.add).then_inc(zeroed, 1)
                dve.wait_ge(zeroed, 1)
                experts(1)
            nc.vector.tensor_copy(most[:, 1:2], most[:, 0:1]).then_inc(x_final, 1)
            norm(2 * DEPTH, final=True)


def pack_cols(w, kt, cols):
    return w.reshape(kt, P, cols).transpose(1, 0, 2)


def part_of(w, kind, i):
    kt = {"n": 4, "h": 8, "w": 2}[kind]
    return pack_cols(w[i * kt * P:(i + 1) * kt * P], kt, w.shape[1]).reshape(P, PART)


def weight_stream(inp):
    out = np.empty((TOTAL_PARTS, P, PART), np.float32)
    n = 0

    def put(*part):
        nonlocal n
        out[n] = part_of(*part)
        n += 1

    g0 = 2 * D + 3 * VW
    for L in range(DEPTH):
        w_in = inp["w_in"][L]
        for (what, i), kind, part in MIXER:
            c = i * CB
            if what == "x":
                w = w_in[:, c:c + CB]
            elif what == "y":
                w = w_in[:, D + c:D + c + CB]
            elif what == "qkv":
                w = w_in[:, 2 * D + c:2 * D + min(c + CB, 3 * VW)]
            elif what == "g0":
                w = w_in[:, g0 + c:g0 + c + CB]
            elif what == "g1":
                w = w_in[:, g0 + D + c:g0 + D + c + CB]
            elif what == "lru":
                w = inp["w_proj_lru"][L][:, c:c + CB]
            elif what == "att":
                w = inp["w_proj_att"][L]
            else:
                w = inp["w_out"][L][:, c:c + CB]
            put(w, kind, part)
        if L == 0:
            for name, kind, part in dense_order():
                f = name[1] * CB
                if name[0] == "down":
                    w = inp["w_dense_down"][0][f:f + CB]
                    if kind == "n":
                        w = w[:, name[2] * CB:(name[2] + 1) * CB]
                else:
                    w = inp["w_dense_" + name[0]][0][:, f:f + CB]
                put(w, kind, part)
    for e in range(EXPERTS):
        for what, c in expert_order():
            f = c * CB
            for part in range(2):
                if what == "down":
                    put(inp["w_exp_down"][0, e][f:f + CB], "w", part)
                else:
                    put(inp["w_exp_" + what][0, e][:, f:f + CB], "n", part)
    assert n == TOTAL_PARTS
    return out


def constants():
    c = np.zeros((P, C_END), np.float32)
    i = np.arange(P)
    c[:, C_ID:C_ID + P] = np.eye(P)
    c[:, C_IOTA:C_IOTA + P] = i[None, :]
    c[:, C_BEFORE:C_BEFORE + P] = i[:, None] < i[None, :]
    c[:, C_ONES:C_ONES + P] = 1
    k = np.arange(T)
    for b in range(TB):
        rel = (b * P + i)[:, None] - k[None, :]
        for g in range(GROUPS):
            ok = (rel % DILATIONS[g] == 0) & (np.abs(rel) <= WINDOWS[g] // 2)
            o = C_MASK + (b * GROUPS + g) * T
            c[:, o:o + T] = np.where(ok, 0, NEG)
        freq = (np.float32(500000.0) ** (-np.arange(0, 16, 2, dtype=np.float32) / np.float32(16))).astype(np.float32)
        ang = (b * P + i)[:, None].astype(np.float32) * freq[None, :]
        c[:, C_COS + 8 * b:C_COS + 8 * b + 8] = np.cos(ang)
        c[:, C_SIN + 8 * b:C_SIN + 8 * b + 8] = np.sin(ang)
    e = np.arange(EXPERTS)
    c[:, C_LOW:C_END] = (e[None, :] < e[:, None]).astype(np.float32).reshape(1, -1)
    return c


def by_channel(a):
    a = a.reshape(a.shape[:-1] + (a.shape[-1] // P, P))
    return np.moveaxis(a, -1, 0).reshape(P, -1)


def kernel(**inputs):
    import concourse.bacc as bacc
    from concourse.bass_utils import run_bass_kernel_spmd

    inp = {k: np.asarray(a) for k, a in inputs.items()}
    router = inp["w_router"][0].reshape(KT, P, EXPERTS).transpose(1, 0, 2).reshape(P, -1)
    vecs = np.concatenate([by_channel(inp["conv_w"]), by_channel(inp["conv_b"]), by_channel(inp["b_rgate"]),
                           by_channel(inp["b_igate"]), by_channel(inp["lru_lambda"]), router], axis=1)
    gates = np.stack([inp["w_rgate"], inp["w_igate"]], axis=2)
    gates = gates.transpose(0, 4, 1, 2, 3, 5).reshape(DEPTH, P, -1)
    norms = np.stack([inp["norm_mix_g"][0], inp["norm_ffn_g"][0], inp["norm_mix_g"][1],
                      inp["norm_ffn_g"][1], inp["final_norm_g"]])
    arrays = {
        "stream": weight_stream(inp), "gates": np.ascontiguousarray(gates),
        "x": inp["x"].reshape(T, D), "norms": norms, "consts": constants(),
        "vecs": np.ascontiguousarray(vecs),
    }
    nc = bacc.Bacc("TRN2", target_bir_lowering=False, num_devices=1)
    aps = [nc.dram_tensor(f"in_{k}", a.shape, mybir.dt.from_np(a.dtype), kind="ExternalInput").ap()
           for k, a in arrays.items()]
    out = nc.dram_tensor("out_x", (T, D), F32, kind="ExternalOutput").ap()
    build(nc, *aps, out)
    r = run_bass_kernel_spmd(nc, [{f"in_{k}": a for k, a in arrays.items()}], core_ids=[0])
    return r.results[0]["out_x"].reshape(1, T, D)
```

```python
from contextlib import ExitStack

import numpy as np
import concourse.bass as bass
from concourse import mybir

F32 = mybir.dt.float32
F32R = mybir.dt.float32r
I32 = mybir.dt.int32
ALU = mybir.AluOpType
ACT = mybir.ActivationFunctionType
AX = mybir.AxisListType

P = 128
D = 1024
KT = D // P
T = 256
TB = T // P
DEPTH = 2
CB = 512
HEADS, SLOTS, GROUPS, DH = 12, 4, 3, 64
QK = 2 * HEADS * DH
VW = HEADS * DH
WINDOWS, DILATIONS = (128, 512, 2048), (1, 4, 16)
UNITS = TB * SLOTS
F_DENSE, F_EXP, EXPERTS = 2816, 3584, 8
EPS = 1e-6
SCALE = DH ** -0.5
NEG = -1e30

PART = 2048
HALF = PART // 2
R = 6
H = 4
LAG = 3
SPARE = (LAG + 1) // 2

MIXER = ([(("x", n), "n", i) for i in range(2) for n in range(2)]
         + [(("qkv", n), "n", i) for n in range(4) for i in range(2)] + [(("qkv", 4), "h", 0)]
         + [((w, n), "n", i) for w in ("y", "g1", "g0") for n in range(2) for i in range(2)]
         + [(("lru", 0), "n", i) for i in range(2)] + [(("att", 0), "w", 0)]
         + [(("lru", 1), "n", i) for i in range(2)]
         + [(("out", n), "n", i) for n in range(2) for i in range(2)])
DSTEPS = F_DENSE // CB
ESTEPS = F_EXP // CB
E_PARTS = 6 * ESTEPS
NPASS_TOKENS = P


def dense_order():
    out = []
    for c in range(DSTEPS + 1):
        kind, parts = ("n", 2) if c < DSTEPS else ("h", 1)
        step = [((w, c), kind, i) for w in ("gate", "up") for i in range(parts)]
        out += sorted(step, key=lambda part: part[2]) if c == 0 else step
        if c:
            out += [(("down", c - 1, n), "n", 0) for n in range(2)]
    return out[:-1] + [(("down", DSTEPS, 0), "s", 0)] + out[-1:]


def expert_order():
    out = []
    for c in range(ESTEPS):
        out += [("gate", c), ("up", c)]
        if 0 < c < ESTEPS - 2:
            out += [("down", c - 1)]
    return out + [("down", c) for c in range(ESTEPS - 3, ESTEPS)]


def schedule():
    steps = []

    def norm_half(k, n):
        steps.extend([("xg", k, n), ("sq", k, n)])

    norm_half(0, 0)
    steps.append(("tn", 0, 0))
    norm_half(0, 1)
    for L in range(DEPTH):
        side = {}

        def at(gap, *what):
            side.setdefault(gap, []).extend(what)

        if L == 0:
            for i in range(4):
                at(1 + i / 2, ("rate", i))
        at(3, ("evac", ("x", 0)))
        at(4, ("tx", 0), ("evac", ("x", 1)), ("conv", 0))
        at(5, ("tx", 1), ("lg", 0, 0), ("conv", 1))
        at(6, ("evac", ("qkv", 0)), ("conv", 2), ("lg", 0, 1))
        at(7, ("conv", 3), ("lg", 0, 2))
        at(8, ("evac", ("qkv", 1)), ("lg", 0, 3))
        at(10, ("evac", ("qkv", 2)), ("rope",))
        at(12, ("evac", ("qkv", 3)), ("lg", 1, 0))
        at(13, ("evac", ("qkv", 4)), ("lg", 1, 1))
        at(14, ("lg", 1, 2))
        at(14.5, ("lg", 1, 3))
        at(15, ("evac", ("y", 0)))
        at(17, ("evac", ("y", 1)))
        for (d, hf), (tanh, decay, root, scan) in zip(
                ((0, 0), (0, 1), (1, 0), (1, 1)),
                ((8, 8.5, 9.5, 10), (10.5, 11, 12, 12.5), (13.5, 14, 15, 15.5), (16.5, 17, 17.5, 18))):
            at(tanh, ("la", d, hf))
            at(decay, ("le", d, hf))
            at(root, ("lb", d, hf))
            at(scan, ("ls", d, hf))
        at(16, ("ty", 0))
        at(18, ("ty", 1))
        at(19, ("tq", 0), ("tq", 1))
        at(19.5, ("tq", 2), ("tq", 3))
        at(20, ("tq", 4), ("tq", 5), ("evac", ("g1", 0)))
        for i in range(UNITS + 3):
            stages = [("ap", i - 2), ("as", i), ("av", i - 3), ("aq", i - 2), ("am", i)]
            at(20.5 + i / 2, *(s for s in stages if 0 <= s[1] < UNITS))
        at(21, ("evac", ("g1", 1)), ("lf", 0))
        at(22, ("lf", 1))
        at(23, ("evac", ("g0", 0)), ("lf", 2))
        at(24, ("lf", 3))
        at(25, ("evac", ("g0", 1)))
        for gap, gate in ((24.5, ("g1", 0)), (25, ("g1", 1)), (25.5, ("g0", 0)), (26, ("g0", 1))):
            at(gap, ("sg", gate))
        at(26.5, ("ta",))
        at(27, ("evac", ("lru", 0)))
        at(28, ("ga", 0), ("merge", 0))
        at(29, ("tm", 0), ("ga", 1))
        at(30, ("evac", ("lru", 1)), ("merge", 1))
        at(30.5, ("tm", 1))
        at(32, ("evac", ("out", 0)))
        at(34, ("evac", ("out", 1)))
        for g, (name, _, i) in enumerate(MIXER):
            for hh in range(2):
                steps.append(("G", (L, name), i, hh))
                if (g, hh) == (0, 1):
                    steps += [("tn", 2 * L, 1), ("rs", 2 * L)]
                steps += [(s[0], L) + s[1:] for s in side.get(g + (hh + 1) / 2, [])]
            if name == ("out", 0) and i == 1:
                norm_half(2 * L + 1, 0)
            elif name == ("out", 1):
                if i == 0:
                    steps.append(("tn", 2 * L + 1, 0))
                else:
                    norm_half(2 * L + 1, 1)
                if L == DEPTH - 1 and i == 0:
                    steps.append(("router",))
        if L == 0:
            order = dense_order()
            for j, (name, kind, i) in enumerate(order):
                steps.append(("G", (L, name), i, 0))
                if j == len(order) - 1:
                    steps += [("tn", 2, 0), ("evac", L, ("down", DSTEPS, 0, 1))]
                if name == ("down", DSTEPS - 1, 0):
                    steps.append(("th", L, DSTEPS))
                steps.append(("G", (L, name), i, 1))
                if j == 0:
                    steps += [("tn", 1, 1), ("rs", 1)]
                ended = kind != "n" or name[0] == "down" or i == 1
                if ended:
                    steps.append(("evac", L, name))
                if name[0] == "down" and name[1] == DSTEPS:
                    norm_half(2, 0)
                elif j == len(order) - 1:
                    norm_half(2, 1)
                if ended and name[0] == "gate" and name[1]:
                    steps.append(("th", L, name[1] - 1))
    return steps + [("tn", 2 * DEPTH - 1, 1), ("rs", 2 * DEPTH - 1)]


STEPS = schedule()


def tables():
    half_at, last_half, pair, freed, kinds = {}, {}, {}, {}, {}
    uses, ring = [0, 0, 0], {2: 0, 3: 1}
    todo = []
    for L in range(DEPTH):
        todo += [((L, n), k, i, 2) for n, k, i in MIXER]
        if L == 0:
            todo += [((L, n), k, i, 3) for n, k, i in dense_order()]
    for j, (key, kind, i, width) in enumerate(todo):
        half_at[key, i], last_half[key] = 2 * j, 2 * j + 2
        if key not in kinds:
            kinds[key] = kind
            pair[key], freed[key] = [], []
            for _ in range(2 if kind in "ws" else 1):
                if key[1][0] == "lru":
                    p = 2
                else:
                    p = ring[width] % width
                    ring[width] += 1
                pair[key].append(p)
                freed[key].append(uses[p])
                uses[p] += TB
    turn, n = {}, 0
    count = {"tn": 2, "tx": 2, "ty": 2, "tq": 1, "ap": 1, "aq": 1, "av": 1, "ta": 1, "tm": 2, "th": 2}
    for s in STEPS:
        if s[0] in count:
            turn[s] = n
            n += count[s[0]]
    return half_at, last_half, pair, freed, kinds, turn, n, 2 * len(todo)


HALF_AT, LAST_HALF, PAIR, FREED, KIND, TURN, N_TURN, N_HALF = tables()
STATIC_PARTS = N_HALF // 2
TOTAL_PARTS = STATIC_PARTS + EXPERTS * E_PARTS
assert E_PARTS % R == 0 and (2 * E_PARTS) % H == 0

C_ID, C_IOTA, C_BEFORE, C_ONES = 0, P, 2 * P, 3 * P
C_MASK = 4 * P
C_COS = C_MASK + TB * GROUPS * T
C_SIN = C_COS + TB * 8
C_LOW = C_SIN + TB * 8
C_END = C_LOW + EXPERTS * EXPERTS
V_CONVW = 0
V_CONVB = V_CONVW + DEPTH * 4 * KT
V_BR = V_CONVB + DEPTH * KT
V_BI = V_BR + DEPTH * 2 * KT
V_LAM = V_BI + DEPTH * 2 * KT
V_ROUTER = V_LAM + DEPTH * 2 * KT
V_END = V_ROUTER + KT * EXPERTS

E_AT = {key: 4 * i for i, key in enumerate(expert_order())}
E_HALVES = 2 * E_PARTS
AT_COMBINE = [E_AT["up", 0] + 2 + 4 * i for i in range(4)]
AT_SLOT = E_AT["down", 0] + 6
AT_SELECT = AT_SLOT + 2
AT_HID = [E_AT["up", c + 1] for c in range(ESTEPS - 2)] + [E_AT["down", c] for c in
                                                          range(ESTEPS - 3, ESTEPS - 1)]
AT_GATHER = [E_AT["down", ESTEPS - 2] + 2 + j for j in range(2)]
E_USE = {what: n for n, (_, what) in enumerate(sorted(
    [(h, ("combine", i)) for i, h in enumerate(AT_COMBINE)] + [(AT_SLOT, ("slot", 0))]
    + [(h, ("hid", c)) for c, h in enumerate(AT_HID)] + [(h, ("gather", j)) for j, h in enumerate(AT_GATHER)]))}
E_TURNS = len(E_USE)
assert E_TURNS % 2 == 0


def build(nc, stream, gates_w, x_in, norms, consts_in, vecs_in, out):
    with ExitStack() as ctx:
        def keep(name, shape, dt=F32, into=ctx):
            return into.enter_context(nc.sbuf_tensor(name, shape, dt))

        def sem(name):
            return ctx.enter_context(nc.semaphore(name))

        raw = keep("raw", [P, R, PART])
        w_hi = keep("w_hi", [P, H, HALF], F32R)
        w_lo = keep("w_lo", [P, H, HALF], F32R)
        x = keep("x", [P, TB, D])
        a_hi = keep("a_hi", [P, KT, T], F32R)
        a_lo = keep("a_lo", [P, KT, T], F32R)
        xn = keep("xn", [P, TB, D])
        gain = keep("gain", [P, D])
        const = keep("const", [P, C_END])
        vec = keep("vec", [P, V_END])
        NC = DEPTH * 2 * KT
        rate = keep("rate", [P, 3, NC])
        small = keep("small", [P, 64])
        with ExitStack() as m:
            wg = keep("wg", [P, 2, 2, KT, P], into=m)
        with ExitStack() as m:
            sm = keep("sm", [P, 2, GROUPS * T], into=m)
            pt = [keep("pt0", [P, 2 * GROUPS, P], into=m)]
            att = keep("att", [P, TB, T], into=m)
            with ExitStack() as m2:
                pt.append(keep("pt1", [P, 2 * GROUPS, P], into=m2))
            att_hi = keep("att_hi", [P, 2, T], F32R, m)
            att_lo = keep("att_lo", [P, 2, T], F32R, m)
        keep("wg_place", [P, 4 * KT * P])
        arena = ExitStack()
        with arena:
            qk = keep("qk", [P, TB, QK], into=arena)
            v = keep("v", [P, TB, VW], into=arena)
            gy = keep("gy", [P, KT, T], into=arena)
            with ExitStack() as m:
                rg = keep("rg", [P, KT, T], into=m)
                ig = keep("ig", [P, KT, T], into=m)
                root = keep("root", [P, 4, T], into=m)
            with ExitStack() as m:
                qkT = keep("qkT", [P, HEADS // 2, 2, T], into=m)
                sg0 = keep("sg0", [P, TB, D], into=m)
            keep("u_place", [P, 2 * KT * T + 4 * T], into=arena)
            with ExitStack() as m:
                xT = keep("xT", [P, KT, T + 3], into=m)
                xc = keep("xc", [P, KT, T], into=m)
            with ExitStack() as m:
                lru_lo = keep("lru_lo", [P, KT, T], F32R, m)
                keep("gap", [P, KT * 3], into=m)
                lru_hi = keep("lru_hi", [P, KT, T], F32R, m)
        with ExitStack() as m:
            hid = [keep(f"hid{i}", [P, TB, CB], into=m) for i in range(2)]
            hT_hi = [keep(f"hT_hi{i}", [P, 4, T], F32R, m) for i in range(2)]
            hT_lo = [keep(f"hT_lo{i}", [P, 4, T], F32R, m) for i in range(2)]
        with ExitStack() as m:
            xn_hi = keep("xn_hi", [P, TB, D], F32R, m)
            xn_lo = keep("xn_lo", [P, TB, D], F32R, m)
            g_hi = keep("g_hi", [P, KT, P], F32R, m)
            g_lo = keep("g_lo", [P, KT, P], F32R, m)
            eh = [keep(f"eh{i}", [P, CB], into=m) for i in range(2)]
            eT_hi = [keep(f"eT_hi{i}", [P, 4, P], F32R, m) for i in range(2)]
            eT_lo = [keep(f"eT_lo{i}", [P, 4, P], F32R, m) for i in range(2)]
            y_hi = keep("y_hi", [P, D], F32R, m)
            y_lo = keep("y_lo", [P, D], F32R, m)
            sel = keep("sel", [P, TB, P], F32R, m)
            selT = keep("selT", [P, T], F32R, m)
            rw = keep("rw", [P, 2, KT * EXPERTS], F32R, m)
            lg = keep("lg", [P, TB, EXPERTS], into=m)
            lgT = keep("lgT", [EXPERTS, T], into=m)
            cmp_ = keep("cmp", [P, TB, EXPERTS, EXPERTS], into=m)
            cmp2 = keep("cmp2", [P, TB, EXPERTS, EXPERTS], into=m)
            mask = keep("mask", [P, TB, EXPERTS], into=m)
            top = keep("top", [P, TB, 8], into=m)
            wsum = keep("wsum", [P, TB, 4], into=m)
            slot = keep("slot", [P, TB, EXPERTS + 2], into=m)
            share = keep("share", [P, TB, EXPERTS + 2], into=m)
            most = keep("most", [P, 2], into=m)
            most_i = keep("most_i", [P, 2], I32, m)

        bank = [ctx.enter_context(nc.psum_tensor(f"bank{i}", [P, CB], F32)) for i in range(4)]
        mid = ctx.enter_context(nc.psum_tensor("mid", [P, 2, CB], F32))
        turn = [ctx.enter_context(nc.psum_tensor(f"turn{i}", [P, CB], F32)) for i in range(2)]

        def acc(p, b):
            return mid[:, b, :] if p == 2 else bank[2 * p + b][:, :]

        ident = const[:, C_ID:C_ID + P]
        iota = const[:, C_IOTA:C_IOTA + P]
        before = const[:, C_BEFORE:C_BEFORE + P]
        ones = const[:, C_ONES:C_ONES + P]
        band = const[:, C_MASK:C_COS].rearrange("p (b k) -> p b k", b=TB)
        cos = const[:, C_COS:C_SIN].rearrange("p (b k) -> p b k", b=TB)
        sin = const[:, C_SIN:C_LOW].rearrange("p (b k) -> p b k", b=TB)
        lower = const[:, C_LOW:C_END].rearrange("p (a b) -> p a b", a=EXPERTS)
        convw = vec[:, V_CONVW:V_CONVB].rearrange("p (l j n) -> p l j n", l=DEPTH, j=4)
        convb = vec[:, V_CONVB:V_BR].rearrange("p (l n) -> p l n", l=DEPTH)
        b_r = vec[:, V_BR:V_BI].rearrange("p (l d n) -> p l d n", l=DEPTH, d=2)
        b_i = vec[:, V_BI:V_LAM].rearrange("p (l d n) -> p l d n", l=DEPTH, d=2)
        lam = vec[:, V_LAM:V_ROUTER]
        router = vec[:, V_ROUTER:V_END]
        ms, sd, rstd = (small[:, 2 * i:2 * i + 2] for i in range(3))
        mx, nm, rs, rr = (small[:, 8 + 2 * i:10 + 2 * i] for i in range(4))
        ss = small[:, 16:20].rearrange("p (n b) -> p n b", n=2)

        idle = small[:, 20:21]

        s_id = sem("identity_landed")
        s_const = sem("consts_landed")
        s_vec = sem("channel_parameters_landed")
        s_x = [sem(f"x_half_landed{n}") for n in range(2)]
        s_gain0 = [sem(f"first_gain_half_landed{n}") for n in range(2)]
        first_landed = sem("first_half_landed")
        s_gain = sem("gain_landed")
        s_wg = sem("gate_weights_landed")
        landed = [sem(f"part_landed{i}") for i in range(R)]
        hi_ready = sem("hi_ready")
        lo_ready = sem("lo_ready")
        used = sem("halves_used")
        pair_free = [sem(f"pair_free{i}") for i in range(3)]
        turned = sem("turned")
        turn_hi = sem("turn_hi")
        turn_free = [sem(f"turn_free{i}") for i in range(2)]
        chain = sem("vector_chain")
        rate_s = sem("rate_exp")
        rate_ready = sem("rate_ready")
        sq_sum = sem("squares_summed")
        ms_ready = sem("mean_square_ready")
        sd_ready = sem("deviation_ready")
        rstd_ready = sem("inverse_deviation_ready")
        xn_ready = sem("xn_ready")
        xc_ready = sem("xc_ready")
        mid_full = sem("mid_full")
        mid_free = sem("mid_free")
        tanh_ready = sem("tanh_ready")
        decay_ready = sem("decay_ready")
        ix_ready = sem("gated_input_ready")
        sq_ready = sem("root_ready")
        scanned = sem("scanned")
        rope_s = sem("rope_parts")
        rope_done = sem("rope_done")
        gelu_ready = sem("gelu_ready")
        lru_full = sem("lru_full")
        lru_hi_ready = sem("lru_hi_ready")
        lru_ready = sem("lru_ready")
        nm_ready = sem("neg_max_ready")
        p_ready = sem("probs_ready")
        gate_ready = sem("branch_gate_ready")
        merged = sem("merged")
        silu_ready = sem("silu_ready")
        xn_hi_ready = sem("xn_hi_ready")
        xn_lo_ready = sem("xn_lo_ready")
        rw_ready = sem("router_weights_ready")
        logit_full = sem("logits_full")
        logit_rows = sem("logit_rows")
        top_ready = sem("top_ready")
        share_exp = sem("share_exp")
        mask_ready = sem("mask_ready")
        rank_full = sem("rank_full")
        route_ready = sem("route_ready")
        sel_ready = sem("sel_ready")
        g_hi_ready = sem("gathered_hi")
        e_silu = sem("expert_silu")
        e_hid = sem("expert_hidden")
        eT_hi_ready = sem("expert_hidden_hi")
        y_hi_ready = sem("y_hi_ready")
        y_ready = sem("y_ready")
        zeroed = sem("zeroed")
        out_sem = sem("out_landed")
        final_sum = sem("final_squares_summed")
        idle_s = sem("root_table_fetched")
        done = sem("final_ready")

        def product_done(eng, key):
            eng.wait_ge(used, LAST_HALF[key])

        def bank_full(eng, idx):
            eng.wait_ge(turned, idx + 1)

        def bank_read(eng, idx):
            eng.wait_ge(turn_free[idx % 2], idx // 2 + 1)

        def split_hi(act, h, e=0):
            part = h // 2
            if h == 0:
                act.wait_ge(first_landed, 16)
            elif h % 2 == 0 or h == 1:
                act.wait_ge(landed[part % R], 16 * (part // R + 1) + e * (16 * E_PARTS // R))
            if h >= H:
                act.wait_ge(used, h - H + 1 + e * 2 * E_PARTS)
            lo = (h % 2) * HALF
            nc.scalar.activation(w_hi[:, h % H, :], raw[:, part % R, lo:lo + HALF],
                                 ACT.Copy).then_inc(hi_ready, 1)

        def split_lo(dve, h, e=0):
            part = h // 2
            lo = (h % 2) * HALF
            dve.wait_ge(hi_ready, h + 1 + e * 2 * E_PARTS)
            nc.vector.tensor_tensor(w_lo[:, h % H, :], raw[:, part % R, lo:lo + HALF],
                                    w_hi[:, h % H, :].bitcast(F32), ALU.subtract).then_inc(lo_ready, 1)

        def mm3(out_, s_hi, s_lo, wh, wl, start, stop):
            nc.tensor.matmul(out_, s_hi, wh, start=start, stop=False)
            nc.tensor.matmul(out_, s_hi, wl, start=False, stop=False)
            return nc.tensor.matmul(out_, s_lo, wh, start=False, stop=stop)

        def half_of(key, part):
            return HALF_AT[key, part]

        def scans_done(L, d, hf):
            return (L * 2 + d) * KT + 4 * (hf + 1)

        def evac_value(key, n=0):
            return FREED[key][n] + TB

        def evacuated(eng, key, n=0):
            eng.wait_ge(pair_free[PAIR[key][n]], evac_value(key, n))

        def mid_before(L, use):
            lru = min(use, 8)
            at_ = use - lru
            return L * 16 + use, L * (8 * 4 + 8) + 4 * lru + at_

        def xslice(n):
            return slice(n * CB, (n + 1) * CB)

        def x_done(eng, k, n, b):
            L = (k - 1) // 2
            if k == 0:
                eng.wait_ge(s_x[n], 16)
                return
            if k % 2:
                key = (L, ("out", n))
            else:
                key = (L, ("down", DSTEPS, 0) if n == 0 else ("down", DSTEPS - 1, 1))
            eng.wait_ge(pair_free[PAIR[key][0]], FREED[key][0] + b + 1)

        H0 = N_HALF
        T0 = N_TURN

        block = ctx.enter_context(nc.Block())

        @block.sync
        def _(sp):
            def load(slot_, part):
                sp.dma_start(raw[:, slot_, :], stream[part, :, :]).then_inc(landed[slot_], 16)

            def load_x(n):
                sp.dma_start(x[:, :, xslice(n)], x_in.rearrange("(b p) d -> p b d", p=P)[:, :, xslice(n)]
                             ).then_inc(s_x[n], 16)

            def load_first_gain(n):
                sp.dma_start(gain[:, xslice(n)], norms[0:1, xslice(n)].to_broadcast([P, CB])
                             ).then_inc(s_gain0[n], 16)

            load_x(0)
            load_first_gain(0)
            sp.dma_start(raw[:, 0, 0:HALF], stream[0, :, 0:HALF]).then_inc(first_landed, 16)
            sp.dma_start(raw[:, 0, HALF:PART], stream[0, :, HALF:PART]).then_inc(landed[0], 16)
            load_x(1)
            load_first_gain(1)
            for i in range(1, R):
                load(i, i)
            with sp.Fori(1, TOTAL_PARTS // R) as g:
                for i in range(R):
                    sp.wait_ge(lo_ready, 2 * R * g + 2 * (i + 1) - 2 * R)
                    load(i, g * R + i)
            for part in range(TOTAL_PARTS // R * R, TOTAL_PARTS + SPARE):
                sp.wait_ge(lo_ready, 2 * (part - R + 1))
                load(part % R, part)
            sp.wait_ge(route_ready, 1)
            n = sp.value_load(most_i[0:1, 0:1], min_val=0, max_val=T)
            with sp.If(n > NPASS_TOKENS):
                with sp.Fori(0, EXPERTS) as e:
                    for i in range(SPARE, E_PARTS + SPARE):
                        part = TOTAL_PARTS + i
                        sp.wait_ge(lo_ready, 2 * (part - R + 1) + e * 2 * E_PARTS)
                        load(part % R, STATIC_PARTS + e * E_PARTS + i)
            for n in range(2):
                for b in range(TB):
                    sp.wait_ge(done, 2 * n + b + 1)
                    sp.dma_start(out[b * P:(b + 1) * P, xslice(n)], xn[:, b, xslice(n)]).then_inc(out_sem, 16)
            sp.wait_ge(out_sem, 16 * 2 * TB)

        @block.gpsimd
        def _(pool):
            def load_gain(k):
                pool.dma_start(gain[:, :], norms[k:k + 1, :].to_broadcast([P, D])).then_inc(s_gain, 16)

            pool.wait_ge(s_x[1], 16)
            pool.dma_start(wg[:, :, :, :, :].rearrange("p a b n d -> p (a b n d)"),
                           gates_w[0, :, :]).then_inc(s_wg, 16)
            for s in STEPS:
                if s[0] == "xg" and s[2] == 1:
                    pool.wait_ge(xn_ready, 2 * TB * (s[1] + 1))
                    load_gain(s[1] + 1)
                elif s == ("evac", 0, ("out", 0)):
                    product_done(pool, (0, ("att", 0)))
                    pool.dma_start(wg[:, :, :, :, :].rearrange("p a b n d -> p (a b n d)"),
                                   gates_w[1, :, :]).then_inc(s_wg, 16)
                elif s[0] == "la":
                    _, L, d, hf = s
                    n = slice(4 * hf, 4 * hf + 4)
                    pool.wait_ge(mid_free, mid_before(L, d * 4 + 2 * hf + 1)[1] + 4)
                    nc.gpsimd.tensor_tensor(ig[:, n, :], ig[:, n, :], xc[:, n, :],
                                            ALU.mult).then_inc(ix_ready, 1)
                elif s[0] == "rope":
                    L = s[1]
                    for n in range(3):
                        evacuated(pool, (L, ("qkv", n)))
                    bank_read(pool, TURN[("tx", L, 1)] + 1)
                    bank_read(pool, TURN[("tx", L, 1)])
                    z = qk[:, :, :].rearrange("p b (h w) -> p b h w", w=DH)
                    NH = QK // DH
                    t1, t2 = z[:, :, :, 0:8], z[:, :, :, 8:16]
                    cb = cos.rearrange("p b (o k) -> p b o k", o=1).to_broadcast([P, TB, NH, 8])
                    sb_ = sin.rearrange("p b (o k) -> p b o k", o=1).to_broadcast([P, TB, NH, 8])
                    flat = xn[:, :, :].rearrange("p b w -> p (b w)")
                    W = TB * NH * 8
                    tmp = [flat[:, i * W:(i + 1) * W].rearrange("p (b h k) -> p b h k", b=TB, k=8)
                           for i in range(4)]
                    for o, (a, c) in zip(tmp, ((t1, cb), (t2, sb_), (t2, cb), (t1, sb_))):
                        nc.gpsimd.tensor_tensor(o, a, c, ALU.mult).then_inc(rope_s, 1)
                    pool.wait_ge(rope_s, 4 * (L + 1))
                    nc.gpsimd.tensor_tensor(t1, tmp[0], tmp[1], ALU.subtract).then_inc(rope_done, 1)
                    nc.gpsimd.tensor_tensor(t2, tmp[2], tmp[3], ALU.add).then_inc(rope_done, 1)
            pool.wait_ge(s_gain, 16 * 2 * DEPTH)

        @block.scalar
        def _(act):
            act.dma_start(const[:, 0:P], consts_in[:, 0:P]).then_inc(s_id, 16)
            act.dma_start(vec[:, :], vecs_in).then_inc(s_vec, 16)

            hi = [0]

            def turn_high(dst, src, idx):
                bank_full(act, idx)
                nc.scalar.activation(dst, src, ACT.Copy).then_inc(turn_hi, 1)
                hi[0] += 1

            ahead = [0]

            def split_half():
                split_hi(act, ahead[0])
                ahead[0] += 1

            def square(k, n, b, place, ready=sq_sum):
                if n == 0 and b == 0 and k:
                    act.wait_ge(ms_ready, k)
                nc.scalar.activation(place, x[:, b, xslice(n)], ACT.Square,
                                     accum_out=ss[:, n, b:b + 1]).then_inc(ready, 1)

            def deviation(k):
                act.wait_ge(ms_ready, k + 1)
                nc.scalar.activation(sd, ms, ACT.Sqrt).then_inc(sd_ready, 1)

            for s in STEPS:
                kind = s[0]
                if kind == "sq":
                    _, k, n = s
                    if (k, n) == (0, 1):
                        act.dma_start(const[:, P:C_END], consts_in[:, P:C_END]).then_inc(s_const, 16)
                    for b in range(TB):
                        x_done(act, k, n, b)
                        o = 4 * n + 2 * b
                        square(k, n, b, xc[:, o:o + 2, :].rearrange("p n t -> p (n t)"))
                    if k == 0:
                        for _ in range(1 + (LAG > 2) * n):
                            split_half()
                elif kind == "rs":
                    deviation(s[1])
                elif kind == "rate" and s[2] == 0:
                    act.wait_ge(rate_s, 1)
                    nc.scalar.activation(rate[:, 1, :], rate[:, 0, :], ACT.Exp).then_inc(rate_s, 1)
                elif kind == "tn":
                    j = s[2]
                    for b in range(TB):
                        idx = TURN[s] + b
                        turn_high(a_hi[:, 4 * j:4 * j + 4, b * P:(b + 1) * P],
                                  turn[idx % 2][:, :].rearrange("p (k t) -> p k t", k=4), idx)
                elif kind == "G":
                    split_half()
                elif kind == "evac":
                    L, name = s[1:]
                    key = (L, name)
                    what, n = name[0], name[1]
                    if what in ("lru", "out", "down"):
                        continue
                    p = PAIR[key][0]
                    if what in ("x", "y", "qkv"):
                        product_done(act, key)
                        act.wait_ge(rstd_ready, 2 * L + 1)
                        if what == "y" and n == 0:
                            act.wait_ge(rope_done, 2 * (L + 1))
                        w = CB
                        if what != "qkv":
                            dst = xn[:, 0, xslice(n)]
                        else:
                            w = CB if n < 4 else VW - CB
                            dst = qk[:, 0, xslice(n)] if n < 3 else v[:, 0, (n - 3) * CB:(n - 3) * CB + w]
                        nc.scalar.activation(dst, acc(p, 0)[:, 0:w], ACT.Copy,
                                             scale=rstd[:, 0:1]).then_inc(pair_free[p], 1)
                    elif what in ("g0", "g1"):
                        product_done(act, key)
                        if what == "g1":
                            bank_read(act, TURN[("tq", L, 4)])
                            bank_read(act, TURN[("tq", L, 5)])
                        else:
                            act.wait_ge(scanned, scans_done(L, 1, 1))
                        for b in range(TB):
                            dst = qk[:, b, xslice(n)] if what == "g1" else sg0[:, b, xslice(n)]
                            nc.scalar.activation(dst, acc(p, b), ACT.Copy,
                                                 scale=rstd[:, b:b + 1]).then_inc(pair_free[p], 1)
                    elif what == "gate":
                        product_done(act, key)
                        act.wait_ge(rstd_ready, 2)
                        w = CB if n < DSTEPS else 2 * P
                        if n >= 2:
                            bank_full(act, TURN[("th", 0, n - 2)] + 1)
                        for b in range(TB):
                            nc.scalar.activation(hid[n % 2][:, b, 0:w], acc(p, b)[:, 0:w],
                                                 ACT.Silu, scale=rstd[:, b:b + 1]
                                                 ).then_inc(pair_free[p], 1)
                elif kind == "sg":
                    _, L, (which, n) = s
                    evacuated(act, (L, (which, n)))
                    g = (qk if which == "g1" else sg0)[:, :, xslice(n)]
                    nc.scalar.activation(g, g, ACT.Sigmoid).then_inc(gate_ready, 1)
                elif kind == "ty":
                    _, L, c = s
                    for k in range(2):
                        idx = TURN[s] + k
                        n = 4 * c + 2 * k
                        bank_full(act, idx)
                        nc.scalar.activation(gy[:, n:n + 2, :],
                                             turn[idx % 2][:, :].rearrange("p (n t) -> p n t", n=2),
                                             ACT.Gelu_apprx_tanh).then_inc(turn_free[idx % 2], 1)
                elif kind == "lg":
                    _, L, d, pr = s
                    act.wait_ge(mid_full, mid_before(L, d * 4 + pr)[0] + 1)
                    if L or d:
                        act.wait_ge(scanned, scans_done(L, d - 1, pr // 2))
                    for q in range(2):
                        n = 2 * pr + q
                        for g, (dst, bias) in enumerate(((rg, b_r), (ig, b_i))):
                            nc.scalar.activation(dst[:, n, :], mid[:, q, g * T:(g + 1) * T], ACT.Sigmoid,
                                                 bias=bias[:, L, d, n:n + 1]).then_inc(mid_free, 1)
                elif kind == "la":
                    _, L, d, hf = s
                    k = (L * 2 + d) * 2 + hf
                    if k == 0:
                        act.wait_ge(rate_ready, 2)
                    else:
                        act.wait_ge(scanned, 4 * k)
                    act.wait_ge(mid_free, mid_before(L, d * 4 + 2 * hf + 1)[1] + 4)
                    for q in range(4):
                        n = 4 * hf + q
                        col = (L * 2 + d) * KT + n
                        nc.scalar.activation(root[:, q, :], rg[:, n, :], ACT.Tanh,
                                             scale=rate[:, 0, col:col + 1]).then_inc(tanh_ready, 1)
                elif kind == "router":
                    nc.scalar.activation(rw[:, 0, :], router, ACT.Copy).then_inc(rw_ready, 1)
                elif kind == "le":
                    _, L, d, hf = s
                    k = (L * 2 + d) * 2 + hf
                    act.wait_ge(tanh_ready, 4 * (k + 1))
                    for q in range(4):
                        n = 4 * hf + q
                        col = (L * 2 + d) * KT + n
                        nc.scalar.activation(rg[:, n, :], rg[:, n, :], ACT.Exp,
                                             scale=rate[:, 1, col:col + 1]).then_inc(decay_ready, 1)
                elif kind == "lb":
                    nc.scalar.activation(root[:, :, :], root[:, :, :], ACT.Sqrt).then_inc(sq_ready, 1)
                elif kind == "lf":
                    _, L, pr = s
                    act.wait_ge(lru_full, 4 * L + pr + 1)
                    nc.scalar.activation(lru_hi[:, 2 * pr:2 * pr + 2, :], gy[:, 2 * pr:2 * pr + 2, :],
                                         ACT.Copy).then_inc(lru_hi_ready, 1)
                elif kind == "tq" and s[2] % 2 == 0:
                    idx = TURN[s]
                    bank_full(act, idx)
                    act.wait_ge(scanned, scans_done(s[1], 1, 1))
                    nc.scalar.activation(qkT[:, s[2], :, :],
                                         turn[idx % 2][:, :].rearrange("p (a t) -> p a t", a=2),
                                         ACT.Copy).then_inc(turn_free[idx % 2], 1)
                elif kind == "am":
                    _, L, u = s
                    k = 8 * L + u
                    act.wait_ge(nm_ready, k + 1)
                    nc.scalar.activation(sm[:, u % 2, :], sm[:, u % 2, :], ACT.Exp,
                                         bias=nm[:, u % 2:u % 2 + 1], scale=SCALE,
                                         accum_out=rs[:, u % 2:u % 2 + 1]).then_inc(p_ready, 1)
                elif kind == "ap":
                    idx = TURN[s]
                    bank_full(act, idx)
                    nc.scalar.activation(pt[s[2] % 2][:, 0:4, :],
                                         turn[idx % 2][:, :].rearrange("p (a t) -> p a t", a=4),
                                         ACT.Copy).then_inc(turn_free[idx % 2], 1)
                elif kind == "ta":
                    turn_high(att_hi[:, :, :],
                              turn[TURN[s] % 2][:, :].rearrange("p (a t) -> p a t", a=2), TURN[s])
                elif kind == "tm":
                    j = s[2]
                    for b in range(TB):
                        idx = TURN[s] + b
                        turn_high(a_hi[:, 4 * j:4 * j + 4, b * P:(b + 1) * P],
                                  turn[idx % 2][:, :].rearrange("p (k t) -> p k t", k=4), idx)
                elif kind == "th":
                    c = s[2]
                    w = 4 if c < DSTEPS else 2
                    for b in range(TB):
                        idx = TURN[s] + b
                        if b == 0 and c >= 2:
                            product_done(act, (0, ("down", c - 2, 1)))
                        turn_high(hT_hi[c % 2][:, 0:w, b * P:(b + 1) * P],
                                  turn[idx % 2][:, 0:w * P].rearrange("p (k t) -> p k t", k=w), idx)

            act.wait_ge(rstd_ready, 2 * DEPTH)
            for b in range(TB):
                nc.scalar.activation(xn_hi[:, b, :], xn[:, b, :], ACT.Copy,
                                     scale=rstd[:, b:b + 1]).then_inc(xn_hi_ready, 1)
            act.wait_ge(top_ready, 1)
            nc.scalar.activation(lg[:, :, :], lg[:, :, :], ACT.Exp).then_inc(share_exp, 1)

            def experts(pas):
                t0 = T0 + pas * (2 + EXPERTS * E_TURNS + 4)
                h0 = H0 + pas * EXPERTS * E_HALVES

                def full(idx, e):
                    act.wait_ge(turned, idx + 1 + e * E_TURNS)

                def gather_hi(first, j, e):
                    full(first + j, e)
                    nc.scalar.activation(g_hi[:, 4 * j:4 * j + 4, :],
                                         turn[(first + j) % 2][:, :].rearrange("p (k t) -> p k t", k=4),
                                         ACT.Copy).then_inc(g_hi_ready, 1)

                def output_hi(n, e):
                    act.wait_ge(used, h0 + e * E_HALVES)
                    nc.scalar.activation(y_hi[:, xslice(n)], mid[:, n, :], ACT.Copy).then_inc(y_hi_ready, 1)

                for j in range(2):
                    gather_hi(t0, j, 0)
                tl = t0 + 2
                with act.Fori(0, EXPERTS) as e:
                    for i in range(E_HALVES):
                        split_hi(act, h0 + i + LAG, e)
                        for n in range(2):
                            if i == n:
                                output_hi(n, e)
                        for c in range(ESTEPS):
                            if i == AT_HID[c]:
                                idx = tl + E_USE["hid", c]
                                full(idx, e)
                                nc.scalar.activation(eT_hi[c % 2][:, :, :],
                                                     turn[idx % 2][:, :].rearrange("p (k t) -> p k t", k=4),
                                                     ACT.Copy).then_inc(eT_hi_ready, 1)
                            if i == E_AT["gate", c] + 4:
                                act.wait_ge(used, h0 + E_AT["gate", c] + 4 + e * E_HALVES)
                                nc.scalar.activation(eh[c % 2][:, :], bank[2 * (c % 2)][:, :],
                                                     ACT.Silu).then_inc(e_silu, 1)
                        for j in range(2):
                            if i == AT_GATHER[j]:
                                gather_hi(tl + E_USE["gather", 0], j, e)
                for n in range(2):
                    output_hi(n, EXPERTS)
                nc.scalar.activation(idle, ident[:, 0:1], ACT.Sqrt).then_inc(idle_s, 1)
                for i in range(4):
                    bank_read(act, tl + EXPERTS * E_TURNS + i)
                    square(2 * DEPTH, i % 2, i // 2, xn[:, i // 2, xslice(i % 2)], final_sum)

            experts(0)
            act.wait_ge(route_ready, 1)
            n = act.value_load(most_i[0:1, 0:1], min_val=0, max_val=T)
            with act.If(n > NPASS_TOKENS):
                experts(1)
            deviation(2 * DEPTH)

        @block.tensor
        def _(pe):
            def turn_bank(idx):
                if idx >= 2:
                    pe.wait_ge(turn_free[idx % 2], idx // 2)
                return turn[idx % 2]

            def gemm(key, part, hh, s_hi, s_lo):
                kind = KIND[key]
                kts, cols, width = {"n": (2, CB, 1), "h": (4, 2 * P, 1), "w": (1, CB, 2), "s": (2, CB, 2)}[kind]
                last_kt = (1 if (key, 1) not in HALF_AT else 2) * 2 * kts - 1
                if kind == "s":
                    last_kt = kts - 1
                if part == 0 and hh == 0:
                    for n in range(width):
                        if FREED[key][n]:
                            pe.wait_ge(pair_free[PAIR[key][n]], FREED[key][n])
                    if key[1] == ("lru", 0):
                        pe.wait_ge(mid_free, mid_before(key[0], 8 + UNITS)[1])
                h = half_of(key, part) + hh
                pe.wait_ge(lo_ready, h + 1)
                for k in range(kts):
                    kt = k if kind == "s" else (part * 2 + hh) * kts + k
                    for n in range(width) if kind != "s" else (hh,):
                        o = k * cols if kind == "s" else (k * width + n) * cols
                        wh = w_hi[:, h % H, o:o + cols]
                        wl = w_lo[:, h % H, o:o + cols]
                        for b in range(TB):
                            ins = mm3(acc(PAIR[key][n], b)[:, 0:cols],
                                      s_hi[:, kt, b * P:(b + 1) * P], s_lo[:, kt, b * P:(b + 1) * P],
                                      wh, wl, start=kt == 0, stop=kt == last_kt)
                ins.then_inc(used, 1)

            pe.wait_ge(s_id, 16)
            a_from = [None, None]
            for s in STEPS:
                kind = s[0]
                if kind == "tn":
                    _, k, j = s
                    for b in range(TB):
                        pe.wait_ge(xn_ready, 2 * TB * k + 2 * j + b + 1)
                        idx = TURN[s] + b
                        t_ = turn_bank(idx)
                        for q in range(4):
                            kt = 4 * j + q
                            ins = nc.tensor.transpose(t_[:, q * P:(q + 1) * P],
                                                      xn[:, b, kt * P:(kt + 1) * P], ident)
                        ins.then_inc(turned, 1)
                    a_from[j] = TURN[s]
                elif kind == "G":
                    key = s[1]
                    what = key[1][0]
                    if what == "lru":
                        if s[2:] == (0, 0) and key[1][1] == 0:
                            pe.wait_ge(lru_ready, 4 * (key[0] + 1))
                        gemm(key, *s[2:], lru_hi, lru_lo)
                    elif what == "att":
                        bank_read(pe, TURN[("ta", key[0])])
                        gemm(key, *s[2:], att_hi, att_lo)
                    elif what == "down":
                        for b in range(TB):
                            bank_read(pe, TURN[("th", 0, key[1][1])] + b)
                        gemm(key, *s[2:], hT_hi[key[1][1] % 2], hT_lo[key[1][1] % 2])
                    else:
                        halves = s[2:3] if KIND[key] == "n" else range(2)
                        for j in halves:
                            for b in range(TB):
                                bank_read(pe, a_from[j] + b)
                        gemm(key, *s[2:], a_hi, a_lo)
                elif kind in ("tx", "ty"):
                    _, L, c = s
                    evacuated(pe, (L, ("x" if kind == "tx" else "y", c)))
                    for k in range(2):
                        idx = TURN[s] + k
                        t_ = turn_bank(idx)
                        for q in range(2):
                            n = 4 * c + 2 * k + q
                            for b in range(TB):
                                ins = nc.tensor.transpose(t_[:, q * T + b * P:q * T + (b + 1) * P],
                                                          xn[:, b, n * P:(n + 1) * P], ident)
                        ins.then_inc(turned, 1)
                elif kind == "lg":
                    _, L, d, pr = s
                    uses, frees = mid_before(L, d * 4 + pr)
                    if frees:
                        pe.wait_ge(mid_free, frees)
                    pe.wait_ge(xc_ready, KT * L + 2 * pr + 2)
                    pe.wait_ge(s_wg, 16 * (L + 1))
                    for q in range(2):
                        n = 2 * pr + q
                        for g in range(2):
                            ins = nc.tensor.matmul(mid[:, q, g * T:(g + 1) * T], wg[:, d, g, n, :],
                                                   xc[:, n, :], start=True, stop=True)
                    ins.then_inc(mid_full, 1)
                elif kind == "tq":
                    _, L, j = s
                    pe.wait_ge(rope_done, 2 * (L + 1))
                    idx = TURN[s]
                    t_ = turn_bank(idx)
                    for a in range(2):
                        for b in range(TB):
                            o = a * (QK // 2) + j * P
                            ins = nc.tensor.transpose(t_[:, a * T + b * P:a * T + (b + 1) * P],
                                                      qk[:, b, o:o + P], ident)
                    ins.then_inc(turned, 1)
                elif kind == "as":
                    _, L, u = s
                    b, sl = u // SLOTS, u % SLOTS
                    uses, frees = mid_before(L, 8 + u)
                    pe.wait_ge(mid_free, frees)
                    if u == 0:
                        for j in range(4, 6):
                            bank_read(pe, TURN[("tq", L, j)])
                    flat = mid[:, :, :].rearrange("p a c -> p (a c)")
                    for g in range(GROUPS):
                        head = g * SLOTS + sl
                        o = DH * (head % 2)
                        ins = nc.tensor.matmul(flat[:, g * T:(g + 1) * T],
                                               qkT[o:o + DH, head // 2, 0, b * P:(b + 1) * P],
                                               qkT[o:o + DH, head // 2, 1, :], start=True, stop=True)
                    ins.then_inc(mid_full, 1)
                elif kind in ("ap", "aq"):
                    _, L, u = s
                    pe.wait_ge(p_ready, 8 * L + u + 1)
                    t_ = turn_bank(TURN[s])
                    for k, c in enumerate(range(4) if kind == "ap" else range(4, 2 * GROUPS)):
                        ins = nc.tensor.transpose(t_[:, k * P:(k + 1) * P], sm[:, u % 2, c * P:(c + 1) * P],
                                                  ident)
                    ins.then_inc(turned, 1)
                elif kind == "av":
                    _, L, u = s
                    b, sl = u // SLOTS, u % SLOTS
                    for part in ("ap", "aq"):
                        bank_read(pe, TURN[(part, L, u)])
                    idx = TURN[s]
                    t_ = turn_bank(idx)
                    for i in range(2 * GROUPS):
                        g, kb = i // 2, i % 2
                        o = (g * SLOTS + sl) * DH
                        ins = nc.tensor.matmul(t_[:, 0:DH], pt[u % 2][:, i, :], v[:, kb, o:o + DH],
                                               start=i == 0, stop=i == 2 * GROUPS - 1)
                    ins.then_inc(turned, 1)
                elif kind == "ta":
                    _, L = s
                    for u in range(6, 8):
                        bank_read(pe, TURN[("av", L, u)])
                    idx = TURN[s]
                    t_ = turn_bank(idx)
                    for a in range(2):
                        for b in range(TB):
                            ins = nc.tensor.transpose(t_[:, a * T + b * P:a * T + (b + 1) * P],
                                                      att[:, b, a * P:(a + 1) * P], ident)
                    ins.then_inc(turned, 1)
                elif kind == "tm":
                    _, L, j = s
                    pe.wait_ge(merged, 2 * L + j + 1)
                    for b in range(TB):
                        idx = TURN[s] + b
                        t_ = turn_bank(idx)
                        for k in range(4):
                            kt = 4 * j + k
                            ins = nc.tensor.transpose(t_[:, k * P:(k + 1) * P],
                                                      qk[:, b, kt * P:(kt + 1) * P], ident)
                        ins.then_inc(turned, 1)
                    a_from[j] = TURN[s]
                elif kind == "th":
                    _, L, c = s
                    evacuated(pe, (L, ("up", c)))
                    w = 4 if c < DSTEPS else 2
                    for b in range(TB):
                        idx = TURN[s] + b
                        t_ = turn_bank(idx)
                        for k in range(w):
                            ins = nc.tensor.transpose(t_[:, k * P:(k + 1) * P],
                                                      hid[c % 2][:, b, k * P:(k + 1) * P], ident)
                        ins.then_inc(turned, 1)

            pe.wait_ge(rw_ready, 2)
            for kt in range(KT):
                if kt % 4 == 0:
                    for b in range(TB):
                        bank_read(pe, a_from[kt // 4] + b)
                hi_, lo_ = (rw[:, i, kt * EXPERTS:(kt + 1) * EXPERTS] for i in range(2))
                ins = mm3(mid[0:EXPERTS, 0, 0:T], hi_, lo_, a_hi[:, kt, :], a_lo[:, kt, :],
                          start=kt == 0, stop=kt == KT - 1)
            ins.then_inc(logit_full, 1)
            pe.wait_ge(logit_rows, 1)
            for b in range(TB):
                ins = nc.tensor.transpose(mid[:, 1, b * EXPERTS:(b + 1) * EXPERTS],
                                          lgT[:, b * P:(b + 1) * P], ident[0:EXPERTS, 0:EXPERTS])
            ins.then_inc(logit_full, 1)
            pe.wait_ge(mask_ready, 1)
            nc.tensor.matmul(mid[:, 0, 0:EXPERTS], before, mask[:, 0, :], start=True, stop=True)
            nc.tensor.matmul(mid[:, 1, 0:EXPERTS], before, mask[:, 1, :], start=True, stop=False)
            nc.tensor.matmul(mid[:, 1, 0:EXPERTS], ones, mask[:, 0, :], start=False, stop=True)
            nc.tensor.matmul(bank[0][:, 0:EXPERTS], ones, mask[:, 0, :], start=True, stop=False)
            nc.tensor.matmul(bank[0][:, 0:EXPERTS], ones, mask[:, 1, :], start=False,
                             stop=True).then_inc(rank_full, 1)

            def wait_turn(idx, e):
                pe.wait_ge(turn_free[idx % 2], idx // 2 + e * (E_TURNS // 2))
                return turn[idx % 2]

            def read_out(idx, e):
                pe.wait_ge(turn_free[idx % 2], idx // 2 + 1 + e * (E_TURNS // 2))

            def gather(idx, j, e):
                t_ = wait_turn(idx + j, e)
                for k in range(4):
                    kt = 4 * j + k
                    for i, (src, b) in enumerate([(s_, b) for b in range(TB) for s_ in (xn_hi, xn_lo)]):
                        ins = nc.tensor.matmul(t_[:, k * P:(k + 1) * P], src[:, b, kt * P:(kt + 1) * P],
                                               sel[:, b, :], start=i == 0, stop=i == 2 * TB - 1)
                ins.then_inc(turned, 1)

            def combine(idx, i, e):
                b, n = i // 2, i % 2
                t_ = wait_turn(idx, e)
                nc.tensor.matmul(t_[:, :], selT[:, b * P:(b + 1) * P], y_hi[:, xslice(n)],
                                 start=True, stop=False)
                nc.tensor.matmul(t_[:, :], selT[:, b * P:(b + 1) * P], y_lo[:, xslice(n)],
                                 start=False, stop=True).then_inc(turned, 1)

            def experts(pas):
                g0 = pas * (EXPERTS + 1)
                t0 = T0 + pas * (2 + EXPERTS * E_TURNS + 4)
                h0 = H0 + pas * EXPERTS * E_HALVES
                s0 = pas * EXPERTS * ESTEPS
                pe.wait_ge(sel_ready, TB * (g0 + 1))
                for j in range(2):
                    gather(t0, j, 0)
                tl = t0 + 2
                with pe.Fori(0, EXPERTS) as e:
                    for i in range(E_HALVES):
                        for m, at_ in enumerate(AT_COMBINE):
                            if i == at_:
                                if m == 0:
                                    pe.wait_ge(y_ready, 2 + 2 * (g0 + 1) + e * 2)
                                combine(tl + E_USE["combine", m], m, e)
                        if i == AT_SLOT:
                            t_ = wait_turn(tl + E_USE["slot", 0], e)
                            for b in range(TB):
                                ins = nc.tensor.transpose(t_[:, b * P:(b + 1) * P],
                                                          sel[:, b, :].bitcast(F32), ident)
                            ins.then_inc(turned, 1)
                        for c in range(ESTEPS):
                            if i == AT_HID[c]:
                                t_ = wait_turn(tl + E_USE["hid", c], e)
                                pe.wait_ge(e_hid, s0 + c + 1 + e * ESTEPS)
                                for k in range(4):
                                    ins = nc.tensor.transpose(t_[:, k * P:(k + 1) * P],
                                                              eh[c % 2][:, k * P:(k + 1) * P], ident)
                                ins.then_inc(turned, 1)
                        for j in range(2):
                            if i == AT_GATHER[j]:
                                if j == 0:
                                    pe.wait_ge(sel_ready, TB * (g0 + 2) + e * TB)
                                gather(tl + E_USE["gather", 0], j, e)
                        (what, c), hh = expert_order()[i // 4], i % 4
                        h = h0 + i
                        if what == "down":
                            if hh == 0:
                                read_out(tl + E_USE["hid", c], e)
                            pe.wait_ge(lo_ready, h + 1 + e * E_HALVES)
                            for n in range(2):
                                ins = mm3(mid[:, n, :], eT_hi[c % 2][:, hh, :], eT_lo[c % 2][:, hh, :],
                                          w_hi[:, h % H, xslice(n)], w_lo[:, h % H, xslice(n)],
                                          start=c == 0 and hh == 0, stop=c == ESTEPS - 1 and hh == 3)
                        else:
                            o_ = bank[2 * (c % 2) + (what == "up")]
                            if what == "gate" and c == 0 and hh % 2 == 0:
                                read_out(t0 + hh // 2, e)
                            pe.wait_ge(lo_ready, h + 1 + e * E_HALVES)
                            for k in range(2):
                                kt = 2 * hh + k
                                ins = mm3(o_[:, :], g_hi[:, kt, :], g_lo[:, kt, :],
                                          w_hi[:, h % H, xslice(k)], w_lo[:, h % H, xslice(k)],
                                          start=kt == 0, stop=kt == KT - 1)
                        ins.then_inc(used, 1)
                pe.wait_ge(y_ready, 2 + 2 * (EXPERTS + 1) * (pas + 1))
                for m in range(4):
                    combine(tl + EXPERTS * E_TURNS + m, m, 0)

            experts(0)
            pe.wait_ge(route_ready, 1)
            n = pe.value_load(most_i[0:1, 0:1], min_val=0, max_val=T)
            with pe.If(n > NPASS_TOKENS):
                experts(1)

        @block.vector
        def _(dve):
            links = [0]
            hi = [0]

            def link(ins):
                ins.then_inc(chain, 1)
                links[0] += 1
                dve.wait_ge(chain, links[0])

            def turn_low(dst, dst_hi, src, idx):
                hi[0] += 1
                dve.wait_ge(turn_hi, hi[0])
                nc.vector.tensor_tensor(dst, src, dst_hi.bitcast(F32),
                                        ALU.subtract).then_inc(turn_free[idx % 2], 1)

            def inverse_deviation(k):
                if k < 2 * DEPTH:
                    dve.wait_ge(sq_sum, 4 * (k + 1))
                link(nc.vector.tensor_tensor(ms, ss[:, 0, :], ss[:, 1, :], ALU.add))
                nc.vector.tensor_scalar(ms, ms, 1.0 / D, EPS, ALU.mult, ALU.add).then_inc(ms_ready, 1)
                dve.wait_ge(sd_ready, k + 1)
                nc.vector.reciprocal(rstd, sd).then_inc(rstd_ready, 1)
                dve.wait_ge(rstd_ready, k + 1)

            def rates(stage):
                r0, r1, r2 = rate[:, 0, :], rate[:, 1, :], rate[:, 2, :]
                TERMS = 9
                if stage == 0:
                    dve.wait_ge(s_vec, 16)
                    nc.vector.scalar_tensor_tensor(out=r0, in0=lam, scalar=-1.0, in1=lam, op0=ALU.mult,
                                                   op1=ALU.min).then_inc(rate_s, 1)
                    return
                if stage == 1:
                    dve.wait_ge(rate_s, 2)
                    link(nc.vector.tensor_scalar(r2, r1, 2.0, None, ALU.add))
                    link(nc.vector.reciprocal(r2, r2))
                    link(nc.vector.tensor_tensor(r0, r1, r2, ALU.mult))
                    link(nc.vector.tensor_tensor(r1, r0, r0, ALU.mult))
                    link(nc.vector.tensor_scalar(r2, r1, 1.0 / (2 * TERMS + 1), 1.0 / (2 * TERMS - 1),
                                                 ALU.mult, ALU.add))
                    return
                for i in range(TERMS - 2, TERMS // 2 - 1, -1) if stage == 2 else range(TERMS // 2 - 1, -1, -1):
                    link(nc.vector.tensor_tensor(r2, r2, r1, ALU.mult))
                    link(nc.vector.tensor_scalar(r2, r2, 1.0 / (2 * i + 1), None, ALU.add))
                if stage == 2:
                    return
                dve.wait_ge(s_const, 16)
                link(nc.vector.scalar_tensor_tensor(out=r2, in0=r2, scalar=2.0, in1=r0, op0=ALU.mult,
                                                    op1=ALU.mult))
                link(nc.vector.tensor_scalar(r1, lam, -1.0, 0.0, ALU.mult, ALU.max))
                link(nc.vector.tensor_tensor(r2, r2, r1, ALU.add))
                nc.vector.tensor_scalar(r0, r2, 4.0, None, ALU.mult).then_inc(rate_ready, 1)
                nc.vector.tensor_scalar(r1, r2, -8.0, None, ALU.mult).then_inc(rate_ready, 1)

            ahead = [0]

            def split_half():
                split_lo(dve, ahead[0])
                ahead[0] += 1

            last_sum = {}
            for s in STEPS:
                kind = s[0]
                if kind == "xg":
                    _, k, n = s
                    if k == 0:
                        dve.wait_ge(s_gain0[n], 16)
                    else:
                        dve.wait_ge(s_gain, 16 * k)
                    for b in range(TB):
                        x_done(dve, k, n, b)
                        nc.vector.tensor_tensor(xn[:, b, xslice(n)], x[:, b, xslice(n)],
                                                gain[:, xslice(n)], ALU.mult).then_inc(xn_ready, 1)
                    if k == 0:
                        for _ in range(1 + (LAG > 2) * n):
                            split_half()
                elif kind == "rs":
                    k = s[1]
                    inverse_deviation(k)
                    if k % 2 == 0:
                        nc.vector.memset(xT[:, :, 0:1], 0.0).then_inc(chain, 1)
                        nc.vector.memset(xT[:, :, T + 1:T + 3], 0.0).then_inc(chain, 1)
                        links[0] += 2
                elif kind == "rate":
                    rates(s[2])
                elif kind == "tn":
                    j = s[2]
                    for b in range(TB):
                        idx = TURN[s] + b
                        c = (slice(None), slice(4 * j, 4 * j + 4), slice(b * P, (b + 1) * P))
                        turn_low(a_lo[c], a_hi[c],
                                 turn[idx % 2][:, :].rearrange("p (k t) -> p k t", k=4), idx)
                elif kind == "G":
                    split_half()
                elif kind == "evac":
                    L, name = s[1:]
                    key = (L, name)
                    what, n = name[0], name[1]
                    p = PAIR[L, name[:3]][0]
                    if what in ("x", "y", "qkv"):
                        product_done(dve, key)
                        if what == "y" and n == 0:
                            dve.wait_ge(rope_done, 2 * (L + 1))
                        w = CB
                        if what != "qkv":
                            dst = xn[:, 1, xslice(n)]
                        else:
                            w = CB if n < 4 else VW - CB
                            dst = qk[:, 1, xslice(n)] if n < 3 else v[:, 1, (n - 3) * CB:(n - 3) * CB + w]
                        nc.vector.tensor_scalar(dst, acc(p, 1)[:, 0:w], rstd[:, 1:2], None,
                                                ALU.mult).then_inc(pair_free[p], 1)
                    elif what == "lru":
                        product_done(dve, key)
                        dve.wait_ge(gate_ready, 4 * L + 3 + n)
                        for b in range(TB):
                            g = sg0[:, b, xslice(n)]
                            nc.vector.tensor_tensor(g, acc(p, b), g, ALU.mult).then_inc(pair_free[p], 1)
                    elif what in ("out", "down"):
                        key, second = (L, name[:3]), len(name) == 4
                        product_done(dve, key)
                        for i in (int(second),):
                            n_ = i if KIND[key] == "s" else name[-1]
                            if n_ in last_sum:
                                evacuated(dve, *last_sum[n_])
                            last_sum[n_] = (key, i)
                            for b in range(TB):
                                xs = x[:, b, xslice(n_)]
                                nc.vector.tensor_tensor(xs, acc(PAIR[key][i], b), xs,
                                                        ALU.add).then_inc(pair_free[PAIR[key][i]], 1)
                    elif what == "up":
                        product_done(dve, key)
                        evacuated(dve, (L, ("gate", n)))
                        w = CB if n < DSTEPS else 2 * P
                        for b in range(TB):
                            hs = hid[n % 2][:, b, 0:w]
                            nc.vector.scalar_tensor_tensor(out=hs, in0=acc(p, b)[:, 0:w],
                                                           scalar=rstd[:, b:b + 1], in1=hs, op0=ALU.mult,
                                                           op1=ALU.mult).then_inc(pair_free[p], 1)
                elif kind == "ga":
                    _, L, n = s
                    key = (L, ("att", 0))
                    product_done(dve, key)
                    dve.wait_ge(gate_ready, 4 * L + 1 + n)
                    for b in range(TB):
                        g = qk[:, b, xslice(n)]
                        nc.vector.tensor_tensor(g, acc(PAIR[key][n], b), g,
                                                ALU.mult).then_inc(pair_free[PAIR[key][n]], 1)
                elif kind == "merge":
                    _, L, j = s
                    evacuated(dve, (L, ("att", 0)), j)
                    evacuated(dve, (L, ("lru", j)))
                    g = qk[:, :, xslice(j)]
                    nc.vector.tensor_tensor(g, g, sg0[:, :, xslice(j)], ALU.add).then_inc(merged, 1)
                elif kind == "tx":
                    _, L, c = s
                    for k in range(2):
                        idx = TURN[s] + k
                        n = 4 * c + 2 * k
                        bank_full(dve, idx)
                        nc.vector.tensor_copy(xT[:, n:n + 2, 1:T + 1],
                                              turn[idx % 2][:, :].rearrange("p (n t) -> p n t", n=2)
                                              ).then_inc(turn_free[idx % 2], 1)
                elif kind == "conv":
                    _, L, pr = s
                    bank_read(dve, TURN[("tx", L, pr // 2)] + pr % 2)
                    for q in range(2):
                        n = 2 * pr + q
                        nc.vector.tensor_scalar(xc[:, n, :], xT[:, n, 0:T], convw[:, L, 0, n:n + 1],
                                                convb[:, L, n:n + 1], ALU.mult, ALU.add).then_inc(chain, 1)
                        links[0] += 1
                    for j in range(1, 4):
                        for q in range(2):
                            n = 2 * pr + q
                            dve.wait_ge(chain, links[0] - 1)
                            ins = nc.vector.scalar_tensor_tensor(
                                out=xc[:, n, :], in0=xT[:, n, j:j + T], scalar=convw[:, L, j, n:n + 1],
                                in1=xc[:, n, :], op0=ALU.mult, op1=ALU.add)
                            if j < 3:
                                ins.then_inc(chain, 1)
                                links[0] += 1
                            else:
                                ins.then_inc(xc_ready, 1)
                            if j == 3 and q == 0:
                                dve.wait_ge(chain, links[0])
                elif kind == "lb":
                    _, L, d, hf = s
                    k = (L * 2 + d) * 2 + hf
                    n4 = slice(4 * hf, 4 * hf + 4)
                    dve.wait_ge(decay_ready, 4 * (k + 1))
                    dve.wait_ge(sq_ready, k + 1)
                    link(nc.vector.scalar_tensor_tensor(out=root[:, :, :], in0=rg[:, n4, :], scalar=1.0,
                                                        in1=root[:, :, :], op0=ALU.add, op1=ALU.mult))
                    dve.wait_ge(ix_ready, k + 1)
                    link(nc.vector.tensor_tensor(ig[:, n4, :], root[:, :, :], ig[:, n4, :], ALU.mult))
                elif kind == "router":
                    dve.wait_ge(rw_ready, 1)
                    nc.vector.tensor_tensor(rw[:, 1, :], router, rw[:, 0, :].bitcast(F32),
                                            ALU.subtract).then_inc(rw_ready, 1)
                elif kind == "ls":
                    _, L, d, hf = s
                    n4 = slice(4 * hf, 4 * hf + 4)
                    for q in range(4):
                        n = 4 * hf + q
                        if d == 0:
                            nc.vector.tensor_tensor_scan(xT[:, n, 0:T], rg[:, n, :], ig[:, n, :], 0.0,
                                                         ALU.mult, ALU.add).then_inc(scanned, 1)
                        else:
                            back = slice(T - 1, None, -1)
                            nc.vector.tensor_tensor_scan(root[:, q, back], rg[:, n, back], ig[:, n, back],
                                                         0.0, ALU.mult, ALU.add).then_inc(chain, 1)
                            links[0] += 1
                    if d == 1:
                        dve.wait_ge(chain, links[0])
                        nc.vector.tensor_tensor(xT[:, n4, 0:T], xT[:, n4, 0:T], root[:, :, :],
                                                ALU.add).then_inc(scanned, 4)
                elif kind == "lf":
                    _, L, pr = s
                    dve.wait_ge(scanned, scans_done(L, 1, 1))
                    for i in range(2):
                        bank_read(dve, TURN[("ty", L, 1)] + i)
                    y2 = gy[:, 2 * pr:2 * pr + 2, :]
                    nc.vector.tensor_tensor(y2, xT[:, 2 * pr:2 * pr + 2, 0:T], y2,
                                            ALU.mult).then_inc(lru_full, 1)
                    dve.wait_ge(lru_hi_ready, 4 * L + pr + 1)
                    nc.vector.tensor_tensor(lru_lo[:, 2 * pr:2 * pr + 2, :], y2,
                                            lru_hi[:, 2 * pr:2 * pr + 2, :].bitcast(F32),
                                            ALU.subtract).then_inc(lru_ready, 1)
                elif kind == "tq" and s[2] % 2 == 1:
                    idx = TURN[s]
                    bank_full(dve, idx)
                    dve.wait_ge(scanned, scans_done(s[1], 1, 1))
                    nc.vector.tensor_copy(qkT[:, s[2], :, :],
                                          turn[idx % 2][:, :].rearrange("p (a t) -> p a t", a=2)
                                          ).then_inc(turn_free[idx % 2], 1)
                elif kind == "am":
                    _, L, u = s
                    b = u // SLOTS
                    uses, frees = mid_before(L, 8 + u)
                    dve.wait_ge(mid_full, uses + 1)
                    if u >= 2:
                        bank_full(dve, TURN[("aq", L, u - 2)])
                    flat = mid[:, :, :].rearrange("p a c -> p (a c)")
                    nc.vector.tensor_tensor_reduce(out=sm[:, u % 2, :], in0=flat[:, 0:GROUPS * T],
                                                   in1=band[:, b, :], scale=1.0, scalar=NEG, op0=ALU.add,
                                                   op1=ALU.max,
                                                   accum_out=mx[:, u % 2:u % 2 + 1]).then_inc(mid_free, 1)
                    dve.wait_ge(mid_free, frees + 1)
                    nc.vector.tensor_scalar(nm[:, u % 2:u % 2 + 1], mx[:, u % 2:u % 2 + 1], -SCALE, None,
                                            ALU.mult).then_inc(nm_ready, 1)
                elif kind == "aq":
                    _, L, u = s
                    idx = TURN[s]
                    bank_full(dve, idx)
                    nc.vector.tensor_copy(pt[u % 2][:, 4:6, :],
                                          turn[idx % 2][:, 0:2 * P].rearrange("p (a t) -> p a t", a=2)
                                          ).then_inc(turn_free[idx % 2], 1)
                    dve.wait_ge(p_ready, 8 * L + u + 1)
                    link(nc.vector.reciprocal(rr[:, u % 2:u % 2 + 1], rs[:, u % 2:u % 2 + 1]))
                elif kind == "av":
                    _, L, u = s
                    b, sl = u // SLOTS, u % SLOTS
                    idx = TURN[s]
                    bank_full(dve, idx)
                    nc.vector.tensor_scalar(att[:, b, sl * DH:(sl + 1) * DH], turn[idx % 2][:, 0:DH],
                                            rr[:, u % 2:u % 2 + 1], None,
                                            ALU.mult).then_inc(turn_free[idx % 2], 1)
                elif kind == "ta":
                    turn_low(att_lo[:, :, :], att_hi[:, :, :],
                             turn[TURN[s] % 2][:, :].rearrange("p (a t) -> p a t", a=2), TURN[s])
                elif kind == "tm":
                    j = s[2]
                    for b in range(TB):
                        idx = TURN[s] + b
                        c = (slice(None), slice(4 * j, 4 * j + 4), slice(b * P, (b + 1) * P))
                        turn_low(a_lo[c], a_hi[c],
                                 turn[idx % 2][:, :].rearrange("p (k t) -> p k t", k=4), idx)
                elif kind == "th":
                    c = s[2]
                    w = 4 if c < DSTEPS else 2
                    for b in range(TB):
                        idx = TURN[s] + b
                        r_ = (slice(None), slice(0, w), slice(b * P, (b + 1) * P))
                        turn_low(hT_lo[c % 2][r_], hT_hi[c % 2][r_],
                                 turn[idx % 2][:, 0:w * P].rearrange("p (k t) -> p k t", k=w), idx)

            nc.vector.memset(y_hi[:, :].bitcast(F32), 0.0).then_inc(chain, 1)
            nc.vector.memset(y_lo[:, :].bitcast(F32), 0.0).then_inc(chain, 1)
            nc.vector.memset(selT[:, :].bitcast(F32), 0.0).then_inc(chain, 1)
            nc.vector.memset(slot[:, :, :], -1.0).then_inc(chain, 1)
            links[0] += 4
            dve.wait_ge(chain, links[0])
            nc.vector.memset(share[:, :, :], 0.0).then_inc(y_ready, 2)
            dve.wait_ge(y_ready, 2)
            dve.wait_ge(logit_full, 1)
            nc.vector.tensor_copy(lgT[:, :], mid[0:EXPERTS, 0, 0:T]).then_inc(logit_rows, 1)
            dve.wait_ge(logit_full, 2)
            for b in range(TB):
                nc.vector.tensor_scalar(lg[:, b, :], mid[:, 1, b * EXPERTS:(b + 1) * EXPERTS],
                                        rstd[:, b:b + 1], None, ALU.mult).then_inc(chain, 1)
            links[0] += TB
            dve.wait_ge(chain, links[0])
            shape = [P, TB, EXPERTS, EXPERTS]
            for b in range(TB):
                nc.vector.max(top[:, b, :], lg[:, b, :]).then_inc(chain, 1)
            rival = lg[:, :, :].rearrange("p b (o e) -> p b o e", o=1).to_broadcast(shape)
            own = lg[:, :, :].rearrange("p b (e o) -> p b e o", o=1).to_broadcast(shape)
            low = lower.rearrange("p (o a) e -> p o a e", o=1).to_broadcast(shape)
            nc.vector.tensor_tensor(cmp_[:, :, :, :], rival, own, ALU.is_gt).then_inc(chain, 1)
            nc.vector.tensor_tensor(cmp2[:, :, :, :], rival, own, ALU.is_equal).then_inc(chain, 1)
            links[0] += TB + 2
            dve.wait_ge(chain, links[0])
            link(nc.vector.tensor_tensor(cmp2[:, :, :, :], cmp2[:, :, :, :], low, ALU.mult))
            link(nc.vector.tensor_tensor(cmp_[:, :, :, :], cmp_[:, :, :, :], cmp2[:, :, :, :], ALU.add))
            link(nc.vector.tensor_reduce(mask[:, :, :], cmp_[:, :, :, :], AX.X, ALU.add))
            nc.vector.tensor_scalar(mask[:, :, :], mask[:, :, :], 1.5, None, ALU.is_lt).then_inc(mask_ready, 1)
            for b in range(TB):
                ins = nc.vector.tensor_scalar(lg[:, b, :], lg[:, b, :], top[:, b, 0:1], None, ALU.subtract)
                ins.then_inc(chain, 1) if b == 0 else ins.then_inc(top_ready, 1)
            links[0] += 1
            dve.wait_ge(mask_ready, 1)
            for b in range(TB):
                dve.wait_ge(xn_hi_ready, b + 1)
                nc.vector.scalar_tensor_tensor(out=xn_lo[:, b, :], in0=xn[:, b, :], scalar=rstd[:, b:b + 1],
                                               in1=xn_hi[:, b, :].bitcast(F32), op0=ALU.mult,
                                               op1=ALU.subtract).then_inc(xn_lo_ready, 1)
            dve.wait_ge(rank_full, 1)
            ranks = slot[:, :, 1:EXPERTS + 1]
            link(nc.vector.tensor_scalar(ranks, mid[:, :, 0:EXPERTS], 1.0, None, ALU.add))
            link(nc.vector.tensor_tensor(ranks, ranks, mask[:, :, :], ALU.mult))
            link(nc.vector.tensor_scalar(ranks, ranks, -1.0, None, ALU.add))
            def select(col):
                for b in range(TB):
                    nc.vector.tensor_scalar(sel[:, b, :], iota, slot[:, b, col], None,
                                            ALU.is_equal).then_inc(sel_ready, 1)

            for b in range(TB):
                dve.wait_ge(xn_lo_ready, b + 1)
            select(slice(1, 2))
            link(nc.vector.tensor_reduce(most[:, 0:1], bank[0][:, 0:EXPERTS], AX.X, ALU.max))
            nc.vector.tensor_copy(most_i[:, 0:1], most[:, 0:1]).then_inc(route_ready, 1)
            dve.wait_ge(share_exp, 1)
            link(nc.vector.tensor_tensor(lg[:, :, :], lg[:, :, :], mask[:, :, :], ALU.mult))
            link(nc.vector.tensor_reduce(wsum[:, :, 0:1], lg[:, :, :], AX.X, ALU.add))
            link(nc.vector.reciprocal(wsum[:, :, 1:2], wsum[:, :, 0:1]))
            for b in range(TB):
                link(nc.vector.tensor_scalar(share[:, b, 1:EXPERTS + 1], lg[:, b, :], wsum[:, b, 1:2], None,
                                             ALU.mult))

            def experts(pas):
                g0 = pas * (EXPERTS + 1)
                t0 = T0 + pas * (2 + EXPERTS * E_TURNS + 4)
                h0 = H0 + pas * EXPERTS * E_HALVES
                s0 = pas * EXPERTS * ESTEPS

                def gather_lo(first, j, n):
                    dve.wait_ge(g_hi_ready, n)
                    nc.vector.tensor_tensor(g_lo[:, 4 * j:4 * j + 4, :],
                                            turn[(first + j) % 2][:, :].rearrange("p (k t) -> p k t", k=4),
                                            g_hi[:, 4 * j:4 * j + 4, :].bitcast(F32),
                                            ALU.subtract).then_inc(turn_free[(first + j) % 2], 1)

                def output_lo(n, e):
                    dve.wait_ge(y_hi_ready, 2 * g0 + n + 1 + e * 2)
                    nc.vector.tensor_tensor(y_lo[:, xslice(n)], mid[:, n, :], y_hi[:, xslice(n)].bitcast(F32),
                                            ALU.subtract).then_inc(y_ready, 1)

                def add_output(idx, i, e, col):
                    b, n = i // 2, i % 2
                    dve.wait_ge(turned, idx + 1 + e * E_TURNS)
                    xs = x[:, b, xslice(n)]
                    nc.vector.scalar_tensor_tensor(out=xs, in0=turn[idx % 2][:, :], scalar=share[:, b, col],
                                                   in1=xs, op0=ALU.mult,
                                                   op1=ALU.add).then_inc(turn_free[idx % 2], 1)

                if pas:
                    select(slice(1, 2))
                for j in range(2):
                    gather_lo(t0, j, 2 * g0 + j + 1)
                tl = t0 + 2
                with dve.Fori(0, EXPERTS) as e:
                    for i in range(E_HALVES):
                        split_lo(dve, h0 + i + LAG, e)
                        for n in range(2):
                            if i == n:
                                output_lo(n, e)
                        for m, at_ in enumerate(AT_COMBINE):
                            if i == at_:
                                add_output(tl + E_USE["combine", m], m, e, bass.ds(e, 1))
                        if i == AT_SLOT:
                            idx = tl + E_USE["slot", 0]
                            dve.wait_ge(turned, idx + 1 + e * E_TURNS)
                            nc.vector.tensor_copy(selT[:, :], turn[idx % 2][:, 0:T]
                                                  ).then_inc(turn_free[idx % 2], 1)
                        if i == AT_SELECT:
                            select(bass.ds(e + 2, 1))
                        for c in range(ESTEPS):
                            if i == E_AT["up", c] + 4:
                                dve.wait_ge(e_silu, s0 + c + 1 + e * ESTEPS)
                                dve.wait_ge(used, h0 + E_AT["up", c] + 4 + e * E_HALVES)
                                nc.vector.tensor_tensor(eh[c % 2][:, :], bank[2 * (c % 2) + 1][:, :],
                                                        eh[c % 2][:, :], ALU.mult).then_inc(e_hid, 1)
                            if i == AT_HID[c]:
                                idx = tl + E_USE["hid", c]
                                dve.wait_ge(eT_hi_ready, s0 + c + 1 + e * ESTEPS)
                                nc.vector.tensor_tensor(eT_lo[c % 2][:, :, :],
                                                        turn[idx % 2][:, :].rearrange("p (k t) -> p k t", k=4),
                                                        eT_hi[c % 2][:, :, :].bitcast(F32),
                                                        ALU.subtract).then_inc(turn_free[idx % 2], 1)
                        for j in range(2):
                            if i == AT_GATHER[j]:
                                gather_lo(tl + E_USE["gather", 0], j, 2 * (g0 + 1) + j + 1 + e * 2)
                for n in range(2):
                    output_lo(n, EXPERTS)
                for m in range(4):
                    add_output(tl + EXPERTS * E_TURNS + m, m, 0, slice(EXPERTS, EXPERTS + 1))
                dve.wait_ge(final_sum, 4 * (pas + 1))

            experts(0)
            n = dve.value_load(most_i[0:1, 0:1], min_val=0, max_val=T)
            with dve.If(n > NPASS_TOKENS):
                nc.vector.tensor_scalar(slot[:, :, :], slot[:, :, :], -float(NPASS_TOKENS), None,
                                        ALU.add).then_inc(zeroed, 1)
                dve.wait_ge(zeroed, 1)
                experts(1)
            inverse_deviation(2 * DEPTH)
            dve.wait_ge(s_gain, 16 * 2 * DEPTH)
            for n in range(2):
                for b in range(TB):
                    nc.vector.scalar_tensor_tensor(
                        out=xn[:, b, xslice(n)], in0=x[:, b, xslice(n)], scalar=rstd[:, b:b + 1],
                        in1=gain[:, xslice(n)], op0=ALU.mult, op1=ALU.mult).then_inc(done, 1)


def pack_cols(w, kt, cols):
    return w.reshape(kt, P, cols).transpose(1, 0, 2)


def part_of(w, kind, i):
    if kind == "s":
        return pack_cols(w, 2, D).reshape(P, 2, 2, CB).transpose(0, 2, 1, 3).reshape(P, PART)
    kt = {"n": 4, "h": 8, "w": 2}[kind]
    return pack_cols(w[i * kt * P:(i + 1) * kt * P], kt, w.shape[1]).reshape(P, PART)


def weight_stream(inp):
    out = np.empty((TOTAL_PARTS + SPARE, P, PART), np.float32)
    n = 0

    def put(*part):
        nonlocal n
        out[n] = part_of(*part)
        n += 1

    g0 = 2 * D + 3 * VW
    for L in range(DEPTH):
        w_in = inp["w_in"][L]
        for (what, i), kind, part in MIXER:
            c = i * CB
            if what == "x":
                w = w_in[:, c:c + CB]
            elif what == "y":
                w = w_in[:, D + c:D + c + CB]
            elif what == "qkv":
                w = w_in[:, 2 * D + c:2 * D + min(c + CB, 3 * VW)]
            elif what == "g0":
                w = w_in[:, g0 + c:g0 + c + CB]
            elif what == "g1":
                w = w_in[:, g0 + D + c:g0 + D + c + CB]
            elif what == "lru":
                w = inp["w_proj_lru"][L][:, c:c + CB]
            elif what == "att":
                w = inp["w_proj_att"][L]
            else:
                w = inp["w_out"][L][:, c:c + CB]
            put(w, kind, part)
        if L == 0:
            for name, kind, part in dense_order():
                f = name[1] * CB
                if name[0] == "down":
                    w = inp["w_dense_down"][0][f:f + CB]
                    if kind == "n":
                        w = w[:, name[2] * CB:(name[2] + 1) * CB]
                else:
                    w = inp["w_dense_" + name[0]][0][:, f:f + CB]
                put(w, kind, part)
    for e in range(EXPERTS):
        for what, c in expert_order():
            f = c * CB
            for part in range(2):
                if what == "down":
                    put(inp["w_exp_down"][0, e][f:f + CB], "w", part)
                else:
                    put(inp["w_exp_" + what][0, e][:, f:f + CB], "n", part)
    assert n == TOTAL_PARTS
    out[n:] = out[STATIC_PARTS:STATIC_PARTS + SPARE]
    return out


def constants():
    c = np.zeros((P, C_END), np.float32)
    i = np.arange(P)
    c[:, C_ID:C_ID + P] = np.eye(P)
    c[:, C_IOTA:C_IOTA + P] = i[None, :]
    c[:, C_BEFORE:C_BEFORE + P] = i[:, None] < i[None, :]
    c[:, C_ONES:C_ONES + P] = 1
    k = np.arange(T)
    for b in range(TB):
        rel = (b * P + i)[:, None] - k[None, :]
        for g in range(GROUPS):
            ok = (rel % DILATIONS[g] == 0) & (np.abs(rel) <= WINDOWS[g] // 2)
            o = C_MASK + (b * GROUPS + g) * T
            c[:, o:o + T] = np.where(ok, 0, NEG)
        freq = (np.float32(500000.0) ** (-np.arange(0, 16, 2, dtype=np.float32) / np.float32(16))).astype(np.float32)
        ang = (b * P + i)[:, None].astype(np.float32) * freq[None, :]
        c[:, C_COS + 8 * b:C_COS + 8 * b + 8] = np.cos(ang)
        c[:, C_SIN + 8 * b:C_SIN + 8 * b + 8] = np.sin(ang)
    e = np.arange(EXPERTS)
    c[:, C_LOW:C_END] = (e[None, :] < e[:, None]).astype(np.float32).reshape(1, -1)
    return c


def by_channel(a):
    a = a.reshape(a.shape[:-1] + (a.shape[-1] // P, P))
    return np.moveaxis(a, -1, 0).reshape(P, -1)


def kernel(**inputs):
    import concourse.bacc as bacc
    from concourse.bass_utils import run_bass_kernel_spmd

    inp = {k: np.asarray(a) for k, a in inputs.items()}
    router = inp["w_router"][0].reshape(KT, P, EXPERTS).transpose(1, 0, 2).reshape(P, -1)
    vecs = np.concatenate([by_channel(inp["conv_w"]), by_channel(inp["conv_b"]), by_channel(inp["b_rgate"]),
                           by_channel(inp["b_igate"]), by_channel(inp["lru_lambda"]), router], axis=1)
    gates = np.stack([inp["w_rgate"], inp["w_igate"]], axis=2)
    gates = gates.transpose(0, 4, 1, 2, 3, 5).reshape(DEPTH, P, -1)
    norms = np.stack([inp["norm_mix_g"][0], inp["norm_ffn_g"][0], inp["norm_mix_g"][1],
                      inp["norm_ffn_g"][1], inp["final_norm_g"]])
    arrays = {
        "stream": weight_stream(inp), "gates": np.ascontiguousarray(gates),
        "x": inp["x"].reshape(T, D), "norms": norms, "consts": constants(),
        "vecs": np.ascontiguousarray(vecs),
    }
    nc = bacc.Bacc("TRN2", target_bir_lowering=False, num_devices=1)
    aps = [nc.dram_tensor(f"in_{k}", a.shape, mybir.dt.from_np(a.dtype), kind="ExternalInput").ap()
           for k, a in arrays.items()]
    out = nc.dram_tensor("out_x", (T, D), F32, kind="ExternalOutput").ap()
    build(nc, *aps, out)
    r = run_bass_kernel_spmd(nc, [{f"in_{k}": a for k, a in arrays.items()}], core_ids=[0])
    return r.results[0]["out_x"].reshape(1, T, D)
```
